# Optimizing a Trainium2 kernel written in Bass

```python
import jax, jax.numpy as jnp
from jax import lax
import numpy as np

D_MODEL = 1024
BATCH = 1
SEQ = 1024
DEPTH = 2

CTX_LEN = 256
GRID_W = 64
CHUNK = 128
Q_BLOCK = 128
W_A = D_MODEL // 4
A_HEADS = 4
A_HEAD_DIM = W_A // A_HEADS
W_B = D_MODEL // 4
POOL_WINDOWS = (2, 4, 8, 16)
B_GROUP = W_B // len(POOL_WINDOWS)
V_DIM = 64
W_C = D_MODEL // 2
MLA_HEADS = W_C // V_DIM
QK_NOPE = 64
QK_ROPE = 32
QK_HEAD = QK_NOPE + QK_ROPE
Q_RANK = 256
KV_RANK = 128
D_MIX = W_A + W_B + W_C
SPLIT_POINTS = (2 * W_A, 2 * W_A + W_B, 2 * W_A + W_B + Q_RANK, 2 * W_A + W_B + Q_RANK + KV_RANK)
D_IN = 2 * W_A + W_B + Q_RANK + KV_RANK + QK_ROPE
D_FF = -(-8 * D_MODEL // (3 * 256)) * 256
ROPE_BASE = 10000.0
EPS = 1e-6
N_MOD = 6

kernel_name = "hybrid_parallel_groups_dit_block"

def rms_norm(x, g):
    xf = x.astype(jnp.float32)
    y = xf * lax.rsqrt(jnp.mean(xf * xf, axis=-1, keepdims=True) + EPS)
    return (y * g.astype(jnp.float32)).astype(x.dtype)

def axial_rope_tables(n_tokens):
    rows = n_tokens // GRID_W
    row = jnp.repeat(jnp.arange(rows), GRID_W).astype(jnp.float32)
    col = jnp.tile(jnp.arange(GRID_W), rows).astype(jnp.float32)
    n_freq = QK_ROPE // 4
    inv = ROPE_BASE ** (-jnp.arange(n_freq, dtype=jnp.float32) / n_freq)
    ang = jnp.concatenate([row[:, None] * inv, col[:, None] * inv], axis=-1)
    return jnp.cos(ang), jnp.sin(ang)

def apply_rope(x, cos, sin):
    shp = x.shape
    xp = x.astype(jnp.float32).reshape(shp[:-1] + (QK_ROPE // 2, 2))
    x1, x2 = xp[..., 0], xp[..., 1]
    c = cos[None, :, None, :]
    s = sin[None, :, None, :]
    out = jnp.stack([x1 * c - x2 * s, x1 * s + x2 * c], axis=-1)
    return out.reshape(shp).astype(x.dtype)

def chunk_mlp(z, norm_g, w_spatial, b_spatial):
    bn, n_tok = z.shape[0], z.shape[1]
    u, v = z[..., :W_A], z[..., W_A:]
    v = rms_norm(v, norm_g).reshape(bn, n_tok // CHUNK, CHUNK, A_HEADS, A_HEAD_DIM)
    mixed = jnp.einsum('hij,bnjhd->bnihd', w_spatial, v) + b_spatial.T[:, :, None]
    return u * mixed.reshape(bn, n_tok, W_A)

def multiscale_pool(z, w_pool, pool_scale):
    n_tok = z.shape[1]
    zf = z.astype(jnp.float32)
    cs = jnp.concatenate([jnp.zeros_like(zf[:, :1]), jnp.cumsum(zf, axis=1)], axis=1)
    t = jnp.arange(n_tok)
    outs = []
    for g, w in enumerate(POOL_WINDOWS):
        lo = jnp.clip(t - w // 2, 0, n_tok)
        hi = jnp.clip(t + w // 2, 0, n_tok)
        seg = cs[:, :, g * B_GROUP:(g + 1) * B_GROUP]
        mean = (jnp.take(seg, hi, axis=1) - jnp.take(seg, lo, axis=1)) / (hi - lo).astype(jnp.float32)[None, :, None]
        d = (mean - zf[:, :, g * B_GROUP:(g + 1) * B_GROUP]).astype(z.dtype)
        outs.append(jnp.einsum('blc,cd->bld', d, w_pool[g]))
    return jnp.concatenate(outs, axis=-1) * pool_scale

def mla_qkv(p_q, p_kv, p_kr, q_a_norm_g, w_q_b, kv_a_norm_g, w_kv_b, q_norm_g, k_norm_g, rope):
    bn, n_tok = p_q.shape[0], p_q.shape[1]
    q = (rms_norm(p_q, q_a_norm_g) @ w_q_b).reshape(bn, n_tok, MLA_HEADS, QK_HEAD)
    kv = (rms_norm(p_kv, kv_a_norm_g) @ w_kv_b).reshape(bn, n_tok, MLA_HEADS, QK_NOPE + V_DIM)
    k_nope, v = kv[..., :QK_NOPE], kv[..., QK_NOPE:]
    k_rope = jnp.broadcast_to(p_kr[:, :, None, :], (bn, n_tok, MLA_HEADS, QK_ROPE))
    k = jnp.concatenate([k_nope, k_rope], axis=-1)
    q = rms_norm(q, q_norm_g)
    k = rms_norm(k, k_norm_g)
    if rope is not None:
        cos, sin = rope
        q = jnp.concatenate([q[..., :QK_NOPE], apply_rope(q[..., QK_NOPE:], cos, sin)], axis=-1)
        k = jnp.concatenate([k[..., :QK_NOPE], apply_rope(k[..., QK_NOPE:], cos, sin)], axis=-1)
    return q, k, v

def attend_blocks(q, k, v):
    bn, n_tok = q.shape[0], q.shape[1]
    nb = n_tok // Q_BLOCK
    scale = QK_HEAD ** -0.5
    qb = q.reshape(bn, nb, Q_BLOCK, MLA_HEADS, QK_HEAD).transpose(1, 0, 2, 3, 4)

    def one_block(qblk):
        s = jnp.einsum('bqhd,bkhd->bhqk', qblk, k, preferred_element_type=jnp.float32) * scale
        p = jax.nn.softmax(s, axis=-1)
        return jnp.einsum('bhqk,bkhd->bqhd', p.astype(v.dtype), v)

    o = lax.map(one_block, qb)
    return o.transpose(1, 0, 2, 3, 4).reshape(bn, n_tok, MLA_HEADS * V_DIM)

def swiglu(h, w_gate_up, w_down):
    gu = h @ w_gate_up
    return (jax.nn.silu(gu[..., :D_FF]) * gu[..., D_FF:]) @ w_down

def hybrid_layer(x, xc, s_lat, s_ctx, rope, norm1_g, norm2_g, w_ada, b_ada, w_in,
                 sgu_norm_g, w_spatial, b_spatial, w_pool, pool_scale,
                 q_a_norm_g, w_q_b, kv_a_norm_g, w_kv_b, q_norm_g, k_norm_g,
                 w_out, w_gate_up, w_down, update_ctx):
    bn = x.shape[0]
    mod = (s_lat @ w_ada + b_ada).reshape(bn, N_MOD, 1, D_MODEL)
    modc = (s_ctx @ w_ada + b_ada).reshape(N_MOD, 1, 1, D_MODEL)
    sh1, sc1, g1, sh2, sc2, g2 = [mod[:, i] for i in range(N_MOD)]
    sh1c, sc1c, g1c, sh2c, sc2c, g2c = [modc[i] for i in range(N_MOD)]

    h = rms_norm(x, norm1_g) * (1 + sc1) + sh1
    hc = rms_norm(xc, norm1_g) * (1 + sc1c) + sh1c
    a, b, pq, pkv, pkr = jnp.split(h @ w_in, SPLIT_POINTS, axis=-1)
    ac, bc, pqc, pkvc, pkrc = jnp.split(hc @ w_in, SPLIT_POINTS, axis=-1)

    y_a = chunk_mlp(jax.nn.gelu(a, approximate=False), sgu_norm_g, w_spatial, b_spatial)
    y_b = multiscale_pool(b, w_pool, pool_scale)
    q, k, v = mla_qkv(pq, pkv, pkr, q_a_norm_g, w_q_b, kv_a_norm_g, w_kv_b, q_norm_g, k_norm_g, rope)
    qc, kc, vc = mla_qkv(pqc, pkvc, pkrc, q_a_norm_g, w_q_b, kv_a_norm_g, w_kv_b, q_norm_g, k_norm_g, None)
    y_c = attend_blocks(q, jnp.concatenate([kc, k], axis=1), jnp.concatenate([vc, v], axis=1))
    x = x + g1 * (jnp.concatenate([y_a, y_b, y_c], axis=-1) @ w_out)

    h2 = rms_norm(x, norm2_g) * (1 + sc2) + sh2
    x = x + g2 * swiglu(h2, w_gate_up, w_down)

    if update_ctx:
        y_ac = chunk_mlp(jax.nn.gelu(ac, approximate=False), sgu_norm_g, w_spatial, b_spatial)
        y_bc = multiscale_pool(bc, w_pool, pool_scale)
        y_cc = attend_blocks(qc, kc, vc)
        xc = xc + g1c * (jnp.concatenate([y_ac, y_bc, y_cc], axis=-1) @ w_out)
        h2c = rms_norm(xc, norm2_g) * (1 + sc2c) + sh2c
        xc = xc + g2c * swiglu(h2c, w_gate_up, w_down)
    return x, xc

def setup_inputs(seed: int = 0) -> dict:
    key = jax.random.key(seed)
    ks = jax.random.split(key, 28)
    f32 = jnp.float32

    def nrm(k, shape, scale):
        return jax.random.normal(k, shape, f32) * scale

    def gain(k, shape):
        return 1.0 + 0.02 * jax.random.normal(k, shape, f32)

    L = DEPTH
    return {
        "x": nrm(ks[0], (BATCH, SEQ, D_MODEL), 1.0),
        "c": nrm(ks[1], (BATCH, D_MODEL), 1.0),
        "ctx": nrm(ks[2], (BATCH, CTX_LEN, D_MODEL), 1.0),
        "c_ctx": nrm(ks[3], (D_MODEL,), 1.0),
        "norm1_g": gain(ks[4], (L, D_MODEL)),
        "norm2_g": gain(ks[5], (L, D_MODEL)),
        "w_ada": nrm(ks[6], (L, D_MODEL, N_MOD * D_MODEL), 0.5 * D_MODEL ** -0.5),
        "b_ada": nrm(ks[7], (L, N_MOD * D_MODEL), 0.02),
        "w_in": nrm(ks[8], (L, D_MODEL, D_IN), D_MODEL ** -0.5),
        "sgu_norm_g": gain(ks[9], (L, W_A)),
        "w_spatial": nrm(ks[10], (L, A_HEADS, CHUNK, CHUNK), CHUNK ** -0.5),
        "b_spatial": gain(ks[11], (L, A_HEADS, CHUNK)),
        "w_pool": nrm(ks[12], (L, len(POOL_WINDOWS), B_GROUP, B_GROUP), B_GROUP ** -0.5),
        "pool_scale": gain(ks[13], (L, W_B)),
        "q_a_norm_g": gain(ks[14], (L, Q_RANK)),
        "w_q_b": nrm(ks[15], (L, Q_RANK, MLA_HEADS * QK_HEAD), Q_RANK ** -0.5),
        "kv_a_norm_g": gain(ks[16], (L, KV_RANK)),
        "w_kv_b": nrm(ks[17], (L, KV_RANK, MLA_HEADS * (QK_NOPE + V_DIM)), KV_RANK ** -0.5),
        "q_norm_g": gain(ks[18], (L, QK_HEAD)),
        "k_norm_g": gain(ks[19], (L, QK_HEAD)),
        "w_out": nrm(ks[20], (L, D_MIX, D_MODEL), D_MIX ** -0.5),
        "w_gate_up": nrm(ks[21], (L, D_MODEL, 2 * D_FF), D_MODEL ** -0.5),
        "w_down": nrm(ks[22], (L, D_FF, D_MODEL), D_FF ** -0.5),
    }

def reference(x, c, ctx, c_ctx, norm1_g, norm2_g, w_ada, b_ada, w_in, sgu_norm_g,
              w_spatial, b_spatial, w_pool, pool_scale, q_a_norm_g, w_q_b,
              kv_a_norm_g, w_kv_b, q_norm_g, k_norm_g, w_out, w_gate_up, w_down):
    n_tok = x.shape[1]
    rope = axial_rope_tables(n_tok)
    s_lat = jax.nn.silu(c)
    s_ctx = jax.nn.silu(c_ctx)
    xc = ctx
    for i in range(DEPTH):
        x, xc = hybrid_layer(
            x, xc, s_lat, s_ctx, rope, norm1_g[i], norm2_g[i], w_ada[i], b_ada[i], w_in[i],
            sgu_norm_g[i], w_spatial[i], b_spatial[i], w_pool[i], pool_scale[i],
            q_a_norm_g[i], w_q_b[i], kv_a_norm_g[i], w_kv_b[i], q_norm_g[i], k_norm_g[i],
            w_out[i], w_gate_up[i], w_down[i], update_ctx=(i < DEPTH - 1))
    return x


_drawn_inputs = setup_inputs


def setup_inputs(seed=0):
    import zlib

    import numpy as np

    out = dict(_drawn_inputs(seed))
    spreads = {}
    factors = {'ctx': 8.0,
     'c_ctx': 3.38,
     'norm1_g': 8.0,
     'norm2_g': 27.691,
     'sgu_norm_g': 66.336,
     'b_spatial': 69.834,
     'pool_scale': 54.044,
     'q_a_norm_g': 43.526,
     'kv_a_norm_g': 50.246,
     'q_norm_g': 43.25,
     'k_norm_g': 41.374}
    for name, (base, spread) in spreads.items():
        noise = np.random.default_rng([zlib.crc32(name.encode()), seed]).standard_normal(out[name].shape)
        drawn = base * np.exp(spread * noise) if base else spread * noise
        out[name] = __import__('jax').numpy.asarray(drawn.astype(out[name].dtype))
    for name, factor in factors.items():
        out[name] = (out[name] * factor).astype(out[name].dtype)
    return out
```

```python
import math
from contextlib import ExitStack

import concourse.bass as bass
from concourse import mybir

F32 = mybir.dt.float32
F32R = mybir.dt.float32r
ALU = mybir.AluOpType
ACT = mybir.ActivationFunctionType
AX = mybir.AxisListType

P = 128
DM = 1024
KT = DM // P
CTX = 256
SEQ = 1024
NTOK = CTX + SEQ
DEPTH = 2
HEADS = 8
VD = 64
NOPE = 64
ROPE = 32
QKD = NOPE + ROPE
DFF = 2816
FT = DFF // P
WINDOWS = (2, 4, 8, 16)
HALO = max(WINDOWS) // 2
EPS = 1e-6
SCALE = QKD ** -0.5

BLOCKS = ((0, CTX), (CTX, 512), (CTX + 512, 512))
NMAX = 512
CH = KT * P

C_IN, N_IN = 0, 10
C_OUT = C_IN + N_IN
C_GU = C_OUT + KT
DN_K = (8, 7, 7)
C_DN = C_GU + 2 * FT
NCH = C_DN + KT * len(DN_K)
P1_CHUNKS = {True: tuple(range(N_IN)), False: (8, 9)}
NQ = HEADS * QKD
NKV = HEADS * (NOPE + VD)

PRM = {}
_at = 0
for _n, _w in (("sgu", 2), ("pscale", 2), ("qa", 2), ("kva", 1),
               ("gq", QKD), ("gk", QKD), ("bsp", 256), ("wpool", 256), ("wsp", 512)):
    PRM[_n] = (_at, _at + _w)
    _at += _w
NPRM = _at

ADA_W = 256
ADA_N = 6 * DM // ADA_W


def full(l, b):
    return not (l == DEPTH - 1 and b == 0)


def layer_blocks(l):
    return [b for b in range(len(BLOCKS)) if full(l, b)]


class Count:

    def __init__(self, nc, ctx, known):
        self.nc, self.ctx, self.known = nc, ctx, known
        self.sems, self.total, self.value = {}, {}, {}

    def sem(self, name):
        if name not in self.sems:
            self.sems[name] = self.ctx.enter_context(self.nc.semaphore(name))
            self.total[name] = 0
        return self.sems[name]

    def inc(self, name, key=None, by=1):
        s = self.sem(name)
        self.total[name] += by
        self.value[name, key] = name, self.total[name]
        return s, by

    def alias(self, name, key, of):
        self.value[name, key] = of, self.total[of]

    def skip(self, name, n):
        self.sem(name)
        self.total[name] += n

    def now(self, name, tag):
        self.sem(name)
        self.value[name, tag] = name, self.total[name]

    def at(self, name, key=None, plus=0):
        of, value = self.known.get((name, key), (name, 1))
        return self.sem(of), value + plus


def build(nc, t_in, known):
    ctx = ExitStack()
    with ctx:
        C = Count(nc, ctx, known)
        inc, at = C.inc, C.at

        def sb(name, shape, dt=F32):
            return ctx.enter_context(nc.sbuf_tensor(name, shape, dt))

        X = sb("X", [P, KT, NTOK])
        raw = sb("raw", [P, 2, CH])
        w_hi = sb("w_hi", [P, 2, CH], F32R)
        w_lo = sb("w_lo", [P, 2, CH], F32R)
        prm = sb("prm", [P, NPRM])
        ada_p = sb("ada_p", [P, DEPTH, 64])
        mod = sb("mod", [P, DEPTH, 48, 2])
        gain = sb("gain", [P, DEPTH, 2, KT, 2])
        ident = sb("ident", [P, P])
        ones = sb("ones", [P, P])
        half = sb("half", [P, 1])
        t32 = sb("t32", [P, 2, NMAX])
        rstd = sb("rstd", [P, NMAX])
        trig = sb("trig", [P, SEQ // P, 2, ROPE // 2])
        var, ssum = t32[:, 0, :], t32[:, 1, :]

        psum = ctx.enter_context(nc.psum_tensor("psum", [P, 8, 512], F32))

        qk_scr = nc.dram_tensor("qk_scr", [DEPTH, 2, HEADS, QKD, 2, NTOK], F32).ap()
        v_scr = nc.dram_tensor("v_scr", [DEPTH, HEADS, NTOK, 2 * VD], F32).ap()
        y_scr = nc.dram_tensor("y_scr", [DEPTH, DM, NTOK], F32).ap()
        b_scr = nc.dram_tensor("b_scr", [DEPTH, 2, P, NTOK], F32).ap()

        def overlay(specs):
            with ExitStack() as st:
                return [st.enter_context(nc.sbuf_tensor(n, s, d)) for n, s, d in specs]

        kh, qh, vh, prob, pt_hi, pt_lo, yc, yc_lo, amax, den = overlay([
            ("kh", [QKD, 2, 2, NTOK], F32R), ("qh", [QKD, 2, 2, NTOK], F32R),
            ("vh", [P, 2, NTOK // P, 2 * VD], F32R), ("prob", [P, 4, NTOK], F32),
            ("pt_hi", [P, 2, NTOK // P, 256], F32R), ("pt_lo", [P, 2, NTOK // P, 256], F32R),
            ("yc", [VD, 2, 256], F32), ("yc_lo", [VD, 2, 256], F32),
            ("amax", [P, 2, 4], F32), ("den", [P, 2, 4], F32)])
        h_hi = sb("h_hi", [P, KT, NMAX], F32R)
        h_lo = sb("h_lo", [P, KT, NMAX], F32R)
        ada_w, silu_c = overlay([("ada_w", [P, 3, KT, ADA_W], F32), ("silu_c", [P, 2, KT, 2], F32)])
        (nrm_t, wqkv_hi, wqkv_lo, pq_sq, pq_hi, pq_lo, u_sb, v_sb, vtok, kr_sb, qk, qk_sq, v_st, st_qk, mixo, yst,
         stat, krt) = overlay([
             ("nrm_t", [P, 4, NMAX], F32), ("wqkv_hi", [P, 2 * NQ + NKV], F32R), ("wqkv_lo", [P, 2 * NQ + NKV], F32R),
             ("pq_sq", [P, 3, NMAX], F32), ("pq_hi", [P, 3, NMAX], F32R), ("pq_lo", [P, 3, NMAX], F32R),
             ("u_sb", [P, 2, NMAX], F32), ("v_sb", [P, 2, NMAX], F32),
             ("vtok", [P, 2, 256], F32), ("kr_sb", [P, NMAX], F32),
             ("qk", [P, 2, 2, HEADS, QKD], F32), ("qk_sq", [P, 2, HEADS, QKD], F32),
             ("v_st", [P, 2, HEADS, 2, VD], F32R), ("st_qk", [QKD, 2, 2, 256], F32R),
             ("mixo", [P, 2, 256], F32), ("yst", [P, 2, NMAX], F32),
             ("stat", [P, 256], F32), ("krt", [P, 2, ROPE], F32)])
        pq32 = nrm_t
        pz, ps2, ps4, pinv, pd = overlay([
            ("pz", [P, 2, SEQ + 2 * HALO], F32), ("ps2", [P, SEQ + 2 * HALO], F32),
            ("ps4", [P, SEQ + 2 * HALO], F32), ("pinv", [P, 2, SEQ], F32), ("pd", [P, 2, SEQ], F32)])
        yraw, = overlay([("yraw", [P, KT, NMAX], F32)])
        fnrm_t, gu_hi, gu_lo = overlay([
            ("fnrm_t", [P, 4, NMAX], F32), ("gu_hi", [P, FT, NMAX], F32R), ("gu_lo", [P, FT, NMAX], F32R)])
        sg, gu32 = fnrm_t[:, 0:2, :], fnrm_t[:, 2:4, :]

        def pcol(name, a=0, b=None):
            s, e = PRM[name]
            return prm[:, s + a:(s + b if b is not None else e)]

        block = ctx.enter_context(nc.Block())

        start, stream = {}, []
        for l in range(DEPTH):
            for b in range(len(BLOCKS)):
                start["p1", l, b] = len(stream)
                stream += [(l, c) for c in P1_CHUNKS[full(l, b)]]
            for b in layer_blocks(l):
                start["out", l, b] = len(stream)
                stream += [(l, c) for c in range(C_OUT, C_GU)]
            for b in layer_blocks(l):
                start["ffn", l, b] = len(stream)
                stream += [(l, c) for c in range(C_GU, NCH)]
        n_chunks = len(stream)

        def steps(l):
            lat = [(CTX + P * t, NTOK // P) for t in range(SEQ // P)]
            return lat + ([(P * t, CTX // P) for t in range(CTX // P)] if l < DEPTH - 1 else [])

        def t_groups(nk):
            return [(k, min(4, nk - k)) for k in range(0, nk, 4)]

        sub_tiles = lambda T: [(s, min(2, T // P - s)) for s in range(0, T // P, 2)]

        def mixsq(t):
            return qk_sq[:, t].rearrange("p h d -> p (h d)")[:, 0:256]

        def at_prev(l, b):
            seq = [(i, j) for i in range(DEPTH) for j in range(len(BLOCKS)) if full(i, j)]
            before = [x for x in seq if x < (l, b)]
            return before[-1]

        def pool_seq(l):
            return [(l, g, i, q) for g, L in enumerate((CTX, SEQ)) if g or full(l, 0) for i in range(2) for q in range(0, L, NMAX)]

        def prev_banks(pe, l, b):
            pl, pb = (l, b - 1) if b else (l - 1, len(BLOCKS) - 1)
            if b:
                pe.wait_ge(*at("kr_sb", (pl, pb)))
            else:
                pe.wait_ge(*at("dn_acc_end", (pl, pb)))

        def subs():
            return [(l, b, s) for l in range(DEPTH) for b in range(len(BLOCKS)) for s, _ in sub_tiles(BLOCKS[b][1])]

        def prev_sub_wait(eng, l, b, s, w):
            i = subs().index((l, b, s))
            if i == 0:
                return
            pl, pb, pss = subs()[i - 1]
            if w == 1 or full(pl, pb):
                eng.wait_ge(*at("qk_tr", (pl, pb, pss, w, HEADS - 1)))
            if w == 1:
                eng.wait_ge(*at("v_store", (pl, pb, pss)))

        def head_seq():
            return [(l, b, s, w, h) for l, b, s in subs() for w in ((0, 1) if full(l, b) else (1,)) for h in range(HEADS)]

        def prev_head_wait(eng, l, b, s, w, hd):
            i = head_seq().index((l, b, s, w, hd))
            if i >= 2:
                k = head_seq()[i - 2]
                eng.wait_ge(*at(f"qk_store{hd % 2}", k))

        def att_plan(l):
            st, tg = [], []
            for hd in range(HEADS):
                for i, (col, nk) in enumerate(steps(l)):
                    st.append((hd, i, col, nk))
            out = []
            for g, (hd, i, col, nk) in enumerate(st):
                grp = []
                for k0, n in t_groups(nk):
                    grp.append((len(tg), k0, n))
                    tg.append((g, k0, n))
                out.append(grp)
            return st, out

        psum_flat = psum[:, :, :].rearrange("p a n -> p (a n)")

        def scores(g, nk):
            at0 = (g % 2) * NTOK
            return psum_flat[:, at0:at0 + nk * P]

        def score_parts(g, nk):
            cuts = (0, 512, 1024, NTOK) if g % 2 == 0 else (0, 256, 768, NTOK)
            parts = [(a, min(b, nk * P) - a) for a, b in zip(cuts, cuts[1:]) if a < nk * P]
            return parts if g % 2 == 0 else parts[1:] + parts[:1]

        def att_act(act, l):
            st, groups = att_plan(l)
            G = len(st)
            per = len(steps(l))
            npair = per // 2
            for g in range(G + 4):
                if 0 <= g - 2 < G:
                    q = g - 2
                    for tg, k0, n in groups[q]:
                        act.wait_ge(*at("t_mm", (l, tg)))
                        if k0 == 0 and q // 2 >= 2:
                            hq, pq_ = divmod(q // 2 - 2, npair)
                            act.wait_ge(*at("pv_mm", (l, hq, pq_)))
                        if k0 == 0 and q // 2 < 2:
                            act.wait_ge(*at("att_free", l))
                        act.activation(pt_hi[:, (q // 2) % 2, k0:k0 + n, (q % 2) * P:(q % 2) * P + P],
                                       psum[:, 5 + tg % 2, 0:n * P].rearrange("p (k n) -> p k n", n=P), ACT.Copy)\
                           .then_inc(*inc("t_hi", (l, tg)))
                if g < G:
                    hd, i, col, nk = st[g]
                    act.wait_ge(*at("amax", (l, g)))
                    if g >= 4:
                        act.wait_ge(*at("t_mm", (l, groups[g - 4][-1][0])))
                    sc = scores(g, nk)
                    act.activation(prob[:, g % 4, 0:nk * P], sc, ACT.Exp, bias=amax[:, 1, g % 4:g % 4 + 1], scale=SCALE,
                                   accum_out=den[:, 0, g % 4:g % 4 + 1]).then_inc(*inc("exp", (l, g)))
                if g >= 4 and g % 2 == 0 and (g - 4) // 2 < G // 2:
                    pr = (g - 4) // 2
                    hq, pq_ = divmod(pr, npair)
                    act.wait_ge(*at("pv_mm", (l, hq, pq_)))
                    if pr >= 2:
                        h2, p2 = divmod(pr - 2, npair)
                        act.wait_ge(*at("yc", (l, h2, p2)))
                    act.activation(yc_lo[:, pr % 2, :], psum[VD:2 * VD, 7, 0:256], ACT.Copy).then_inc(*inc("yc_lo", (l, hq, pq_)))

        @block.sync
        def _(sp):
            sp.dma_start(X[:, :, :], t_in["x"].rearrange("(k p) n -> p k n", p=P)).then_inc(*inc("x_in", by=16))
            sp.dma_start(ident[:, :], t_in["ident"]).then_inc(*inc("consts", by=16))
            sp.dma_start(trig[:, :, :, :], t_in["trig"]).then_inc(*inc("consts", by=16))
            sp.dma_start(ada_p[:, :, :], t_in["ada_p"]).then_inc(*inc("consts", by=16))
            sp.dma_start(prm[:, :], t_in["prm"][0]).then_inc(*inc("prm", 0, 16))
            sp.dma_start(silu_c[:, 0], t_in["c"]).then_inc(*inc("c_in", by=16))
            for j in range(DEPTH * ADA_N):
                l, m = divmod(j, ADA_N)
                if j >= 3:
                    sp.wait_ge(*at("ada_mm", j - 3))
                sp.dma_start(ada_w[:, j % 3], t_in["w_ada"][l, m]).then_inc(*inc(f"ada_in{j % 3}", j, 16))
            def load_chunks(n0, count):
                for n in range(n0, min(n0 + count, n_chunks)):
                    if n >= 2:
                        sp.wait_ge(C.sem("w_lo"), n - 1)
                    l, c = stream[n]
                    sp.dma_start(raw[:, n % 2, :], t_in["w"][l, c]).then_inc(*inc(f"w_in{n % 2}", n, 16))

            def load_chunks_loop(n0, turns):
                l, c0 = stream[n0]
                with sp.Fori(0, turns, 1) as i:
                    for j in range(4):
                        src = t_in["w"][l, bass.ds(i * 4 + (c0 + j), 1)].rearrange("o p n -> (o p) n")
                        sp.wait_ge(C.sem("w_lo"), i * 4 + (n0 + j - 1))
                        sp.dma_start(raw[:, (n0 + j) % 2, :], src).then_inc(C.sem(f"w_in{(n0 + j) % 2}"), 16)
                for j in range(2):
                    C.skip(f"w_in{j}", 32 * turns)

            load_chunks(0, 2)
            for l in range(DEPTH):
                if l:
                    sp.wait_ge(*at("att_free", l - 1))
                    sp.dma_start(prm[:, :], t_in["prm"][l]).then_inc(*inc("prm", l, 16))
                    sp.wait_ge(C.sem("w_used"), start["p1", l, 0])
                else:
                    sp.wait_ge(*at("ada_mm", DEPTH * ADA_N - 1))
                sp.dma_start(qk[:, :, :, :, :].rearrange("p a b c d -> p (a b c d)")[:, 0:2 * NQ + NKV], t_in["wqkv"][l])\
                  .then_inc(*inc("wqkv_in", l, 16))
                for b, (c0, T) in enumerate(BLOCKS):
                    n0, cs = start["p1", l, b], P1_CHUNKS[full(l, b)]
                    load_chunks(n0 + 2, len(cs))
                    lat = b > 0
                    if full(l, b):
                        for i in range(2):
                            sp.wait_ge(*at("b_out", (l, b, i)))
                            sp.dma_start(b_scr[l, i, :, c0:c0 + T], yst[:, i, :T]).then_inc(*inc("b_store", (l, b, i), 16))
                        for s, nt in sub_tiles(T):
                            sp.wait_ge(*at("mix_out", (l, b, s, 1)))
                            cs0 = c0 + s * P
                            sp.dma_start(y_scr[l, 0:256, cs0:cs0 + nt * P].rearrange("(i p) n -> p i n", p=P),
                                         mixo[:, :, :nt * P]).then_inc(*inc("ya_store", (l, b, s), 16))
                    for s, nt in sub_tiles(T):
                        cs0 = c0 + s * P
                        sp.wait_ge(*at("v_lo", (l, b, s)))
                        for t in range(nt):
                            sp.dma_start(v_scr[l, :, cs0 + t * P:cs0 + t * P + P, :].rearrange("h p d -> p h d"),
                                         v_st[:, t].rearrange("p h two d -> p h (two d)").bitcast(F32)).then_inc(*inc("v_store", (l, b, s), 16))
                        for w in ((0, 1) if full(l, b) else (1,)):
                            for hd in range(HEADS):
                                sp.wait_ge(*at("qk_lo", (l, b, s, w, hd)))
                                sp.dma_start(qk_scr[l, w, hd, :, :, cs0:cs0 + nt * P], st_qk[:, hd % 2, :, :nt * P].bitcast(F32))\
                                  .then_inc(*inc(f"qk_store{hd % 2}", (l, b, s, w, hd), 16))
                for g, (c0, L) in enumerate(((0, CTX), (CTX, SEQ))):
                    if g == 0 and not full(l, 0):
                        continue
                    sp.wait_ge(*at("b_store", (l, min(g * 2, 2), 1)))
                    sp.wait_ge(*at("pool_edge", (l, g)))
                    sp.dma_start(pz[:, :, HALO:HALO + L], b_scr[l, :, :, c0:c0 + L].rearrange("i p n -> p i n"))\
                      .then_inc(*inc("pz_in", (l, g), 16))
                    sp.dma_start(pinv[:, :, :L], t_in["inv_lat" if g else "inv_ctx"]).then_inc(*inc("pinv_in", (l, g), 16))
                    for i in range(2):
                        for q in range(0, L, NMAX):
                            w = min(NMAX, L - q)
                            sp.wait_ge(*at("pool_out", (l, g, i, q)))
                            sp.dma_start(y_scr[l, 256 + i * P:256 + i * P + P, c0 + q:c0 + q + w], pd[:, i, q:q + w])\
                              .then_inc(*inc("yb_store", (l, g, i, q), 16))
                sp.wait_ge(*at("qk_store0", (l, 2, 2, 1, HEADS - 2)))
                sp.wait_ge(*at("qk_store1", (l, 2, 2, 1, HEADS - 1)))
                sp.wait_ge(*at("v_store", (l, 2, 2)))
                sp.wait_ge(*at("yb_store", (l, 1, 1, SEQ - NMAX)))
                sp.wait_ge(*at("ya_store", (l, 2, 2)))
                q0 = 0 if l < DEPTH - 1 else CTX
                npair = len(steps(l)) // 2

                def head_loads(hd, j):
                    one = bass.ds(hd, 1)
                    sp.dma_start(kh[:, j].bitcast(F32), qk_scr[l, 1, one].rearrange("o d s n -> (o d) s n")).then_inc(C.sem(f"kqv{j}"), 16)
                    sp.dma_start(qh[:, j, :, q0:].bitcast(F32), qk_scr[l, 0, one, :, :, q0:].rearrange("o d s n -> (o d) s n")).then_inc(C.sem(f"kqv{j}"), 16)
                    sp.dma_start(vh[:, j].bitcast(F32), v_scr[l, one].rearrange("o (t p) d -> p (o t) d", p=P)).then_inc(C.sem(f"kqv{j}"), 16)
                    C.skip(f"kqv{j}", 48)

                def yc_store(hd, j, pr):
                    col = steps(l)[2 * pr][0]
                    sp.dma_start(y_scr[l, 2 * 256 + hd * VD:2 * 256 + hd * VD + VD, col:col + 256] if isinstance(hd, int) else
                                 y_scr[l].rearrange("(h d) n -> h d n", d=VD)[bass.ds(hd + HEADS, 1), :, col:col + 256]
                                 .rearrange("o d n -> (o d) n"), yc[:, (j * npair + pr) % 2])\
                      .then_inc(C.sem(f"yc_store{(j * npair + pr) % 2}"), 16)
                    C.skip(f"yc_store{(j * npair + pr) % 2}", 16)

                C.now("kqv0", ("att", l)); C.now("kqv1", ("att", l))
                C.now("yc_store0", ("att", l)); C.now("yc_store1", ("att", l))
                head_loads(0, 0)
                head_loads(1, 1)
                for hd in range(HEADS):
                    for pr in range(npair):
                        sp.wait_ge(*at("yc", (l, hd, pr)))
                        yc_store(hd, hd % 2, pr)
                    if hd + 2 < HEADS:
                        sp.wait_ge(*at("pv_mm", (l, hd, npair - 1)))
                        head_loads(hd + 2, hd % 2)
                for b in layer_blocks(l):
                    c0, T = BLOCKS[b]
                    n0 = start["out", l, b]
                    if b == layer_blocks(l)[0]:
                        for j in range(2):
                            sp.wait_ge(C.sem(f"yc_store{j}"), C.total[f"yc_store{j}"])
                    else:
                        sp.wait_ge(*at("y_lo", (l, b - 1, KT - 1)))
                    sp.dma_start(yraw[:, :, :T], y_scr[l, :, c0:c0 + T].rearrange("(k p) n -> p k n", p=P))\
                      .then_inc(*inc("y_in", (l, b), 16))
                    load_chunks(n0 + 2, KT)
                for b in layer_blocks(l):
                    n0 = start["ffn", l, b]
                    n_ffn = 2 * FT + 3 * KT
                    load_chunks_loop(n0 + 2, n_ffn // 4 - 1)
                    load_chunks(n0 + 2 + n_ffn - 4, 4)
                    if l == DEPTH - 1:
                        c0, T = BLOCKS[b]
                        sp.wait_ge(*at("dn_acc_end", (l, b)))
                        sp.dma_start(t_in["out"][:, c0 - CTX:c0 - CTX + T].rearrange("(k p) n -> p k n", p=P),
                                     X[:, :, c0:c0 + T]).then_inc(*inc("out", by=16))
            sp.wait_ge(*at("out"))

        def norm_entry(dve, l, which, b):
            pass

        def split_hi(act, n):
            if isinstance(n, int) and n >= n_chunks:
                return
            slot = n % 2
            act.wait_ge(*at(f"w_in{slot}", n))
            if n >= 2:
                act.wait_ge(C.sem("w_used"), n - 1)
            act.activation(w_hi[:, slot, :], raw[:, slot, :], ACT.Copy).then_inc(*inc("w_hi", n))

        def split_lo(dve, n):
            if n >= n_chunks:
                return
            slot = n % 2
            dve.wait_ge(C.sem("w_hi"), n + 1)
            dve.tensor_tensor(w_lo[:, slot, :], raw[:, slot, :], w_hi[:, slot, :].bitcast(F32), ALU.subtract)\
               .then_inc(*inc("w_lo", n))

        def split_hi_loop(act, n0, i, per, j, last):
            n = n0 + j
            act.wait_ge(C.sem(f"w_in{n % 2}"), i * (8 * per) + 16 * (n // 2 + 1))
            act.wait_ge(C.sem("w_used"), i * per + (n - 1))
            act.activation(w_hi[:, n % 2, :], raw[:, n % 2, :], ACT.Copy).then_inc(C.sem("w_hi"), 1)

        def split_lo_loop(dve, n0, i, per, j):
            n = n0 + j
            dve.wait_ge(C.sem("w_hi"), i * per + (n + 1))
            dve.tensor_tensor(w_lo[:, n % 2, :], raw[:, n % 2, :], w_hi[:, n % 2, :].bitcast(F32), ALU.subtract)\
               .then_inc(C.sem("w_lo"), 1)

        qk_flat = qk[:, :, :, :, :].rearrange("p a b c d -> p (a b c d)")[:, 0:2 * NQ + NKV]

        @block.scalar
        def _(act):
            def norm(l, which, b):
                c0, T = BLOCKS[b]
                key = (l, which, b)
                s = 1 if b == 0 else 0
                tmp = nrm_t if which == 0 else fnrm_t
                parts = 4
                for h in range(KT // parts):
                    if h:
                        act.wait_ge(*at("norm_sum", (key, h - 1)))
                    elif which == 1:
                        act.wait_ge(*at("out_end", (l, b)))
                    elif l:
                        act.wait_ge(*at("dn_acc_end", (l - 1, layer_blocks(l - 1)[-1])))
                    else:
                        act.wait_ge(*at("x_in"))
                    if which == 0 and (l, b) == (0, 0):
                        act.wait_ge(*at("ada_end"))
                    if which == 0 and b > 0:
                        act.wait_ge(*at("pq_lo", ((l, b - 1), 2)))
                    act.activation(tmp[:, :parts, :T], X[:, h * parts:(h + 1) * parts, c0:c0 + T], ACT.Square)\
                       .then_inc(*inc("norm_sq", (key, h)))
                for k in range(KT):
                    act.wait_ge(*at("norm_t", (key, k)))
                    if k >= 2:
                        act.wait_ge(*at("h_lo", (key, k - 2)))
                    act.activation(t32[:, k % 2, :T], tmp[:, k % parts, :T], ACT.Identity,
                                   bias=mod[:, l, 24 * which + k, s:s + 1]).then_inc(*inc("h32", (key, k)))
                    act.activation(h_hi[:, k, :T], tmp[:, k % parts, :T], ACT.Identity,
                                   bias=mod[:, l, 24 * which + k, s:s + 1]).then_inc(*inc("h_hi", (key, k)))

            C.skip("sg", 2)
            act.wait_ge(*at("c_in"))
            act.activation(silu_c[:, 1], silu_c[:, 0], ACT.Silu).then_inc(*inc("silu_c"))
            for l in range(DEPTH):
                for b, (c0, T) in enumerate(BLOCKS):
                    n0, cs = start["p1", l, b], P1_CHUNKS[full(l, b)]
                    kb = (l, b)
                    if n0 == 0:
                        split_hi(act, 0)
                        split_hi(act, 1)
                    if b == 0:
                        act.wait_ge(*at("wqkv_in", l))
                        if l == 0:
                            act.wait_ge(*at("ada_end"))
                        act.wait_ge(*at("prm", l))
                        act.activation(wqkv_hi[:, :], qk_flat, ACT.Copy).then_inc(*inc("wqkv_hi", l))
                    norm(l, 0, b)
                    for i, c in enumerate(cs):
                        n = n0 + i
                        split_hi(act, n + 2)
                        src = psum[:, i % 2, :T]
                        if c < N_IN:
                            act.wait_ge(C.sem("w_used"), n + 1)
                        if c in (0, 1):
                            if b > 0 or l > 0:
                                act.wait_ge(*at("mix_done", at_prev(l, b)))
                            act.activation(u_sb[:, c, :T], src, ACT.Gelu).then_inc(*inc("in_free", (kb, i)))
                        elif c in (2, 3):
                            act.activation(v_sb[:, c - 2, :T], src, ACT.Gelu).then_inc(*inc("in_free", (kb, i)))
                        elif c in (4, 5):
                            if b > 0 or l > 0:
                                act.wait_ge(*at("b_store", at_prev(l, b) + (1,)))
                            act.activation(yst[:, c - 4, :T], src, ACT.Copy).then_inc(*inc("in_free", (kb, i)))
                            C.alias("b_out", (l, b, c - 4), "in_free")
                        elif c in (6, 7, 8):
                            j = c - 6
                            g = pcol("qa", j, j + 1) if j < 2 else pcol("kva")
                            act.activation(pq32[:, j, :T], src, ACT.Copy, scale=g).then_inc(*inc("pq32", (kb, j)))
                            act.activation(pq_hi[:, j, :T], src, ACT.Copy, scale=g).then_inc(*inc("pq_hi", (kb, j)))
                            act.activation(pq_sq[:, j, :T], src, ACT.Square).then_inc(*inc("in_free", (kb, i)))
                            C.alias("pq_sq", (kb, j), "in_free")
                        elif c == 9:
                            act.activation(kr_sb[:, :T], src, ACT.Copy).then_inc(*inc("in_free", (kb, i)))
                            C.alias("kr_sb", kb, "in_free")
                    if full(l, b):
                        for s, nt in sub_tiles(T):
                            for t in range(nt):
                                key = (l, b, s + t)
                                act.wait_ge(*at("mix_tr", key))
                                act.activation(vtok[:, t, :], psum[:, 2, 0:256], ACT.Copy).then_inc(*inc("vtok", key))
                                act.activation(mixsq(t), psum[:, 2, 0:256], ACT.Square,
                                               accum_out=stat[:, 64 + s + t:65 + s + t]).then_inc(*inc("vt_sq", key))
                    for s, nt in sub_tiles(T):
                        for t in range(nt):
                            key = (l, b, s + t)
                            if full(l, b):
                                for c in range(2):
                                    act.wait_ge(*at("q_mm", (key, c)))
                                    if c == 0 and t == 0:
                                        prev_sub_wait(act, l, b, s, 0)
                                    act.wait_ge(*at("tok_r", kb))
                                    act.activation(qk[:, 0, t, 4 * c:4 * c + 4].rearrange("p h d -> p (h d)"),
                                                   psum[:, 4 + c, 0:384], ACT.Copy, scale=stat[:, 16 + s + t:17 + s + t])\
                                       .then_inc(*inc("q_tok", (key, c)))
                            for c in range(2):
                                act.wait_ge(*at("kv_mm", (key, c)))
                                if c == 0 and t == 0:
                                    prev_sub_wait(act, l, b, s, 1)
                                act.wait_ge(*at("tok_r", kb))
                                src = psum[:, 6 + c, :].rearrange("p (h d) -> p h d", d=P)
                                rs = stat[:, 20 + s + t:21 + s + t]
                                act.activation(qk[:, 1, t, 4 * c:4 * c + 4, 0:NOPE], src[:, :, 0:NOPE], ACT.Copy, scale=rs)\
                                   .then_inc(*inc("k_tok", (key, c)))
                                act.activation(v_st[:, t, 4 * c:4 * c + 4, 0, :], src[:, :, NOPE:P], ACT.Copy, scale=rs)\
                                   .then_inc(*inc("v_hi", (key, c)))
                        act.wait_ge(*at("kr_tr", (l, b, s)))
                        act.activation(krt[:, :nt, :], psum[:, 3, 0:nt * P].rearrange("p (t d) -> p t d", d=P)[:, :, P - ROPE:P],
                                       ACT.Copy).then_inc(*inc("krt", (l, b, s)))
                        for w in ((0, 1) if full(l, b) else (1,)):
                            for hd in range(HEADS):
                                key = (l, b, s, w, hd)
                                act.wait_ge(*at("qk_tr", key))
                                prev_head_wait(act, l, b, s, w, hd)
                                act.activation(st_qk[:, hd % 2, 0, :nt * P], psum[:QKD, 2 + hd % 2, 0:nt * P], ACT.Copy)\
                                   .then_inc(*inc("qk_hi", key))
                for g, (c0, L) in enumerate(((0, CTX), (CTX, SEQ))):
                    if g == 0 and not full(l, 0):
                        continue
                    for i in range(2):
                        for q in range(0, L, NMAX):
                            w = min(NMAX, L - q)
                            act.wait_ge(*at("pool_mm", (l, g, i, q)))
                            act.activation(pd[:, i, q:q + w], psum[:, (i * 2 + q // NMAX) % 2, :w], ACT.Copy,
                                           scale=pcol("pscale", i, i + 1)).then_inc(*inc("pool_out", (l, g, i, q)))
                att_act(act, l)
                for b in layer_blocks(l):
                    c0, T = BLOCKS[b]
                    n0 = start["out", l, b]
                    act.wait_ge(*at("y_in", (l, b)))
                    act.wait_ge(C.sem("w_used"), n0)
                    for k in range(KT):
                        act.activation(h_hi[:, k, :T], yraw[:, k, :T], ACT.Copy).then_inc(*inc("y_hi", (l, b, k)))
                    for m in range(KT):
                        split_hi(act, n0 + m + 2)
                for b in layer_blocks(l):
                    c0, T = BLOCKS[b]
                    n0 = start["ffn", l, b]
                    act.wait_ge(C.sem("w_used"), n0)
                    norm(l, 1, b)
                    base_sg, base_g = C.total.get("sg", 0), C.total.get("gu_hi", 0)
                    C.now("sg", ("ffn", l, b)); C.now("gu_hi", ("ffn", l, b))
                    g32b = at("gu32", ("ffn", l, b))[1]
                    glob = at("gu_lo", ("ffn", l, b))[1]
                    with act.Fori(0, FT // 2, 1) as i:
                        for j in range(2):
                            split_hi_loop(act, n0 + 2, i, 4, 2 * j, 0)
                            act.wait_ge(C.sem("w_used"), i * 4 + (n0 + 2 * j + 1))
                            act.wait_ge(C.sem("gu32"), i * 2 + (g32b + j - 1))
                            act.activation(sg[:, j, :T], psum[:, 2 * j, :T], ACT.Silu).then_inc(C.sem("sg"), 1)
                            split_hi_loop(act, n0 + 2, i, 4, 2 * j + 1, 0)
                            act.wait_ge(C.sem("gu32"), i * 2 + (g32b + j + 1))
                            act.activation(gu_hi[:, bass.ds(i * 2 + j, 1), :T].rearrange("p o n -> p (o n)"),
                                           gu32[:, j, :T], ACT.Copy).then_inc(C.sem("gu_hi"), 1)
                    C.skip("sg", FT); C.skip("gu_hi", FT); C.skip("w_hi", 2 * FT)
                    n1 = n0 + 2 * FT
                    last = n1 + 3 * KT == n_chunks
                    with act.Fori(0, 1 if last else 2, 1) as i:
                        for j in range(12):
                            split_hi_loop(act, n1 + 2, i, 12, j, 0)
                    if last:
                        for j in range(10):
                            n = n1 + 14 + j
                            act.wait_ge(C.sem(f"w_in{n % 2}"), 16 * (n // 2 + 1))
                            act.wait_ge(C.sem("w_used"), n - 1)
                            act.activation(w_hi[:, n % 2, :], raw[:, n % 2, :], ACT.Copy).then_inc(C.sem("w_hi"), 1)
                    C.skip("w_hi", 3 * KT)

        @block.vector
        def _(dve):
            dve.memset(ones[:, :], 1.0).then_inc(*inc("ones"))
            dve.memset(half[:, :], -0.5).then_inc(*inc("ones"))
            dve.memset(rstd[:, 0:1], 0.0).then_inc(C.sem("gu_lo"), 2)
            C.skip("gu_lo", 2)
            dve.memset(rstd[:, 1:2], 0.0).then_inc(C.sem("gu32"), 2)
            C.skip("gu32", 2)
            dve.memset(rstd[:, 2:3], 0.0).then_inc(C.sem("sg"), 2)
            for l in range(DEPTH):
                dve.wait_ge(*at("ada_mm", (l + 1) * ADA_N - 1))
                dve.wait_ge(*at("consts"))
                bias = ada_p[:, l, 16:64]
                dve.tensor_tensor(mod[:, l].rearrange("p m s -> p m s"), psum[:, 4 + l, 0:96].rearrange("p (m s) -> p m s", s=2),
                                  bias.unsqueeze(2).to_broadcast([P, 48, 2]), ALU.add).then_inc(*inc("mod", l))
                dve.wait_ge(*at("mod", l))
                for which in range(2):
                    ng = ada_p[:, l, 8 * which:8 * which + 8]
                    dve.scalar_tensor_tensor(gain[:, l, which], mod[:, l, 24 * which + 8:24 * which + 16, :], 1.0,
                                             ng.unsqueeze(2).to_broadcast([P, KT, 2]), ALU.add, ALU.mult)\
                       .then_inc(*inc("ada_end"))

            def norm(l, which, b):
                c0, T = BLOCKS[b]
                key = (l, which, b)
                s = 1 if b == 0 else 0
                tmp = nrm_t if which == 0 else fnrm_t
                parts = 4
                for h in range(KT // parts):
                    dve.wait_ge(*at("norm_sq", (key, h)))
                    dst = ssum if h == 0 else var
                    if h == 0:
                        norm_entry(dve, l, which, b)
                    dve.tensor_reduce(dst[:, :T], tmp[:, :parts, :T].rearrange("p k n -> p n k"), AX.X, ALU.add)\
                       .then_inc(*inc("norm_sum", (key, h)))
                if KT // parts == 2:
                    dve.wait_ge(*at("norm_sum", (key, 1)))
                    dve.tensor_tensor(ssum[:, :T], ssum[:, :T], var[:, :T], ALU.add).then_inc(*inc("norm_sum", (key, 2)))
                C.alias("norm_ssum", key, "norm_sum")
                dve.wait_ge(*at("norm_mm", key))
                dve.tensor_scalar(var[:, :T], psum[:, 7, :T], 1.0 / DM, EPS, ALU.mult, ALU.add).then_inc(*inc("norm_var", key))
                dve.wait_ge(*at("norm_rstd", key))

                def lo(k):
                    dve.wait_ge(*at("h_hi", (key, k)))
                    dve.tensor_tensor(h_lo[:, k, :T], t32[:, k % 2, :T], h_hi[:, k, :T].bitcast(F32), ALU.subtract)\
                       .then_inc(*inc("h_lo", (key, k)))
                for k in range(KT):
                    if parts < KT and k >= parts:
                        dve.wait_ge(*at("h_hi", (key, k - parts)))
                    dve.scalar_tensor_tensor(tmp[:, k % parts, :T], X[:, k, c0:c0 + T], gain[:, l, which, k, s:s + 1],
                                             rstd[:, :T], ALU.mult, ALU.mult).then_inc(*inc("norm_t", (key, k)))
                    if k >= 1:
                        lo(k - 1)
                lo(KT - 1)

            for l in range(DEPTH):
                for b, (c0, T) in enumerate(BLOCKS):
                    n0, cs = start["p1", l, b], P1_CHUNKS[full(l, b)]
                    kb = (l, b)
                    nt_all = T // P
                    if n0 == 0:
                        split_lo(dve, 0)
                        split_lo(dve, 1)
                    if b == 0:
                        dve.wait_ge(*at("wqkv_hi", l))
                        dve.tensor_tensor(wqkv_lo[:, :], qk_flat, wqkv_hi[:, :].bitcast(F32), ALU.subtract).then_inc(*inc("wqkv_lo", l))
                    norm(l, 0, b)
                    for i, c in enumerate(cs):
                        split_lo(dve, n0 + i + 2)
                        if c in (6, 7, 8):
                            j = c - 6
                            dve.wait_ge(*at("pq_hi", (kb, j)))
                            dve.tensor_tensor(pq_lo[:, j, :T], pq32[:, j, :T], pq_hi[:, j, :T].bitcast(F32), ALU.subtract)\
                               .then_inc(*inc("pq_lo", (kb, j)))
                        if c == 9:
                            dve.wait_ge(*at("tok_mm", kb))
                            if full(l, b):
                                dve.tensor_scalar(stat[:, 0:nt_all], psum[:, 3, 0:nt_all], 1.0 / 256, EPS, ALU.mult, ALU.add)\
                                   .then_inc(*inc("tok_var", kb))
                            dve.tensor_scalar(stat[:, 4:4 + nt_all], psum[:, 3, 4:4 + nt_all], 1.0 / 128, EPS, ALU.mult, ALU.add)\
                               .then_inc(*inc("tok_var", kb))
                    if full(l, b):
                        for s, nt in sub_tiles(T):
                            for t in range(nt):
                                key = (l, b, s + t)
                                dve.wait_ge(*at("vt_sq", key))
                                dve.tensor_scalar(stat[:, 68 + s + t:69 + s + t], stat[:, 64 + s + t:65 + s + t], 1.0 / 256, EPS,
                                                  ALU.mult, ALU.add).then_inc(*inc("vt_var", key))
                                dve.wait_ge(*at("vt_rstd", key))
                                dve.tensor_scalar(vtok[:, t, :], vtok[:, t, :], stat[:, 72 + s + t:73 + s + t], None, ALU.mult)\
                                   .then_inc(*inc("vt_n", key))
                            if s or l or b:
                                prev = (l, b, s - 2) if s else at_prev(l, b) + (sub_tiles(BLOCKS[at_prev(l, b)[1]][1])[-1][0],)
                                dve.wait_ge(*at("ya_store", prev))
                            for pr in range(2):
                                dve.wait_ge(*at("mix_mm", (l, b, s + nt - 1)))
                                bsp = pcol("bsp", pr * P, pr * P + P).unsqueeze(1).to_broadcast([P, nt, P])
                                dve.scalar_tensor_tensor(mixo[:, pr, :nt * P].rearrange("p (t n) -> p t n", n=P),
                                                         psum[:, 4 + pr, 0:nt * P].rearrange("p (t n) -> p t n", n=P),
                                                         pcol("sgu", pr, pr + 1), bsp, ALU.mult, ALU.add)\
                                   .then_inc(*inc("mix_g", (l, b, s, pr)))
                            for pr in range(2):
                                dve.wait_ge(*at("mix_g", (l, b, s, pr)))
                                dve.tensor_tensor(mixo[:, pr, :nt * P], mixo[:, pr, :nt * P], u_sb[:, pr, s * P:(s + nt) * P],
                                                  ALU.mult).then_inc(*inc("mix_out", (l, b, s, pr)))
                        C.alias("mix_done", kb, "mix_out")
                    for s, nt in sub_tiles(T):
                        for t in range(nt):
                            key = (l, b, s + t)
                            for c in range(2):
                                dve.wait_ge(*at("v_hi", (key, c)))
                                src = psum[:, 6 + c, :].rearrange("p (h d) -> p h d", d=P)
                                dve.scalar_tensor_tensor(v_st[:, t, 4 * c:4 * c + 4, 1, :], src[:, :, NOPE:P],
                                                         stat[:, 20 + s + t:21 + s + t], v_st[:, t, 4 * c:4 * c + 4, 0, :].bitcast(F32),
                                                         ALU.mult, ALU.subtract).then_inc(*inc("v_lo", (l, b, s)))
                                C.alias("v_lo_t", (key, c), "v_lo")
                        for w in ((0, 1) if full(l, b) else (1,)):
                            k2 = (l, b, s, w)
                            a = qk[:, w, :nt].rearrange("p t h d -> p (t h) d")
                            dve.wait_ge(*at("hd_sq", k2))
                            dve.tensor_reduce(stat[:, 80:80 + 8 * nt], qk_sq[:, :nt].rearrange("p t h d -> p (t h) d"), AX.X, ALU.add)\
                               .then_inc(*inc("hd_sum", k2))
                            dve.wait_ge(*at("hd_sum", k2))
                            dve.tensor_scalar(stat[:, 96:96 + 8 * nt], stat[:, 80:80 + 8 * nt], 1.0 / QKD, EPS, ALU.mult, ALU.add)\
                               .then_inc(*inc("hd_var", k2))
                            dve.wait_ge(*at("hd_rstd", k2))
                            dve.tensor_tensor(a, a, stat[:, 112:112 + 8 * nt].unsqueeze(2).to_broadcast([P, 8 * nt, QKD]), ALU.mult)\
                               .then_inc(*inc("hd_n", k2))
                            for hd in range(HEADS):
                                key = (l, b, s, w, hd)
                                dve.wait_ge(*at("qk_hi", key))
                                dve.tensor_tensor(st_qk[:, hd % 2, 1, :nt * P], psum[:QKD, 2 + hd % 2, 0:nt * P],
                                                  st_qk[:, hd % 2, 0, :nt * P].bitcast(F32), ALU.subtract).then_inc(*inc("qk_lo", key))
                st, groups = att_plan(l)
                G, npair = len(st), len(steps(l)) // 2
                for g in range(G + 4):
                    if 0 <= g - 1 < G:
                        dve.wait_ge(*at("exp", (l, g - 1)))
                        if g >= 5:
                            dve.wait_ge(*at("pn", (l, g - 5)))
                        sl = (g - 1) % 4
                        dve.reciprocal(den[:, 1, sl:sl + 1], den[:, 0, sl:sl + 1]).then_inc(*inc("rden", (l, g - 1)))
                    if 0 <= g - 2 < G:
                        q = g - 2
                        for tg, k0, n in groups[q]:
                            dve.wait_ge(*at("t_hi", (l, tg)))
                            sl = (slice(None), (q // 2) % 2, slice(k0, k0 + n), slice((q % 2) * P, (q % 2) * P + P))
                            dve.tensor_tensor(pt_lo[sl], psum[:, 5 + tg % 2, 0:n * P].rearrange("p (k n) -> p k n", n=P),
                                              pt_hi[sl].bitcast(F32), ALU.subtract).then_inc(*inc("t_lo", (l, tg)))
                    if g < G:
                        hd, i, col, nk = st[g]
                        dve.wait_ge(*at("s_mm", (l, g)))
                        if g >= 4:
                            dve.wait_ge(*at("exp", (l, g - 4)))
                        else:
                            dve.wait_ge(*at("att_free", l))
                        sc = scores(g, nk)
                        dve.reduce_max(amax[:, 0, g % 4:g % 4 + 1], sc, AX.X).then_inc(*inc("smax", (l, g)))
                        dve.wait_ge(*at("smax", (l, g)))
                        dve.tensor_scalar(amax[:, 1, g % 4:g % 4 + 1], amax[:, 0, g % 4:g % 4 + 1], -SCALE, None, ALU.mult)\
                           .then_inc(*inc("amax", (l, g)))
                    if g >= 4 and g % 2 == 0 and (g - 4) // 2 < G // 2:
                        pr = (g - 4) // 2
                        hq, pq_ = divmod(pr, npair)
                        dve.wait_ge(*at("yc_lo", (l, hq, pq_)))
                        if pr >= 2:
                            dve.wait_ge(*at(f"yc_store{pr % 2}", ("att", l), plus=16 * (pr // 2)))
                        dve.tensor_tensor(yc[:, pr % 2, :], psum[0:VD, 7, 0:256], yc_lo[:, pr % 2, :], ALU.add)\
                           .then_inc(*inc("yc", (l, hq, pq_)))
                for b in layer_blocks(l):
                    c0, T = BLOCKS[b]
                    s = 1 if b == 0 else 0
                    n0 = start["out", l, b]
                    for k in range(KT):
                        dve.wait_ge(*at("y_hi", (l, b, k)))
                        dve.tensor_tensor(h_lo[:, k, :T], yraw[:, k, :T], h_hi[:, k, :T].bitcast(F32), ALU.subtract)\
                           .then_inc(*inc("y_lo", (l, b, k)))
                    for m in range(KT):
                        split_lo(dve, n0 + m + 2)
                        dve.wait_ge(C.sem("w_used"), n0 + m + 1)
                        dve.scalar_tensor_tensor(X[:, m, c0:c0 + T], psum[:, m % 4, :T], mod[:, l, 16 + m, s:s + 1],
                                                 X[:, m, c0:c0 + T], ALU.mult, ALU.add).then_inc(*inc("out_acc", (l, b, m)))
                    C.alias("out_end", (l, b), "out_acc")
                for b in layer_blocks(l):
                    c0, T = BLOCKS[b]
                    s = 1 if b == 0 else 0
                    n0 = start["ffn", l, b]
                    norm(l, 1, b)
                    C.now("gu32", ("ffn", l, b)); C.now("gu_lo", ("ffn", l, b))
                    g32b, glob = C.total["gu32"], C.total["gu_lo"]
                    sgb, ghib = at("sg", ("ffn", l, b))[1], at("gu_hi", ("ffn", l, b))[1]
                    with dve.Fori(0, FT // 2, 1) as i:
                        for j in range(2):
                            split_lo_loop(dve, n0 + 2, i, 4, 2 * j)
                            split_lo_loop(dve, n0 + 2, i, 4, 2 * j + 1)
                            dve.wait_ge(C.sem("w_used"), i * 4 + (n0 + 2 * j + 2))
                            dve.wait_ge(C.sem("sg"), i * 2 + (sgb + j + 1))
                            dve.wait_ge(C.sem("gu_lo"), i * 2 + (glob + j - 1))
                            dve.tensor_tensor(gu32[:, j, :T], sg[:, j, :T], psum[:, 2 * j + 1, :T], ALU.mult).then_inc(C.sem("gu32"), 1)
                            dve.wait_ge(C.sem("gu_hi"), i * 2 + (ghib + j + 1))
                            f1 = bass.ds(i * 2 + j, 1)
                            dve.tensor_tensor(gu_lo[:, f1, :T].rearrange("p o n -> p (o n)"), gu32[:, j, :T],
                                              gu_hi[:, f1, :T].rearrange("p o n -> p (o n)").bitcast(F32), ALU.subtract)\
                               .then_inc(C.sem("gu_lo"), 1)
                    C.skip("gu32", FT); C.skip("gu_lo", FT); C.skip("w_lo", 2 * FT)
                    n1 = n0 + 2 * FT
                    C.now("dn_acc", ("ffn", l, b))
                    last = n1 + 3 * KT == n_chunks
                    for i in range(2):
                        for m in range(4):
                            for j in range(3):
                                n = n1 + i * 12 + m * 3 + j + 2
                                if n < n_chunks:
                                    dve.wait_ge(C.sem("w_hi"), n + 1)
                                    dve.tensor_tensor(w_lo[:, n % 2, :], raw[:, n % 2, :], w_hi[:, n % 2, :].bitcast(F32), ALU.subtract)\
                                       .then_inc(C.sem("w_lo"), 1)
                            mm = 4 * i + m
                            dve.wait_ge(C.sem("w_used"), n1 + 3 * mm + 3)
                            dve.scalar_tensor_tensor(X[:, mm, c0:c0 + T], psum[:, m, :T], mod[:, l, 40 + mm, s:s + 1],
                                                     X[:, mm, c0:c0 + T], ALU.mult, ALU.add).then_inc(*inc("dn_acc", (l, b, mm)))
                    C.skip("w_lo", 3 * KT)
                    C.alias("dn_acc_end", (l, b), "dn_acc")

        @block.gpsimd
        def _(pool):
            def norm(l, which, b):
                c0, T = BLOCKS[b]
                key = (l, which, b)
                pool.wait_ge(*at("norm_var", key))
                pool.tensor_tensor(rstd[:, :T], var[:, :T], half[:, 0:1].to_broadcast([P, T]), ALU.pow).then_inc(*inc("norm_rstd", key))

            def small_pow(dst, src, n, name, key):
                pool.tensor_tensor(stat[:, dst:dst + n], stat[:, src:src + n], half[:, 0:1].to_broadcast([P, n]), ALU.pow).then_inc(*inc(name, key))

            pool.wait_ge(*at("ones"))
            for l in range(DEPTH):
                for b, (c0, T) in enumerate(BLOCKS):
                    kb, nt_all, lat = (l, b), T // P, b > 0
                    norm(l, 0, b)
                    pool.wait_ge(*at("tok_var", kb))
                    if full(l, b):
                        small_pow(16, 0, nt_all, "tok_r", kb)
                    small_pow(20, 4, nt_all, "tok_r", kb)
                    if full(l, b):
                        for t in range(nt_all):
                            pool.wait_ge(*at("vt_var", (l, b, t)))
                            small_pow(72 + t, 68 + t, 1, "vt_rstd", (l, b, t))
                    for s, nt in sub_tiles(T):
                        for w in ((0, 1) if full(l, b) else (1,)):
                            k2 = (l, b, s, w)
                            if w == 0:
                                pool.wait_ge(*at("q_tok", ((l, b, s + nt - 1), 1)))
                            else:
                                pool.wait_ge(*at("k_tok", ((l, b, s + nt - 1), 1)))
                                pool.wait_ge(*at("krt", (l, b, s)))
                                for t in range(nt):
                                    pool.tensor_copy(qk[:, 1, t, :, NOPE:], krt[:, t, :].unsqueeze(1).to_broadcast([P, HEADS, ROPE]))\
                                        .then_inc(*inc("kr_b", k2))
                                pool.wait_ge(*at("kr_b", k2))
                            a = qk[:, w, :nt].rearrange("p t h d -> p (t h d)")
                            sq = qk_sq[:, :nt].rearrange("p t h d -> p (t h d)")
                            pool.tensor_tensor(sq, a, a, ALU.mult).then_inc(*inc("hd_sq", k2))
                            pool.wait_ge(*at("hd_var", k2))
                            small_pow(112, 96, 8 * nt, "hd_rstd", k2)
                            pool.wait_ge(*at("hd_n", k2))
                            a3 = qk[:, w, :nt].rearrange("p t h d -> p (t h) d")
                            g = pcol("gq" if w == 0 else "gk").unsqueeze(1).to_broadcast([P, 8 * nt, QKD])
                            pool.tensor_tensor(a3, a3, g, ALU.mult).then_inc(*inc("qk_gain" if lat else "qk_done", k2))
                            if lat:
                                pool.wait_ge(*at("qk_gain", k2))
                                tmp = qk_sq[:, :nt].rearrange("p t h d -> p t (h d)")
                                for t in range(nt):
                                    tile = (c0 - CTX) // P + s + t
                                    x = [qk[:, w, t, :, NOPE + e:QKD:2] for e in range(2)]
                                    cs = [trig[:, tile, e, :].unsqueeze(1).to_broadcast([P, HEADS, ROPE // 2]) for e in range(2)]
                                    tt = [tmp[:, t, P * e:P * e + P].rearrange("p (h d) -> p h d", h=HEADS) for e in range(4)]
                                    pool.tensor_tensor(tt[0], x[0], cs[0], ALU.mult)
                                    pool.tensor_tensor(tt[1], x[1], cs[1], ALU.mult)
                                    pool.tensor_tensor(tt[2], x[0], cs[1], ALU.mult)
                                    pool.tensor_tensor(tt[3], x[1], cs[0], ALU.mult).then_inc(*inc("rot", (k2, t)))
                                for t in range(nt):
                                    x = [qk[:, w, t, :, NOPE + e:QKD:2] for e in range(2)]
                                    tt = [tmp[:, t, P * e:P * e + P].rearrange("p (h d) -> p h d", h=HEADS) for e in range(4)]
                                    pool.wait_ge(*at("rot", (k2, nt - 1)))
                                    pool.tensor_tensor(x[0], tt[0], tt[1], ALU.subtract)
                                    pool.tensor_tensor(x[1], tt[2], tt[3], ALU.add).then_inc(*inc("qk_done", k2))
                for g, (c0, L) in enumerate(((0, CTX), (CTX, SEQ))):
                    if g == 0 and not full(l, 0):
                        continue
                    if g == 0 or not full(l, 0):
                        pool.wait_ge(*at("qk_store0", (l, 2, 2, 1, HEADS - 2)))
                        pool.wait_ge(*at("qk_store1", (l, 2, 2, 1, HEADS - 1)))
                        pool.wait_ge(*at("v_store", (l, 2, 2)))
                        pool.wait_ge(*at("ya_store", (l, 2, 2)))
                        pool.wait_ge(*at("b_store", (l, 2, 1)))
                    else:
                        pool.wait_ge(*at("yb_store", (l, 0, 1, 0)))
                    pool.memset(pz[:, :, 0:HALO], 0.0).then_inc(*inc("pool_edge", (l, g)))
                    pool.memset(pz[:, :, HALO + L:2 * HALO + L], 0.0).then_inc(*inc("pool_edge", (l, g)))
                    pool.wait_ge(*at("pz_in", (l, g)))
                    pool.wait_ge(*at("pinv_in", (l, g)))
                    pool.wait_ge(*at("pool_edge", (l, g)))
                    W2 = L + 2 * HALO

                    def step(dst, src, d, lo, hi, parts=slice(None)):
                        up = 0 if d == 0 else d
                        pool.tensor_tensor(dst[parts, lo:hi], src[parts, lo - max(d, 1):hi - max(d, 1)], src[parts, lo + up:hi + up],
                                           ALU.add).then_inc(*inc("win", (l, g)))
                        pool.wait_ge(C.sem("win"), C.total["win"])

                    def means(i, parts, ssrc):
                        pool.tensor_tensor(pd[parts, i, :L], ssrc[parts, HALO:HALO + L], pinv[parts, i, :L], ALU.mult)\
                            .then_inc(*inc("win", (l, g)))
                        pool.wait_ge(C.sem("win"), C.total["win"])
                        pool.tensor_tensor(pd[parts, i, :L], pd[parts, i, :L], pz[parts, i, HALO:HALO + L], ALU.subtract)\
                            .then_inc(*inc("pool_d", (l, g, i)))
                        pool.wait_ge(C.sem("pool_d"), C.total["pool_d"])
                    lower, upper = slice(0, 64), slice(64, 128)
                    step(ps2, pz[:, 0, :], 0, 1, W2)
                    step(ps4, ps2, 1, 2, W2 - 1)
                    means(0, lower, ps2)
                    means(0, upper, ps4)
                    step(ps2, pz[:, 1, :], 0, 1, W2)
                    step(ps4, ps2, 1, 2, W2 - 1)
                    step(ps2, ps4, 2, 4, W2 - 3)
                    means(1, lower, ps2)
                    step(ps4, ps2, 4, 8, W2 - 8)
                    means(1, upper, ps4)
                C.alias("pool_done", l, "pool_d")
                st, groups = att_plan(l)
                pool.wait_ge(*at("yb_store", (l, 1, 1, SEQ - NMAX)))
                pool.wait_ge(*at("ones"))
                pool.tensor_copy(rstd[:, 0:1], half[:, 0:1]).then_inc(*inc("att_free", l))
                for g, (hd, i, col, nk) in enumerate(st):
                    pool.wait_ge(*at("rden", (l, g)))
                    pool.tensor_tensor(prob[:, g % 4, 0:nk * P], prob[:, g % 4, 0:nk * P],
                                       den[:, 1, g % 4:g % 4 + 1].to_broadcast([P, nk * P]), ALU.mult).then_inc(*inc("pn", (l, g)))
                for b in layer_blocks(l):
                    norm(l, 1, b)

        @block.tensor
        def _(pe):
            def three(out, wh, wl, hh, hl, first, last, inc_last=None):
                pe.matmul(out, wh, hh, start=first, stop=False)
                pe.matmul(out, wh, hl, start=False, stop=False)
                return pe.matmul(out, wl, hh, start=False, stop=last)

            def norm(l, which, b):
                c0, T = BLOCKS[b]
                key = (l, which, b)
                pe.wait_ge(*at("norm_ssum", key))
                pe.wait_ge(*at("ones"))
                pe.matmul(psum[:, 7, :T], ones[:, :], ssum[:, :T], start=True, stop=True).then_inc(*inc("norm_mm", key))

            pe.wait_ge(*at("silu_c"))
            for j in range(DEPTH * ADA_N):
                l, m = divmod(j, ADA_N)
                pe.wait_ge(*at(f"ada_in{j % 3}", j))
                for h in range(ADA_W // P):
                    col = (m * (ADA_W // P) + h) * 2
                    for k in range(KT):
                        x = pe.matmul(psum[:, 4 + l, col:col + 2], ada_w[:, j % 3, k, h * P:(h + 1) * P], silu_c[:, 1, k, :],
                                      start=(k == 0), stop=(k == KT - 1))
                x.then_inc(*inc("ada_mm", j))

            for l in range(DEPTH):
                for b, (c0, T) in enumerate(BLOCKS):
                    n0, cs = start["p1", l, b], P1_CHUNKS[full(l, b)]
                    kb, nt_all = (l, b), T // P
                    if l == 0 and b == 0:
                        pe.wait_ge(*at("ada_end"))
                        pe.wait_ge(*at("consts"))
                    norm(l, 0, b)
                    for i, c in enumerate(cs):
                        n = n0 + i
                        if c >= N_IN:
                            continue
                        pe.wait_ge(*at("w_lo", n))
                        if i >= 2:
                            pe.wait_ge(*at("in_free", (kb, i - 2)))
                        elif (l, b) > (0, 0):
                            prev_banks(pe, l, b)
                        for k in range(KT):
                            if i == 0:
                                pe.wait_ge(*at("h_lo", ((l, 0, b), k)))
                            x = three(psum[:, i % 2, :T], w_hi[:, n % 2, k * P:(k + 1) * P], w_lo[:, n % 2, k * P:(k + 1) * P],
                                      h_hi[:, k, :T], h_lo[:, k, :T], k == 0, k == KT - 1)
                        x.then_inc(*inc("w_used", n))
                    pe.wait_ge(*at("pq_sq", (kb, 2)))
                    if (l, b) > (0, 0):
                        pass
                    for t in range(nt_all):
                        if full(l, b):
                            for k in range(2):
                                pe.matmul(psum[:, 3, t:t + 1], pq_sq[:, k, t * P:(t + 1) * P], ones[:, 0:1], start=(k == 0), stop=(k == 1))
                        x = pe.matmul(psum[:, 3, 4 + t:5 + t], pq_sq[:, 2, t * P:(t + 1) * P], ones[:, 0:1], start=True, stop=True)
                    x.then_inc(*inc("tok_mm", kb))
                    if full(l, b):
                        pe.wait_ge(*at("in_free", (kb, 3)))
                        for s, nt in sub_tiles(T):
                            for t in range(nt):
                                key = (l, b, s + t)
                                if s + t:
                                    pe.wait_ge(*at("vt_sq", (l, b, s + t - 1)))
                                cols = slice((s + t) * P, (s + t + 1) * P)
                                for i in range(2):
                                    x = pe.transpose(psum[:, 2, i * P:(i + 1) * P], v_sb[:, i, cols], ident[:, :])
                                x.then_inc(*inc("mix_tr", key))
                                pe.wait_ge(*at("vt_n", key))
                                if s and t == 0:
                                    pe.wait_ge(*at("mix_g", (l, b, s - 2, 1)))
                                for hd in range(4):
                                    rows = slice(64 * (hd % 2), 64 * (hd % 2) + 64)
                                    x = pe.matmul(psum[rows, 4 + hd // 2, t * P:(t + 1) * P], vtok[:, t, hd * 64:(hd + 1) * 64],
                                                  pcol("wsp", hd * P, (hd + 1) * P), start=True, stop=True)
                                x.then_inc(*inc("mix_mm", key))
                        pe.wait_ge(*at("mix_g", (l, b, sub_tiles(T)[-1][0], 1)))
                    pe.wait_ge(*at("wqkv_lo", l))
                    pe.wait_ge(*at("pq_lo", (kb, 2)))
                    pe.wait_ge(*at("tok_var", kb))
                    for s, nt in sub_tiles(T):
                        for t in range(nt):
                            key = (l, b, s + t)
                            ts = slice((s + t) * P, (s + t + 1) * P)
                            if full(l, b):
                                for c in range(2):
                                    if s + t:
                                        pe.wait_ge(*at("q_tok", ((l, b, s + t - 1), c)))
                                    for k in range(2):
                                        kc = slice(k * NQ + c * NQ // 2, k * NQ + (c + 1) * NQ // 2)
                                        x = three(psum[:, 4 + c, 0:NQ // 2], pq_hi[:, k, ts], pq_lo[:, k, ts],
                                                  wqkv_hi[:, kc], wqkv_lo[:, kc], k == 0, k == 1)
                                    x.then_inc(*inc("q_mm", (key, c)))
                            for c in range(2):
                                if s + t:
                                    pe.wait_ge(*at("v_lo_t", ((l, b, s + t - 1), c)))
                                    pe.wait_ge(*at("k_tok", ((l, b, s + t - 1), c)))
                                kc = slice(2 * NQ + c * NKV // 2, 2 * NQ + (c + 1) * NKV // 2)
                                three(psum[:, 6 + c, :], pq_hi[:, 2, ts], pq_lo[:, 2, ts], wqkv_hi[:, kc], wqkv_lo[:, kc], True, True)\
                                    .then_inc(*inc("kv_mm", (key, c)))
                        pe.wait_ge(*at("kr_sb", kb))
                        if s:
                            pe.wait_ge(*at("qk_lo", (l, b, s - 2, 1, HEADS - 1)))
                        for t in range(nt):
                            x = pe.transpose(psum[:, 3, t * P:(t + 1) * P], kr_sb[:, (s + t) * P:(s + t + 1) * P], ident[:, :])
                        x.then_inc(*inc("kr_tr", (l, b, s)))
                        for w in ((0, 1) if full(l, b) else (1,)):
                            pe.wait_ge(*at("qk_done", (l, b, s, w)))
                            for hd in range(HEADS):
                                if hd >= 2:
                                    pe.wait_ge(*at("qk_lo", (l, b, s, w, hd - 2)))
                                elif w == 1 and full(l, b):
                                    pe.wait_ge(*at("qk_lo", (l, b, s, 0, HEADS - 2 + hd)))
                                if hd == 1:
                                    pe.wait_ge(*at("krt", (l, b, s)))
                                for t in range(nt):
                                    x = pe.transpose(psum[:QKD, 2 + hd % 2, t * P:(t + 1) * P], qk[:, w, t, hd, :], ident[:, :])
                                x.then_inc(*inc("qk_tr", (l, b, s, w, hd)))
                for g, (c0, L) in enumerate(((0, CTX), (CTX, SEQ))):
                    if g == 0 and not full(l, 0):
                        continue
                    for i in range(2):
                        pe.wait_ge(*at("pool_d", (l, g, i)))
                        for q in range(0, L, NMAX):
                            w = min(NMAX, L - q)
                            if i or q or (g and full(l, 0)):
                                prev = pool_seq(l)[pool_seq(l).index((l, g, i, q)) - 1]
                                pe.wait_ge(*at("pool_out", prev))
                            pe.matmul(psum[:, (i * 2 + q // NMAX) % 2, :w], pcol("wpool", i * P, i * P + P), pd[:, i, q:q + w],
                                      start=True, stop=True).then_inc(*inc("pool_mm", (l, g, i, q)))
                st, groups = att_plan(l)
                G, per = len(st), len(steps(l))
                npair = per // 2
                pe.wait_ge(*at("pool_out", pool_seq(l)[-1]))
                for g in range(G + 4):
                    def t_group(q, tg, k0, n):
                        if k0 == 0:
                            pe.wait_ge(*at("pn", (l, q)))
                        if tg >= 2:
                            pe.wait_ge(*at("t_lo", (l, tg - 2)))
                        for k in range(n):
                            x = pe.transpose(psum[:, 5 + tg % 2, k * P:(k + 1) * P], prob[:, q % 4, (k0 + k) * P:(k0 + k + 1) * P],
                                             ident[:, :])
                        x.then_inc(*inc("t_mm", (l, tg)))

                    def s_part(hd, i, col, nk, part):
                        j = hd % 2
                        k0, w = score_parts(g, nk)[part]
                        if part == 0:
                            if i == 0:
                                pe.wait_ge(*at(f"kqv{j}", ("att", l), plus=48 * (hd // 2 + 1)))
                            if g >= 2:
                                pe.wait_ge(*at("exp", (l, g - 2)))
                        if part == len(score_parts(g, nk)) - 1 and g >= 1:
                            pe.wait_ge(*at("exp", (l, g - 1)))
                        kc, qc = slice(k0, k0 + w), slice(col, col + P)
                        return three(scores(g, nk)[:, kc], qh[:, j, 0, qc], qh[:, j, 1, qc], kh[:, j, 0, kc], kh[:, j, 1, kc], True, True)
                    ts = groups[g - 2] if 0 <= g - 2 < G else []
                    n_parts = len(score_parts(g, st[g][3])) if g < G else 0
                    for part in range(3):
                        if part < len(ts):
                            t_group(g - 2, *ts[part])
                        if part < n_parts:
                            x = s_part(*st[g], part)
                            if part == n_parts - 1:
                                x.then_inc(*inc("s_mm", (l, g)))
                    if g >= 4 and g % 2 == 0 and (g - 4) // 2 < G // 2:
                        pr = (g - 4) // 2
                        hq, pi = divmod(pr, npair)
                        nk = steps(l)[2 * pi][1]
                        pe.wait_ge(*at("t_lo", (l, groups[2 * pr + 1][-1][0])))
                        if pr >= 1:
                            h2, p2 = divmod(pr - 1, npair)
                            pe.wait_ge(*at("yc", (l, h2, p2)))
                        out = psum[:, 7, 0:256]
                        for k in range(nk):
                            pe.matmul(out, vh[:, hq % 2, k, :], pt_hi[:, pr % 2, k, :], start=(k == 0), stop=False)
                            x = pe.matmul(out, vh[:, hq % 2, k, :], pt_lo[:, pr % 2, k, :], start=False, stop=(k == nk - 1))
                        x.then_inc(*inc("pv_mm", (l, hq, pi)))
                for b in layer_blocks(l):
                    c0, T = BLOCKS[b]
                    n0 = start["out", l, b]
                    for m in range(KT):
                        n = n0 + m
                        pe.wait_ge(*at("w_lo", n))
                        if m >= 4:
                            pe.wait_ge(*at("out_acc", (l, b, m - 4)))
                        elif b != layer_blocks(l)[0]:
                            pe.wait_ge(*at("out_acc", (l, b - 1, m + 4)))
                        else:
                            pe.wait_ge(*at("yc", (l, HEADS - 1, npair - 1)))
                        for k in range(KT):
                            if m == 0:
                                pe.wait_ge(*at("y_lo", (l, b, k)))
                            x = three(psum[:, m % 4, :T], w_hi[:, n % 2, k * P:(k + 1) * P], w_lo[:, n % 2, k * P:(k + 1) * P],
                                      h_hi[:, k, :T], h_lo[:, k, :T], k == 0, k == KT - 1)
                        x.then_inc(*inc("w_used", n))
                for b in layer_blocks(l):
                    c0, T = BLOCKS[b]
                    n0 = start["ffn", l, b]
                    norm(l, 1, b)
                    for k in range(KT):
                        pe.wait_ge(*at("h_lo", ((l, 1, b), k)))
                    prev = layer_blocks(l).index(b)
                    pe.wait_ge(*(at("out_acc", (l, layer_blocks(l)[-1], KT - 1)) if prev == 0 else
                                 at("dn_acc_end", (l, layer_blocks(l)[prev - 1]))))
                    g32b = at("gu32", ("ffn", l, b))[1]
                    sgb = at("sg", ("ffn", l, b))[1]
                    with pe.Fori(0, FT // 2, 1) as i:
                        for j in range(4):
                            n = n0 + j
                            pe.wait_ge(C.sem("w_lo"), i * 4 + (n + 1))
                            if j % 2 == 0:
                                pe.wait_ge(C.sem("sg"), i * 2 + (sgb + j // 2 - 1))
                            else:
                                pe.wait_ge(C.sem("gu32"), i * 2 + (g32b + j // 2 - 1))
                            for k in range(KT):
                                x = three(psum[:, j, :T], w_hi[:, n % 2, k * P:(k + 1) * P], w_lo[:, n % 2, k * P:(k + 1) * P],
                                          h_hi[:, k, :T], h_lo[:, k, :T], k == 0, k == KT - 1)
                            x.then_inc(C.sem("w_used"), 1)
                    C.skip("w_used", 2 * FT)
                    n1 = n0 + 2 * FT
                    pe.wait_ge(*at("gu_lo", ("ffn", l, b), plus=FT))
                    dnb = at("dn_acc", ("ffn", l, b))[1]
                    for m in range(KT):
                        k0 = 0
                        for j, nk in enumerate(DN_K):
                            n = n1 + 3 * m + j
                            pe.wait_ge(C.sem("w_lo"), n + 1)
                            if j == 0 and m >= 4:
                                pe.wait_ge(*at("dn_acc", (l, b, m - 4)))
                            for k in range(nk):
                                f = k0 + k
                                x = three(psum[:, m % 4, :T], w_hi[:, n % 2, k * P:(k + 1) * P], w_lo[:, n % 2, k * P:(k + 1) * P],
                                          gu_hi[:, f, :T], gu_lo[:, f, :T], f == 0, f == FT - 1)
                            x.then_inc(C.sem("w_used"), 1)
                            k0 += nk
                    C.skip("w_used", 3 * KT)
    return C


def kernel(**inputs):
    import numpy as np
    import concourse.bacc as bacc
    from concourse import mybir as mb
    from concourse.bass_utils import run_bass_kernel_spmd as run

    a = {k: np.asarray(v) for k, v in inputs.items()}

    def tiles(w):
        return w.reshape(-1, P, w.shape[-1]).transpose(1, 0, 2)

    def cols(v):
        return v.reshape(-1, P).T

    def chunk(w):
        w = tiles(w).reshape(P, -1)
        return np.pad(w, ((0, 0), (0, CH - w.shape[1])))

    chunks, prm, ada_p, w_ada, wqkv = [], [], [], [], []
    for l in range(DEPTH):
        w_in = a["w_in"][l]
        cs = [chunk(w_in[:, P * m:P * m + P]) for m in range(9)] + [chunk(w_in[:, -P:])]
        cs += [chunk(a["w_out"][l][:, P * m:P * m + P]) for m in range(KT)]
        gu = a["w_gate_up"][l]
        for f in range(FT):
            cs += [chunk(gu[:, P * f:P * f + P]), chunk(gu[:, DFF + P * f:DFF + P * f + P])]
        for m in range(KT):
            k0 = 0
            for nk in DN_K:
                cs.append(chunk(a["w_down"][l][k0 * P:(k0 + nk) * P, P * m:P * m + P]))
                k0 += nk
        chunks.append(np.stack(cs))
        wqkv.append(np.concatenate([tiles(a["w_q_b"][l]).reshape(P, -1), a["w_kv_b"][l]], 1))
        pool = np.zeros((P, 2, P), np.float32)
        for g in range(4):
            pool[64 * (g % 2):64 * (g % 2) + 64, g // 2, 64 * (g % 2):64 * (g % 2) + 64] = a["w_pool"][l][g]
        bsp = np.repeat(a["b_spatial"][l].reshape(2, 2, P), 64, axis=1).transpose(1, 0, 2)
        prm.append(np.concatenate([
            cols(a["sgu_norm_g"][l]), cols(a["pool_scale"][l]), cols(a["q_a_norm_g"][l]), cols(a["kv_a_norm_g"][l]),
            np.broadcast_to(a["q_norm_g"][l], (P, QKD)), np.broadcast_to(a["k_norm_g"][l], (P, QKD)),
            bsp.reshape(P, -1), pool.reshape(P, -1), a["w_spatial"][l].transpose(2, 0, 1).reshape(P, -1)], 1))
        ada_p.append(np.concatenate([cols(a["norm1_g"][l]), cols(a["norm2_g"][l]), cols(a["b_ada"][l])], 1))
        w_ada.append(tiles(a["w_ada"][l]).reshape(P, KT, ADA_N, ADA_W).transpose(2, 0, 1, 3))

    def inv(n):
        t = np.arange(n)
        g = [1.0 / (np.clip(t + w // 2, 0, n) - np.clip(t - w // 2, 0, n)) for w in WINDOWS]
        return np.repeat(np.stack(g).reshape(2, 2, n), 64, axis=1).transpose(1, 0, 2).astype(np.float32)

    row, col = np.divmod(np.arange(SEQ), 64)
    f = np.float32(10000.0) ** (-np.arange(ROPE // 4, dtype=np.float32) / np.float32(ROPE // 4))
    ang = np.concatenate([row[:, None].astype(np.float32) * f, col[:, None].astype(np.float32) * f], -1).astype(np.float32)
    trig = np.stack([np.cos(ang), np.sin(ang)], 1).reshape(SEQ // P, P, 2, ROPE // 2).transpose(1, 0, 2, 3)

    arrays = {
        "x": np.concatenate([a["ctx"][0], a["x"][0]]).T,
        "c": np.stack([cols(a["c"][0]), cols(a["c_ctx"])], -1),
        "w": np.stack(chunks), "prm": np.stack(prm), "ada_p": np.stack(ada_p, 1), "w_ada": np.stack(w_ada),
        "wqkv": np.stack(wqkv), "inv_lat": inv(SEQ), "inv_ctx": inv(CTX), "trig": trig.astype(np.float32),
        "ident": np.eye(P, dtype=np.float32),
    }
    arrays = {k: np.ascontiguousarray(v) for k, v in arrays.items()}

    def program(known):
        nc = bacc.Bacc("TRN2", target_bir_lowering=False, num_devices=1)
        t_in = {k: nc.dram_tensor(f"in_{k}", v.shape, mb.dt.from_np(v.dtype), kind="ExternalInput").ap() for k, v in arrays.items()}
        t_in["out"] = nc.dram_tensor("out_0", (DM, SEQ), F32, kind="ExternalOutput").ap()
        return nc, build(nc, t_in, known)

    _, counts = program({})
    nc, _ = program(counts.value)
    r = run(nc, [{f"in_{k}": v for k, v in arrays.items()}], core_ids=[0])
    return np.ascontiguousarray(r.results[0]["out_0"].T)[None]
```

```python
import math
from contextlib import ExitStack

import concourse.bass as bass
from concourse import mybir

F32 = mybir.dt.float32
F32R = mybir.dt.float32r
ALU = mybir.AluOpType
ACT = mybir.ActivationFunctionType
AX = mybir.AxisListType

P = 128
DM = 1024
KT = DM // P
CTX = 256
SEQ = 1024
NTOK = CTX + SEQ
DEPTH = 2
HEADS = 8
VD = 64
NOPE = 64
ROPE = 32
QKD = NOPE + ROPE
DFF = 2816
FT = DFF // P
WINDOWS = (2, 4, 8, 16)
HALO = max(WINDOWS) // 2
EPS = 1e-6
SCALE = QKD ** -0.5

BLOCKS = ((0, CTX), (CTX, 512), (CTX + 512, 512))
NMAX = 512
CH = KT * P

C_IN, N_IN = 0, 10
C_OUT = C_IN + N_IN
C_GU = C_OUT + KT
DN_K = (8, 7, 7)
C_DN = C_GU + 2 * FT
NCH = C_DN + KT * len(DN_K)
P1_CHUNKS = {True: tuple(range(N_IN)), False: (8, 9)}
NQ = HEADS * QKD
NKV = HEADS * (NOPE + VD)

PRM = {}
_at = 0
for _n, _w in (("sgu", 2), ("pscale", 2), ("qa", 2), ("kva", 1),
               ("gfull", 2), ("gnope", 2), ("grope", 2 * ROPE), ("bsp", 256), ("wpool", 256), ("wsp", 512)):
    PRM[_n] = (_at, _at + _w)
    _at += _w
NPRM = _at
N_ST = 4

ADA_W = 512
ADA_K = 4
ADA_M = 6 * DM // ADA_W
ADA_N = ADA_M * KT // ADA_K


def full(l, b):
    return not (l == DEPTH - 1 and b == 0)


def layer_blocks(l):
    return [b for b in range(len(BLOCKS)) if full(l, b)]


class Count:

    def __init__(self, nc, ctx, known):
        self.nc, self.ctx, self.known = nc, ctx, known
        self.sems, self.total, self.value = {}, {}, {}

    def sem(self, name):
        if name not in self.sems:
            self.sems[name] = self.ctx.enter_context(self.nc.semaphore(name))
            self.total[name] = 0
        return self.sems[name]

    def inc(self, name, key=None, by=1):
        s = self.sem(name)
        self.total[name] += by
        self.value[name, key] = name, self.total[name]
        return s, by

    def alias(self, name, key, of):
        self.value[name, key] = of, self.total[of]

    def skip(self, name, n):
        self.sem(name)
        self.total[name] += n

    def now(self, name, tag):
        self.sem(name)
        self.value[name, tag] = name, self.total[name]

    def at(self, name, key=None, plus=0):
        of, value = self.known.get((name, key), (name, 1))
        return self.sem(of), value + plus


def build(nc, t_in, known):
    ctx = ExitStack()
    with ctx:
        C = Count(nc, ctx, known)
        inc, at = C.inc, C.at

        def sb(name, shape, dt=F32):
            return ctx.enter_context(nc.sbuf_tensor(name, shape, dt))

        X = sb("X", [P, KT, NTOK])
        raw = sb("raw", [P, 2, CH])
        w_hi = sb("w_hi", [P, 2, CH], F32R)
        w_lo = sb("w_lo", [P, 2, CH], F32R)
        prm = sb("prm", [P, NPRM])
        ada_p = sb("ada_p", [P, DEPTH, 64])
        mod = sb("mod", [P, DEPTH, 48, 2])
        gain = sb("gain", [P, DEPTH, 2, KT, 2])
        ident = sb("ident", [P, P])
        ones = sb("ones", [P, P])
        half = sb("half", [P, 1])
        t32 = sb("t32", [P, 2, NMAX])
        silu_c = sb("silu_c", [P, 2, KT, 2])
        silu_s = sb("silu_s", [P, KT, 4], F32R)
        diag = sb("diag", [P, NMAX])
        flag = sb("flag", [P, 8])
        nst = sb("nst", [P, 8])
        trig = sb("trig", [P, SEQ // P, 2, ROPE // 2])
        var, ssum = t32[:, 0, :], t32[:, 1, :]

        psum = ctx.enter_context(nc.psum_tensor("psum", [P, 8, 512], F32))

        qk_scr = nc.dram_tensor("qk_scr", [DEPTH, 2, HEADS, QKD, 2, NTOK], F32).ap()
        v_scr = nc.dram_tensor("v_scr", [DEPTH, HEADS, NTOK, 2 * VD], F32).ap()
        y_scr = nc.dram_tensor("y_scr", [DEPTH, DM, NTOK], F32).ap()
        b_scr = nc.dram_tensor("b_scr", [DEPTH, 2, P, NTOK], F32).ap()

        def overlay(specs):
            with ExitStack() as st:
                return [st.enter_context(nc.sbuf_tensor(n, s, d)) for n, s, d in specs]

        kh, qh, vh, prob, pt_hi, pt_lo, yc, yc_lo, amax, den = overlay([
            ("kh", [QKD, 2, 2, NTOK], F32R), ("qh", [QKD, 2, 2, NTOK], F32R),
            ("vh", [P, 2, NTOK // P, 2 * VD], F32R), ("prob", [P, 4, NTOK], F32),
            ("pt_hi", [P, 2, NTOK // P, 256], F32R), ("pt_lo", [P, 2, NTOK // P, 256], F32R),
            ("yc", [VD, 2, 256], F32), ("yc_lo", [VD, 2, 256], F32),
            ("amax", [P, 2, 4], F32), ("den", [P, 2, 4], F32)])
        h_hi = sb("h_hi", [P, KT, NMAX], F32R)
        h_lo = sb("h_lo", [P, KT, NMAX], F32R)
        _, ada_raw, ada_hi, ada_lo, ada_row = overlay([
            ("yraw_place", [P, KT, NMAX], F32), ("ada_raw", [P, 2, ADA_K, ADA_W], F32),
            ("ada_hi", [P, 2, ADA_K, ADA_W], F32R), ("ada_lo", [P, 2, ADA_K, ADA_W], F32R),
            ("ada_row", [4, 2, ADA_W], F32)])
        (nrm_t, wqkv_hi, wqkv_lo, pq_hi, pq_lo, u_sb, v_sb, vtok, kr_sb, qk, qk_sq, v_st, st_qk, mixo, yst,
         stat, krt) = overlay([
             ("nrm_t", [P, 4, NMAX], F32), ("wqkv_hi", [P, 2 * NQ + NKV], F32R), ("wqkv_lo", [P, 2 * NQ + NKV], F32R),
             ("pq_hi", [P, 3, NMAX], F32R), ("pq_lo", [P, 3, NMAX], F32R),
             ("u_sb", [P, 2, NMAX], F32), ("v_sb", [P, 2, NMAX], F32),
             ("vtok", [P, 4, 256], F32), ("kr_sb", [P, NMAX], F32),
             ("qk", [P, 2, 2, HEADS, QKD], F32), ("qk_sq", [P, 2, HEADS, QKD], F32),
             ("v_st", [P, 2, HEADS, 2, VD], F32R), ("st_qk", [QKD, N_ST, 2, 256], F32R),
             ("mixo", [P, 2, 256], F32), ("yst", [P, 2, NMAX], F32),
             ("stat", [P, 256], F32), ("krt", [P, 2, ROPE], F32)])
        pq32 = nrm_t
        pq_sq = qk_sq[:, :, :, :].rearrange("p t h d -> p (t h d)")[:, 0:3 * NMAX].rearrange("p (j n) -> p j n", n=NMAX)
        pz, ps2, ps4, pinv, pd = overlay([
            ("pz", [P, 2, SEQ + 2 * HALO], F32), ("ps2", [P, SEQ + 2 * HALO], F32),
            ("ps4", [P, SEQ + 2 * HALO], F32), ("pinv", [P, 2, SEQ], F32), ("pd", [P, 2, SEQ], F32)])
        yraw, = overlay([("yraw", [P, KT, NMAX], F32)])
        fnrm_t, gu_hi, gu_lo = overlay([
            ("fnrm_t", [P, 4, NMAX], F32), ("gu_hi", [P, FT, NMAX], F32R), ("gu_lo", [P, FT, NMAX], F32R)])
        sg, gu32 = fnrm_t[:, 0:2, :], fnrm_t[:, 2:4, :]

        def pcol(name, a=0, b=None):
            s, e = PRM[name]
            return prm[:, s + a:(s + b if b is not None else e)]

        block = ctx.enter_context(nc.Block())

        start, stream = {}, []
        for l in range(DEPTH):
            for b in range(len(BLOCKS)):
                start["p1", l, b] = len(stream)
                stream += [(l, c) for c in P1_CHUNKS[full(l, b)]]
            for b in layer_blocks(l):
                start["out", l, b] = len(stream)
                stream += [(l, c) for c in range(C_OUT, C_GU)]
            for b in layer_blocks(l):
                start["ffn", l, b] = len(stream)
                stream += [(l, c) for c in range(C_GU, NCH)]
        n_chunks = len(stream)

        def steps(l):
            lat = [(CTX + P * t, NTOK // P) for t in range(SEQ // P)]
            return lat + ([(P * t, CTX // P) for t in range(CTX // P)] if l < DEPTH - 1 else [])

        def t_groups(nk):
            return [(k, min(4, nk - k)) for k in range(0, nk, 4)]

        sub_tiles = lambda T: [(s, min(2, T // P - s)) for s in range(0, T // P, 2)]

        def mixsq(t):
            return qk_sq[:, t].rearrange("p h d -> p (h d)")[:, 0:256]

        def at_prev(l, b):
            seq = [(i, j) for i in range(DEPTH) for j in range(len(BLOCKS)) if full(i, j)]
            before = [x for x in seq if x < (l, b)]
            return before[-1]

        def p1_schedule(l):
            seq = [("norm", 0), ("in", 0, 0, 10), ("wqkv",), ("norm", 1), ("mix", 0), ("tok", 0, 0),
                   ("in", 1, 0, 5), ("head", 0, 0), ("in", 1, 5, 10), ("norm", 2), ("mix", 1), ("tok", 1, 0),
                   ("in", 2, 0, 5), ("head", 1, 0), ("tok", 1, 2), ("in", 2, 5, 10), ("head", 1, 2),
                   ("tok", 2, 0), ("mix", 2), ("head", 2, 0), ("tok", 2, 2), ("head", 2, 2)]
            if l:
                seq = seq[1:]
            return [x for x in seq if x[0] != "mix" or full(l, x[1])]

        def p1_pos(l, x):
            return [y[:len(x)] for y in p1_schedule(l)].index(x)

        def p1_before(h, l, b):
            if h[0] != l:
                return h[0] < l
            end = max(i for i, y in enumerate(p1_schedule(l)) if y[:2] == ("in", b))
            if mix_late(l, b):
                end = p1_pos(l, ("mix", b))
            return p1_pos(l, ("head",) + h[1:3]) < end

        def mix_late(l, b):
            return False

        def tok_before(x, l, b):
            return x[0] < l or (x[0] == l and p1_pos(l, ("tok", x[1], x[2] // 2 * 2)) < p1_pos(l, ("mix", b)))

        def tok_products(l, b, s, t):
            return ([("q", 0), ("q", 1)] if full(l, b) else []) + [("kv", 0), ("kv", 1)]

        tok_seq = []
        for _l in range(DEPTH):
            for _x in p1_schedule(_l):
                if _x[0] == "tok":
                    for _t in range(dict(sub_tiles(BLOCKS[_x[1]][1]))[_x[2]]):
                        tok_seq += [(_l, _x[1], _x[2] + _t) + p for p in tok_products(_l, _x[1], _x[2], _t)]

        def tok_bank(l, b, t, kind, c):
            return 4 + tok_seq.index((l, b, t, kind, c)) % 3

        def norm_next(l, b):
            i = layer_blocks(l).index(b)
            if i + 1 < len(layer_blocks(l)):
                return l, 1, layer_blocks(l)[i + 1]
            return (l + 1, 0, 0) if l + 1 < DEPTH else None

        def pool_seq(l):
            return [(l, g, i, q) for g, L in enumerate((CTX, SEQ)) if g or full(l, 0) for i in range(2) for q in range(0, L, NMAX)]

        def prev_banks(pe, l, b):
            pl, pb = (l, b - 1) if b else (l - 1, len(BLOCKS) - 1)
            if b:
                pe.wait_ge(*at("kr_sb", (pl, pb)))
            else:
                pe.wait_ge(*at("dn_acc_end", (pl, pb)))

        def subs():
            return [(l, x[1], x[2]) for l in range(DEPTH) for x in p1_schedule(l) if x[0] == "tok"]

        def prev_sub_wait(eng, l, b, s, w):
            i = subs().index((l, b, s))
            if i == 0:
                return
            pl, pb, pss = subs()[i - 1]
            if w == 1 or full(pl, pb):
                eng.wait_ge(*at("qk_tr", (pl, pb, pss, w, HEADS - 1)))
            if w == 1:
                eng.wait_ge(*at("v_store", (pl, pb, pss)))

        def head_seq():
            return [(l, b, s, w, h) for l, b, s in subs() for w in ((0, 1) if full(l, b) else (1,)) for h in range(HEADS)]

        def prev_head_wait(eng, l, b, s, w, hd):
            i = head_seq().index((l, b, s, w, hd))
            if i >= N_ST:
                eng.wait_ge(*at(f"qk_store{hd % N_ST}", head_seq()[i - N_ST]))

        def att_plan(l):
            st, tg = [], []
            for hd in range(HEADS):
                for i, (col, nk) in enumerate(steps(l)):
                    st.append((hd, i, col, nk))
            out = []
            for g, (hd, i, col, nk) in enumerate(st):
                grp = []
                for k0, n in t_groups(nk):
                    grp.append((len(tg), k0, n))
                    tg.append((g, k0, n))
                out.append(grp)
            return st, out

        psum_flat = psum[:, :, :].rearrange("p a n -> p (a n)")

        def scores(g, nk):
            at0 = (g % 2) * NTOK
            return psum_flat[:, at0:at0 + nk * P]

        def score_parts(g, nk):
            cuts = (0, 512, 1024, NTOK) if g % 2 == 0 else (0, 256, 768, NTOK)
            parts = [(a, min(b, nk * P) - a) for a, b in zip(cuts, cuts[1:]) if a < nk * P]
            return parts if g % 2 == 0 else parts[1:] + parts[:1]

        def att_act(act, l):
            st, groups = att_plan(l)
            G = len(st)
            per = len(steps(l))
            npair = per // 2
            for g in range(G + 4):
                if 0 <= g - 2 < G:
                    q = g - 2
                    for tg, k0, n in groups[q]:
                        act.wait_ge(*at("t_mm", (l, tg)))
                        if k0 == 0 and q // 2 >= 2:
                            hq, pq_ = divmod(q // 2 - 2, npair)
                            act.wait_ge(*at("pv_mm", (l, hq, pq_)))
                        if k0 == 0 and q // 2 < 2:
                            act.wait_ge(*at("att_free", l))
                        act.activation(pt_hi[:, (q // 2) % 2, k0:k0 + n, (q % 2) * P:(q % 2) * P + P],
                                       psum[:, 5 + tg % 2, 0:n * P].rearrange("p (k n) -> p k n", n=P), ACT.Copy)\
                           .then_inc(*inc("t_hi", (l, tg)))
                if g < G:
                    hd, i, col, nk = st[g]
                    act.wait_ge(*at("amax", (l, g)))
                    if g >= 4:
                        act.wait_ge(*at("t_mm", (l, groups[g - 4][-1][0])))
                    sc = scores(g, nk)
                    act.activation(prob[:, g % 4, 0:nk * P], sc, ACT.Exp, bias=amax[:, 1, g % 4:g % 4 + 1], scale=SCALE,
                                   accum_out=den[:, 0, g % 4:g % 4 + 1]).then_inc(*inc("exp", (l, g)))
                if g >= 4 and g % 2 == 0 and (g - 4) // 2 < G // 2:
                    pr = (g - 4) // 2
                    hq, pq_ = divmod(pr, npair)
                    act.wait_ge(*at("pv_mm", (l, hq, pq_)))
                    if pr >= 2:
                        h2, p2 = divmod(pr - 2, npair)
                        act.wait_ge(*at("yc", (l, h2, p2)))
                    act.activation(yc_lo[:, pr % 2, :], psum[VD:2 * VD, 7, 0:256], ACT.Copy).then_inc(*inc("yc_lo", (l, hq, pq_)))

        @block.sync
        def _(sp):
            sp.dma_start(X[:, :, :], t_in["x"].rearrange("(k p) n -> p k n", p=P)).then_inc(*inc("x_in", by=16))
            sp.dma_start(ident[:, :], t_in["ident"]).then_inc(*inc("consts", by=16))
            sp.dma_start(trig[:, :, :, :], t_in["trig"]).then_inc(*inc("consts", by=16))
            sp.dma_start(ada_p[:, :, :], t_in["ada_p"]).then_inc(*inc("consts", by=16))
            sp.dma_start(prm[:, :], t_in["prm"][0]).then_inc(*inc("prm", 0, 16))
            sp.dma_start(silu_c[:, 0], t_in["c"]).then_inc(*inc("c_in", by=16))

            def load_ada(j):
                if j >= 2:
                    sp.wait_ge(*at("ada_lo", j - 2))
                sp.dma_start(ada_raw[:, j % 2], t_in["w_ada"][j // ADA_N, j % ADA_N]).then_inc(*inc(f"ada_in{j % 2}", j, 16))

            for j in range(ADA_N):
                load_ada(j)

            def load_chunks(n0, count):
                for n in range(n0, min(n0 + count, n_chunks)):
                    if n >= 2:
                        sp.wait_ge(C.sem("w_lo"), n - 1)
                    l, c = stream[n]
                    sp.dma_start(raw[:, n % 2, :], t_in["w"][l, c]).then_inc(*inc(f"w_in{n % 2}", n, 16))

            def load_chunks_loop(n0, turns):
                l, c0 = stream[n0]
                with sp.Fori(0, turns, 1) as i:
                    for j in range(4):
                        src = t_in["w"][l, bass.ds(i * 4 + (c0 + j), 1)].rearrange("o p n -> (o p) n")
                        sp.wait_ge(C.sem("w_lo"), i * 4 + (n0 + j - 1))
                        sp.dma_start(raw[:, (n0 + j) % 2, :], src).then_inc(C.sem(f"w_in{(n0 + j) % 2}"), 16)
                for j in range(2):
                    C.skip(f"w_in{j}", 32 * turns)

            load_chunks(0, 2)
            for l in range(DEPTH):
                if l:
                    sp.wait_ge(*at("att_free", l - 1))
                    sp.dma_start(prm[:, :], t_in["prm"][l]).then_inc(*inc("prm", l, 16))
                    sp.wait_ge(C.sem("w_used"), start["p1", l, 0])
                else:
                    sp.wait_ge(*at("ada_mm", ADA_N - 1))
                sp.dma_start(qk[:, :, :, :, :].rearrange("p a b c d -> p (a b c d)")[:, 0:2 * NQ + NKV], t_in["wqkv"][l])\
                  .then_inc(*inc("wqkv_in", l, 16))
                for what, *arg in p1_schedule(l):
                    if what in ("norm", "wqkv", "tok"):
                        continue
                    b = arg[0]
                    c0, T = BLOCKS[b]
                    cs = P1_CHUNKS[full(l, b)]
                    if what == "in":
                        lo, hi = arg[1], min(arg[2], len(cs))
                        load_chunks(start["p1", l, b] + 2 + lo, hi - lo)
                        if hi == N_IN:
                            for i in range(2):
                                sp.wait_ge(*at("b_out", (l, b, i)))
                                sp.dma_start(b_scr[l, i, :, c0:c0 + T], yst[:, i, :T]).then_inc(*inc("b_store", (l, b, i), 16))
                    elif what == "mix":
                        for s, nt in sub_tiles(T):
                            sp.wait_ge(*at("mix_out", (l, b, s, 1)))
                            cs0 = c0 + s * P
                            sp.dma_start(y_scr[l, 0:256, cs0:cs0 + nt * P].rearrange("(i p) n -> p i n", p=P),
                                         mixo[:, :, :nt * P]).then_inc(*inc("ya_store", (l, b, s), 16))
                    elif what == "head":
                        s, nt = arg[1], dict(sub_tiles(T))[arg[1]]
                        cs0 = c0 + s * P
                        sp.wait_ge(*at("v_lo", (l, b, s)))
                        for t in range(nt):
                            sp.dma_start(v_scr[l, :, cs0 + t * P:cs0 + t * P + P, :].rearrange("h p d -> p h d"),
                                         v_st[:, t].rearrange("p h two d -> p h (two d)").bitcast(F32))\
                              .then_inc(*inc("v_store", (l, b, s), 16))
                        for w in ((0, 1) if full(l, b) else (1,)):
                            for hd in range(HEADS):
                                sp.wait_ge(*at("qk_lo", (l, b, s, w, hd)))
                                sp.dma_start(qk_scr[l, w, hd, :, :, cs0:cs0 + nt * P], st_qk[:, hd % N_ST, :, :nt * P].bitcast(F32))\
                                  .then_inc(*inc(f"qk_store{hd % N_ST}", (l, b, s, w, hd), 16))
                for g, (c0, L) in enumerate(((0, CTX), (CTX, SEQ))):
                    if g == 0 and not full(l, 0):
                        continue
                    sp.wait_ge(*at("b_store", (l, min(g * 2, 2), 1)))
                    sp.wait_ge(*at("pool_edge", (l, g)))
                    sp.dma_start(pz[:, :, HALO:HALO + L], b_scr[l, :, :, c0:c0 + L].rearrange("i p n -> p i n"))\
                      .then_inc(*inc("pz_in", (l, g), 16))
                    sp.dma_start(pinv[:, :, :L], t_in["inv_lat" if g else "inv_ctx"]).then_inc(*inc("pinv_in", (l, g), 16))
                    for i in range(2):
                        for q in range(0, L, NMAX):
                            w = min(NMAX, L - q)
                            sp.wait_ge(*at("pool_out", (l, g, i, q)))
                            sp.dma_start(y_scr[l, 256 + i * P:256 + i * P + P, c0 + q:c0 + q + w], pd[:, i, q:q + w])\
                              .then_inc(*inc("yb_store", (l, g, i, q), 16))
                for j in range(N_ST):
                    sp.wait_ge(*at(f"qk_store{j}", (l, 2, 2, 1, HEADS - N_ST + j)))
                sp.wait_ge(*at("v_store", (l, 2, 2)))
                sp.wait_ge(*at("yb_store", (l, 1, 1, SEQ - NMAX)))
                sp.wait_ge(*at("ya_store", (l, 2, 2)))
                q0 = 0 if l < DEPTH - 1 else CTX
                npair = len(steps(l)) // 2

                def head_loads(hd, j):
                    one = bass.ds(hd, 1)
                    sp.dma_start(kh[:, j].bitcast(F32), qk_scr[l, 1, one].rearrange("o d s n -> (o d) s n")).then_inc(C.sem(f"kqv{j}"), 16)
                    sp.dma_start(qh[:, j, :, q0:].bitcast(F32), qk_scr[l, 0, one, :, :, q0:].rearrange("o d s n -> (o d) s n")).then_inc(C.sem(f"kqv{j}"), 16)
                    sp.dma_start(vh[:, j].bitcast(F32), v_scr[l, one].rearrange("o (t p) d -> p (o t) d", p=P)).then_inc(C.sem(f"kqv{j}"), 16)
                    C.skip(f"kqv{j}", 48)

                def yc_store(hd, j, pr):
                    col = steps(l)[2 * pr][0]
                    sp.dma_start(y_scr[l, 2 * 256 + hd * VD:2 * 256 + hd * VD + VD, col:col + 256] if isinstance(hd, int) else
                                 y_scr[l].rearrange("(h d) n -> h d n", d=VD)[bass.ds(hd + HEADS, 1), :, col:col + 256]
                                 .rearrange("o d n -> (o d) n"), yc[:, (j * npair + pr) % 2])\
                      .then_inc(C.sem(f"yc_store{(j * npair + pr) % 2}"), 16)
                    C.skip(f"yc_store{(j * npair + pr) % 2}", 16)

                C.now("kqv0", ("att", l)); C.now("kqv1", ("att", l))
                C.now("yc_store0", ("att", l)); C.now("yc_store1", ("att", l))
                head_loads(0, 0)
                head_loads(1, 1)
                for hd in range(HEADS):
                    for pr in range(npair):
                        sp.wait_ge(*at("yc", (l, hd, pr)))
                        yc_store(hd, hd % 2, pr)
                    if hd + 2 < HEADS:
                        sp.wait_ge(*at("pv_mm", (l, hd, npair - 1)))
                        head_loads(hd + 2, hd % 2)
                for b in layer_blocks(l):
                    c0, T = BLOCKS[b]
                    n0 = start["out", l, b]
                    if b == layer_blocks(l)[0]:
                        for j in range(2):
                            sp.wait_ge(C.sem(f"yc_store{j}"), C.total[f"yc_store{j}"])
                    else:
                        sp.wait_ge(*at("y_lo", (l, b - 1, KT - 1)))
                    sp.dma_start(yraw[:, :, :T], y_scr[l, :, c0:c0 + T].rearrange("(k p) n -> p k n", p=P))\
                      .then_inc(*inc("y_in", (l, b), 16))
                    for m in range(KT):
                        load_chunks(n0 + 2 + m, 1)
                        if l == 0:
                            load_ada(ADA_N + layer_blocks(l).index(b) * KT + m)
                for b in layer_blocks(l):
                    n0 = start["ffn", l, b]
                    n_ffn = 2 * FT + 3 * KT
                    load_chunks_loop(n0 + 2, n_ffn // 4 - 1)
                    load_chunks(n0 + 2 + n_ffn - 4, 4)
                    if l == DEPTH - 1:
                        c0, T = BLOCKS[b]
                        sp.wait_ge(*at("dn_acc_end", (l, b)))
                        sp.dma_start(t_in["out"][:, c0 - CTX:c0 - CTX + T].rearrange("(k p) n -> p k n", p=P),
                                     X[:, :, c0:c0 + T]).then_inc(*inc("out", by=16))
            sp.wait_ge(*at("out"))

        def norm_entry(dve, l, which, b):
            pass

        def h_free(l, which, b, under):
            if under is not None:
                return start[("ffn",) + under] + 2 * FT
            if which == 0:
                return start["p1", l, b]
            return start["ffn", l, b]

        def split_hi(act, n):
            if isinstance(n, int) and n >= n_chunks:
                return
            slot = n % 2
            act.wait_ge(C.sem(f"w_in{slot}"), 16 * (n // 2 + 1))
            if n >= 2:
                act.wait_ge(C.sem("w_used"), n - 1)
            act.activation(w_hi[:, slot, :], raw[:, slot, :], ACT.Copy).then_inc(*inc("w_hi", n))

        def split_lo(dve, n):
            if n >= n_chunks:
                return
            slot = n % 2
            dve.wait_ge(C.sem("w_hi"), n + 1)
            dve.tensor_tensor(w_lo[:, slot, :], raw[:, slot, :], w_hi[:, slot, :].bitcast(F32), ALU.subtract)\
               .then_inc(*inc("w_lo", n))

        def split_hi_loop(act, n0, i, per, j, last):
            n = n0 + j
            act.wait_ge(C.sem(f"w_in{n % 2}"), i * (8 * per) + 16 * (n // 2 + 1))
            act.wait_ge(C.sem("w_used"), i * per + (n - 1))
            act.activation(w_hi[:, n % 2, :], raw[:, n % 2, :], ACT.Copy).then_inc(C.sem("w_hi"), 1)

        def split_lo_loop(dve, n0, i, per, j):
            n = n0 + j
            dve.wait_ge(C.sem("w_hi"), i * per + (n + 1))
            dve.tensor_tensor(w_lo[:, n % 2, :], raw[:, n % 2, :], w_hi[:, n % 2, :].bitcast(F32), ALU.subtract)\
               .then_inc(C.sem("w_lo"), 1)

        qk_flat = qk[:, :, :, :, :].rearrange("p a b c d -> p (a b c d)")[:, 0:2 * NQ + NKV]

        @block.scalar
        def _(act):
            def norm_piece(l, which, b, piece, under=None):
                c0, T = BLOCKS[b]
                key = (l, which, b)
                s = 1 if b == 0 else 0
                tmp = fnrm_t if which else nrm_t
                if piece in ("sq0", "sq1"):
                    h = int(piece[2])
                    if h:
                        act.wait_ge(*at("norm_sum", (key, 0)))
                    else:
                        if which == 1:
                            act.wait_ge(*at("out_end", (l, b)))
                        elif l:
                            act.wait_ge(*at("dn_acc_end", (l - 1, b)))
                        else:
                            act.wait_ge(*at("x_in"))
                        if key == (0, 0, 0):
                            act.wait_ge(*at("mod", 0))
                        if under is not None:
                            act.wait_ge(*at("gu_lo", ("ffn",) + under, plus=FT))
                        elif which == 0 and b > 0:
                            act.wait_ge(*at("pq_lo", ((l, b - 1), 2)))
                        elif which == 1:
                            act.wait_ge(*at("y_lo", (l, layer_blocks(l)[-1], KT - 1)))
                    act.activation(tmp[:, :, :T], X[:, 4 * h:4 * h + 4, c0:c0 + T], ACT.Square).then_inc(*inc("norm_sq", (key, h)))
                else:
                    k = int(piece)
                    if k == 0:
                        act.wait_ge(C.sem("w_used"), h_free(l, which, b, under)) if h_free(l, which, b, under) else None
                    act.wait_ge(*at("norm_t", (key, k)))
                    if k >= 2:
                        act.wait_ge(*at("h_lo", (key, k - 2)))
                    act.activation(t32[:, k % 2, :T], tmp[:, k % 4, :T], ACT.Identity,
                                   bias=mod[:, l, 24 * which + k, s:s + 1]).then_inc(*inc("h32", (key, k)))
                    act.activation(h_hi[:, k, :T], tmp[:, k % 4, :T], ACT.Identity,
                                   bias=mod[:, l, 24 * which + k, s:s + 1]).then_inc(*inc("h_hi", (key, k)))

            def norm(l, which, b):
                for piece in ["sq0", "sq1"] + list(range(KT)):
                    norm_piece(l, which, b, str(piece))

            def ada_split(j):
                act.wait_ge(*at(f"ada_in{j % 2}", j))
                if j >= 2:
                    act.wait_ge(*at("ada_mm", j - 2))
                act.activation(ada_hi[:, j % 2], ada_raw[:, j % 2], ACT.Copy).then_inc(*inc("ada_hi", j))

            def ada_evac(m):
                act.wait_ge(*at("ada_mm", 2 * m + 1))
                if m >= 2:
                    act.wait_ge(*at("ada_tr", m - 2))
                act.activation(ada_row[:, m % 2, :], psum[0:4, 4 + m % 2, :], ACT.Copy).then_inc(*inc("ada_row", m))

            def in_chunk(l, b, i):
                c0, T = BLOCKS[b]
                c = P1_CHUNKS[full(l, b)][i]
                kb, n = (l, b), start["p1", l, b] + i
                split_hi(act, n + 2)
                src = psum[:, i % 2, :T]
                act.wait_ge(C.sem("w_used"), n + 1)
                if c in (0, 1):
                    if (l, b) > (0, 0):
                        act.wait_ge(*at("mix_done", at_prev(l, b)))
                    act.activation(u_sb[:, c, :T], src, ACT.Gelu).then_inc(*inc("in_free", (kb, i)))
                elif c in (2, 3):
                    act.activation(v_sb[:, c - 2, :T], src, ACT.Gelu).then_inc(*inc("in_free", (kb, i)))
                elif c in (4, 5):
                    if (l, b) > (0, 0):
                        act.wait_ge(*at("b_store", at_prev(l, b) + (1,)))
                    act.activation(yst[:, c - 4, :T], src, ACT.Copy).then_inc(*inc("in_free", (kb, i)))
                    C.alias("b_out", (l, b, c - 4), "in_free")
                elif c in (6, 7, 8):
                    j = c - 6
                    g = pcol("qa", j, j + 1) if j < 2 else pcol("kva")
                    if c == 6 or not full(l, b):
                        act.wait_ge(*at("h_lo", ((l, 0, b), KT - 1)))
                    act.activation(pq32[:, j, :T], src, ACT.Copy, scale=g).then_inc(*inc("pq32", (kb, j)))
                    act.activation(pq_hi[:, j, :T], src, ACT.Copy, scale=g).then_inc(*inc("pq_hi", (kb, j)))
                    act.activation(pq_sq[:, j, :T], src, ACT.Square).then_inc(*inc("in_free", (kb, i)))
                    C.alias("pq_sq", (kb, j), "in_free")
                elif c == 9:
                    act.activation(kr_sb[:, :T], src, ACT.Copy).then_inc(*inc("in_free", (kb, i)))
                    C.alias("kr_sb", kb, "in_free")

            def mix(l, b):
                T = BLOCKS[b][1]
                for s, nt in sub_tiles(T):
                    for t in range(nt):
                        act.wait_ge(*at("mix_tr", (l, b, s)))
                        act.activation(vtok[:, s + t, :], psum[:, 2 + s // 2, t * 256:(t + 1) * 256], ACT.Square,
                                       accum_out=stat[:, 64 + s + t:65 + s + t]).then_inc(*inc("vt_sq", (l, b, s)))

            def tok(l, b, s):
                T = BLOCKS[b][1]
                nt = dict(sub_tiles(T))[s]
                act.wait_ge(*at("tok_r", (l, b)))
                for t in range(nt):
                    for kind, c in tok_products(l, b, s, t):
                        key = (l, b, s + t, kind, c)
                        bank = tok_bank(*key)
                        act.wait_ge(*at("tok_mm2", key))
                        if c == 0 and t == 0:
                            prev_sub_wait(act, l, b, s, 0 if kind == "q" else 1)
                        if kind == "q":
                            act.activation(qk[:, 0, t, 4 * c:4 * c + 4].rearrange("p h d -> p (h d)"), psum[:, bank, 0:384],
                                           ACT.Copy, scale=stat[:, 16 + s + t:17 + s + t]).then_inc(*inc("tok_act", key))
                        else:
                            src = psum[:, bank, :].rearrange("p (h d) -> p h d", d=P)
                            rs = stat[:, 20 + s + t:21 + s + t]
                            act.activation(qk[:, 1, t, 4 * c:4 * c + 4, 0:NOPE], src[:, :, 0:NOPE], ACT.Copy, scale=rs)\
                               .then_inc(*inc("tok_act", key))
                            act.activation(v_st[:, t, 4 * c:4 * c + 4, 0, :], src[:, :, NOPE:P], ACT.Copy, scale=rs)\
                               .then_inc(*inc("tok_act", key))
                act.wait_ge(*at("kr_tr", (l, b, s)))
                act.activation(krt[:, :nt, :], psum[:, 3, 0:nt * P].rearrange("p (t d) -> p t d", d=P)[:, :, P - ROPE:P],
                               ACT.Copy).then_inc(*inc("krt", (l, b, s)))

            def head(l, b, s):
                nt = dict(sub_tiles(BLOCKS[b][1]))[s]
                ws = (0, 1) if full(l, b) else (1,)
                done = [y[1] for y in p1_schedule(l)[:p1_pos(l, ("head", b, s))] if y[0] == "in" and y[3] == N_IN]
                act.wait_ge(*at("tok_mm", (l, done[-1])))
                for w in ws:
                    if w == 1:
                        act.wait_ge(*at("kr_b", (l, b, s)))
                    else:
                        act.wait_ge(*at("tok_act", (l, b, s + nt - 1, "q", 1)))
                    if w == 1 and len(ws) == 2:
                        act.wait_ge(*at("hd_sum", (l, b, s, 0)))
                    act.activation(qk_sq[:, :nt].rearrange("p t h d -> p (t h d)"),
                                   qk[:, w, :nt].rearrange("p t h d -> p (t h d)"), ACT.Square).then_inc(*inc("hd_sq", (l, b, s, w)))
                for w in ws:
                    g = pcol("gnope" if b else "gfull", w, w + 1)[:QKD]
                    for hd in range(HEADS):
                        key = (l, b, s, w, hd)
                        act.wait_ge(*at("qk_tr", key))
                        prev_head_wait(act, l, b, s, w, hd)
                        act.activation(st_qk[:, hd % N_ST, 0, :nt * P], psum[:QKD, 2 + hd % 2, 0:nt * P], ACT.Copy, scale=g)\
                           .then_inc(*inc("qk_hi", key))

            C.skip("sg", 2)
            act.wait_ge(*at("c_in"))
            act.activation(silu_c[:, 1], silu_c[:, 0], ACT.Silu).then_inc(*inc("silu_c"))
            act.wait_ge(*at("silu_c"))
            act.activation(silu_s[:, :, 0:2], silu_c[:, 1], ACT.Copy).then_inc(*inc("silu_hi"))
            for j in range(ADA_N):
                ada_split(j)
                if j % 2 and j > 2:
                    ada_evac(j // 2 - 1)
            ada_evac(ADA_M - 1)
            for l in range(DEPTH):
                if l == 0:
                    act.wait_ge(*at("prm", 0))
                    split_hi(act, 0)
                    split_hi(act, 1)
                for what, *arg in p1_schedule(l):
                    if what == "norm":
                        norm(l, 0, arg[0])
                    elif what == "wqkv":
                        act.wait_ge(*at("wqkv_in", l))
                        act.activation(wqkv_hi[:, :], qk_flat, ACT.Copy).then_inc(*inc("wqkv_hi", l))
                    elif what == "in":
                        for i in range(arg[1], min(arg[2], len(P1_CHUNKS[full(l, arg[0])]))):
                            in_chunk(l, arg[0], i)
                    else:
                        {"mix": mix, "tok": tok, "head": head}[what](l, *arg)
                for g, (c0, L) in enumerate(((0, CTX), (CTX, SEQ))):
                    if g == 0 and not full(l, 0):
                        continue
                    for i in range(2):
                        for q in range(0, L, NMAX):
                            w = min(NMAX, L - q)
                            act.wait_ge(*at("pool_mm", (l, g, i, q)))
                            act.activation(pd[:, i, q:q + w], psum[:, (i * 2 + q // NMAX) % 2, :w], ACT.Copy,
                                           scale=pcol("pscale", i, i + 1)).then_inc(*inc("pool_out", (l, g, i, q)))
                att_act(act, l)
                for b in layer_blocks(l):
                    c0, T = BLOCKS[b]
                    n0 = start["out", l, b]
                    act.wait_ge(*at("y_in", (l, b)))
                    act.wait_ge(C.sem("w_used"), n0)
                    for k in range(KT):
                        act.activation(h_hi[:, k, :T], yraw[:, k, :T], ACT.Copy).then_inc(*inc("y_hi", (l, b, k)))
                    for m in range(KT):
                        split_hi(act, n0 + m + 2)
                        if l == 0:
                            j = layer_blocks(l).index(b) * KT + m
                            ada_split(ADA_N + j)
                            if j % 2 and j > 2:
                                ada_evac(ADA_M + j // 2 - 1)
                if l == 0:
                    ada_evac(2 * ADA_M - 1)
                for b in layer_blocks(l):
                    c0, T = BLOCKS[b]
                    n0 = start["ffn", l, b]
                    if b == layer_blocks(l)[0]:
                        norm(l, 1, b)
                    base_sg, base_g = C.total.get("sg", 0), C.total.get("gu_hi", 0)
                    C.now("sg", ("ffn", l, b)); C.now("gu_hi", ("ffn", l, b))
                    g32b = at("gu32", ("ffn", l, b))[1]
                    glob = at("gu_lo", ("ffn", l, b))[1]
                    with act.Fori(0, FT // 2, 1) as i:
                        for j in range(2):
                            split_hi_loop(act, n0 + 2, i, 4, 2 * j, 0)
                            act.wait_ge(C.sem("w_used"), i * 4 + (n0 + 2 * j + 1))
                            act.wait_ge(C.sem("gu32"), i * 2 + (g32b + j - 1))
                            act.activation(sg[:, j, :T], psum[:, 2 * j, :T], ACT.Silu).then_inc(C.sem("sg"), 1)
                            split_hi_loop(act, n0 + 2, i, 4, 2 * j + 1, 0)
                            act.wait_ge(C.sem("gu32"), i * 2 + (g32b + j + 1))
                            act.activation(gu_hi[:, bass.ds(i * 2 + j, 1), :T].rearrange("p o n -> p (o n)"),
                                           gu32[:, j, :T], ACT.Copy).then_inc(C.sem("gu_hi"), 1)
                    C.skip("sg", FT); C.skip("gu_hi", FT); C.skip("w_hi", 2 * FT)
                    n1 = n0 + 2 * FT
                    nxt = norm_next(l, b)
                    for j in range(3 * KT):
                        split_hi(act, n1 + j + 2)
                        if nxt and j in (0, 2):
                            norm_piece(*nxt, "sq0" if j == 0 else "sq1", (l, b))
                        if nxt and 9 <= j < 9 + KT:
                            norm_piece(*nxt, str(j - 9), (l, b))

        @block.vector
        def _(dve):
            dve.memset(ones[:, :], 1.0).then_inc(*inc("ones"))
            dve.memset(half[:, :], -0.5).then_inc(*inc("ones"))
            dve.memset(flag[:, 0:1], 0.0).then_inc(C.sem("gu_lo"), 2)
            C.skip("gu_lo", 2)
            dve.memset(flag[:, 1:2], 0.0).then_inc(C.sem("gu32"), 2)
            C.skip("gu32", 2)
            dve.memset(flag[:, 2:3], 0.0).then_inc(C.sem("sg"), 2)
            def ada_split(j):
                dve.wait_ge(*at("ada_hi", j))
                dve.tensor_tensor(ada_lo[:, j % 2], ada_raw[:, j % 2], ada_hi[:, j % 2].bitcast(F32), ALU.subtract)\
                   .then_inc(*inc("ada_lo", j))

            def ada_end(l):
                dve.wait_ge(*at("ada_tr", (l + 1) * ADA_M - 1))
                dve.wait_ge(*at("consts"))
                v = psum[:, 6, 0:192].rearrange("p (m s) -> p m s", s=4)
                dve.tensor_tensor(mod[:, l], v[:, :, 0:2], ada_p[:, l, 16:64].unsqueeze(2).to_broadcast([P, 48, 2]), ALU.add)\
                   .then_inc(*inc("mod_hi", l))
                dve.wait_ge(*at("mod_hi", l))
                dve.tensor_tensor(mod[:, l], mod[:, l], v[:, :, 2:4], ALU.add).then_inc(*inc("mod", (l, 0)))
                dve.wait_ge(*at("mod", (l, 0)))
                for which in range(2):
                    ng = ada_p[:, l, 8 * which:8 * which + 8]
                    dve.scalar_tensor_tensor(gain[:, l, which], mod[:, l, 24 * which + 8:24 * which + 16, :], 1.0,
                                             ng.unsqueeze(2).to_broadcast([P, KT, 2]), ALU.add, ALU.mult).then_inc(*inc("mod", l))

            def h_lo_piece(key, T, k):
                dve.wait_ge(*at("h_hi", (key, k)))
                dve.tensor_tensor(h_lo[:, k, :T], t32[:, k % 2, :T], h_hi[:, k, :T].bitcast(F32), ALU.subtract)\
                   .then_inc(*inc("h_lo", (key, k)))

            def norm_piece(l, which, b, piece):
                c0, T = BLOCKS[b]
                key = (l, which, b)
                s, nt = (1 if b == 0 else 0), T // P
                tmp = fnrm_t if which else nrm_t
                if piece in ("sum0", "sum1"):
                    h = int(piece[3])
                    dve.wait_ge(*at("norm_sq", (key, h)))
                    dve.tensor_reduce(t32[:, h, :T], tmp[:, :, :T].rearrange("p k n -> p n k"), AX.X, ALU.add)\
                       .then_inc(*inc("norm_sum", (key, h)))
                elif piece == "var":
                    dve.wait_ge(*at("norm_mm", key))
                    dve.tensor_scalar(nst[:, 0:nt], psum[:, 7, 0:nt], 1.0 / DM, EPS, ALU.mult, ALU.add).then_inc(*inc("norm_var", key))
                elif piece == "diag":
                    dve.wait_ge(*at("norm_r", key))
                    dve.tensor_tensor(diag[:, :T].rearrange("p (t j) -> p t j", j=P), ident[:, :].unsqueeze(1).to_broadcast([P, nt, P]),
                                      nst[:, 4:4 + nt].unsqueeze(2).to_broadcast([P, nt, P]), ALU.mult).then_inc(*inc("norm_diag", key))
                else:
                    k = int(piece)
                    if k == 0:
                        dve.wait_ge(*at("norm_bc", key))
                    if k >= 4:
                        dve.wait_ge(*at("h_hi", (key, k - 4)))
                    if k < KT:
                        dve.scalar_tensor_tensor(tmp[:, k % 4, :T], X[:, k, c0:c0 + T], gain[:, l, which, k, s:s + 1],
                                                 psum[:, 7, :T], ALU.mult, ALU.mult).then_inc(*inc("norm_t", (key, k)))
                    if k >= 1:
                        h_lo_piece(key, T, k - 1)

            def norm(l, which, b):
                for piece in ["sum0", "sum1", "var", "diag"] + list(range(KT + 1)):
                    norm_piece(l, which, b, str(piece))

            def in_chunk(l, b, i):
                c0, T = BLOCKS[b]
                cs = P1_CHUNKS[full(l, b)]
                c, kb, nt_all = cs[i], (l, b), T // P
                split_lo(dve, start["p1", l, b] + i + 2)
                if c in (6, 7, 8):
                    j = c - 6
                    dve.wait_ge(*at("pq_hi", (kb, j)))
                    dve.tensor_tensor(pq_lo[:, j, :T], pq32[:, j, :T], pq_hi[:, j, :T].bitcast(F32), ALU.subtract)\
                       .then_inc(*inc("pq_lo", (kb, j)))
                if c == 9:
                    dve.wait_ge(*at("tok_mm", kb))
                    if full(l, b):
                        dve.tensor_scalar(stat[:, 0:nt_all], psum[:, 3, 0:nt_all], 1.0 / 256, EPS, ALU.mult, ALU.add)\
                           .then_inc(*inc("tok_var", kb))
                    dve.tensor_scalar(stat[:, 4:4 + nt_all], psum[:, 3, 4:4 + nt_all], 1.0 / 128, EPS, ALU.mult, ALU.add)\
                       .then_inc(*inc("tok_var", kb))

            def mix(l, b):
                T = BLOCKS[b][1]
                for s, nt in sub_tiles(T):
                    key = (l, b, s)
                    dve.wait_ge(*at("vt_sq", key))
                    dve.tensor_scalar(stat[:, 68 + s:68 + s + nt], stat[:, 64 + s:64 + s + nt], 1.0 / 256, EPS, ALU.mult, ALU.add)\
                       .then_inc(*inc("vt_var", key))
                    dve.wait_ge(*at("vt_r", key))
                    dve.tensor_tensor(vtok[:, s:s + nt, :], psum[:, 2 + s // 2, 0:nt * 256].rearrange("p (t n) -> p t n", n=256),
                                      stat[:, 72 + s:72 + s + nt].unsqueeze(2).to_broadcast([P, nt, 256]), ALU.mult)\
                       .then_inc(*inc("vt_n", key))
                for s, nt in sub_tiles(T):
                    if s or (l, b) > (0, 0):
                        prev = (l, b, s - 2) if s else at_prev(l, b) + (sub_tiles(BLOCKS[at_prev(l, b)[1]][1])[-1][0],)
                        dve.wait_ge(*at("ya_store", prev))
                    dve.wait_ge(*at("mix_mm", (l, b, s)))
                    for pr in range(2):
                        bsp = pcol("bsp", pr * P, pr * P + P).unsqueeze(1).to_broadcast([P, nt, P])
                        dve.scalar_tensor_tensor(mixo[:, pr, :nt * P].rearrange("p (t n) -> p t n", n=P),
                                                 psum[:, 4 + pr, 0:nt * P].rearrange("p (t n) -> p t n", n=P),
                                                 pcol("sgu", pr, pr + 1), bsp, ALU.mult, ALU.add).then_inc(*inc("mix_g", (l, b, s, pr)))
                    for pr in range(2):
                        dve.wait_ge(*at("mix_g", (l, b, s, pr)))
                        dve.tensor_tensor(mixo[:, pr, :nt * P], mixo[:, pr, :nt * P], u_sb[:, pr, s * P:(s + nt) * P],
                                          ALU.mult).then_inc(*inc("mix_out", (l, b, s, pr)))
                C.alias("mix_done", (l, b), "mix_out")

            def tok(l, b, s):
                nt = dict(sub_tiles(BLOCKS[b][1]))[s]
                for t in range(nt):
                    for c in range(2):
                        key = (l, b, s + t, "kv", c)
                        dve.wait_ge(*at("tok_act", key))
                        src = psum[:, tok_bank(*key), :].rearrange("p (h d) -> p h d", d=P)
                        dve.scalar_tensor_tensor(v_st[:, t, 4 * c:4 * c + 4, 1, :], src[:, :, NOPE:P], stat[:, 20 + s + t:21 + s + t],
                                                 v_st[:, t, 4 * c:4 * c + 4, 0, :].bitcast(F32), ALU.mult, ALU.subtract)\
                           .then_inc(*inc("v_lo", (l, b, s)))
                        C.alias("v_lo_t", key, "v_lo")

            def head(l, b, s):
                nt = dict(sub_tiles(BLOCKS[b][1]))[s]
                ws = (0, 1) if full(l, b) else (1,)
                n = HEADS * nt
                for w in ws:
                    k2 = (l, b, s, w)
                    dve.wait_ge(*at("hd_sq", k2))
                    dve.tensor_reduce(stat[:, 80 + 48 * w:80 + 48 * w + n], qk_sq[:, :nt].rearrange("p t h d -> p (t h) d"), AX.X, ALU.add)\
                       .then_inc(*inc("hd_sum", k2))
                    dve.wait_ge(*at("hd_sum", k2))
                    dve.tensor_scalar(stat[:, 96 + 48 * w:96 + 48 * w + n], stat[:, 80 + 48 * w:80 + 48 * w + n], 1.0 / QKD, EPS,
                                      ALU.mult, ALU.add).then_inc(*inc("hd_var", k2))
                for w in ws:
                    k2 = (l, b, s, w)
                    a = qk[:, w, :nt].rearrange("p t h d -> p (t h) d")
                    dve.wait_ge(*at("hd_r", k2))
                    dve.tensor_tensor(a, a, stat[:, 112 + 48 * w:112 + 48 * w + n].unsqueeze(2).to_broadcast([P, n, QKD]), ALU.mult)\
                       .then_inc(*inc("hd_n", k2))
                for w in ws:
                    g = pcol("gnope" if b else "gfull", w, w + 1)[:QKD]
                    for hd in range(HEADS):
                        key = (l, b, s, w, hd)
                        dve.wait_ge(*at("qk_hi", key))
                        dve.scalar_tensor_tensor(st_qk[:, hd % N_ST, 1, :nt * P], psum[:QKD, 2 + hd % 2, 0:nt * P], g,
                                                 st_qk[:, hd % N_ST, 0, :nt * P].bitcast(F32), ALU.mult, ALU.subtract)\
                           .then_inc(*inc("qk_lo", key))

            dve.wait_ge(*at("silu_hi"))
            dve.tensor_tensor(silu_s[:, :, 2:4], silu_c[:, 1], silu_s[:, :, 0:2].bitcast(F32), ALU.subtract).then_inc(*inc("silu_s"))
            for j in range(ADA_N):
                ada_split(j)
            ada_end(0)
            for l in range(DEPTH):
                if l == 0:
                    split_lo(dve, 0)
                    split_lo(dve, 1)
                for what, *arg in p1_schedule(l):
                    if what == "norm":
                        norm(l, 0, arg[0])
                    elif what == "wqkv":
                        dve.wait_ge(*at("wqkv_hi", l))
                        dve.tensor_tensor(wqkv_lo[:, :], qk_flat, wqkv_hi[:, :].bitcast(F32), ALU.subtract).then_inc(*inc("wqkv_lo", l))
                    elif what == "in":
                        for i in range(arg[1], min(arg[2], len(P1_CHUNKS[full(l, arg[0])]))):
                            in_chunk(l, arg[0], i)
                    else:
                        {"mix": mix, "tok": tok, "head": head}[what](l, *arg)
                st, groups = att_plan(l)
                G, npair = len(st), len(steps(l)) // 2
                for g in range(G + 4):
                    if 0 <= g - 1 < G:
                        dve.wait_ge(*at("exp", (l, g - 1)))
                        if g >= 5:
                            dve.wait_ge(*at("pn", (l, g - 5)))
                        sl = (g - 1) % 4
                        dve.reciprocal(den[:, 1, sl:sl + 1], den[:, 0, sl:sl + 1]).then_inc(*inc("rden", (l, g - 1)))
                    if 0 <= g - 2 < G:
                        q = g - 2
                        for tg, k0, n in groups[q]:
                            dve.wait_ge(*at("t_hi", (l, tg)))
                            sl = (slice(None), (q // 2) % 2, slice(k0, k0 + n), slice((q % 2) * P, (q % 2) * P + P))
                            dve.tensor_tensor(pt_lo[sl], psum[:, 5 + tg % 2, 0:n * P].rearrange("p (k n) -> p k n", n=P),
                                              pt_hi[sl].bitcast(F32), ALU.subtract).then_inc(*inc("t_lo", (l, tg)))
                    if g < G:
                        hd, i, col, nk = st[g]
                        dve.wait_ge(*at("s_mm", (l, g)))
                        if g >= 4:
                            dve.wait_ge(*at("exp", (l, g - 4)))
                        else:
                            dve.wait_ge(*at("att_free", l))
                        sc = scores(g, nk)
                        dve.reduce_max(amax[:, 0, g % 4:g % 4 + 1], sc, AX.X).then_inc(*inc("smax", (l, g)))
                        dve.wait_ge(*at("smax", (l, g)))
                        dve.tensor_scalar(amax[:, 1, g % 4:g % 4 + 1], amax[:, 0, g % 4:g % 4 + 1], -SCALE, None, ALU.mult)\
                           .then_inc(*inc("amax", (l, g)))
                    if g >= 4 and g % 2 == 0 and (g - 4) // 2 < G // 2:
                        pr = (g - 4) // 2
                        hq, pq_ = divmod(pr, npair)
                        dve.wait_ge(*at("yc_lo", (l, hq, pq_)))
                        if pr >= 2:
                            dve.wait_ge(*at(f"yc_store{pr % 2}", ("att", l), plus=16 * (pr // 2)))
                        dve.tensor_tensor(yc[:, pr % 2, :], psum[0:VD, 7, 0:256], yc_lo[:, pr % 2, :], ALU.add)\
                           .then_inc(*inc("yc", (l, hq, pq_)))
                for b in layer_blocks(l):
                    c0, T = BLOCKS[b]
                    s = 1 if b == 0 else 0
                    n0 = start["out", l, b]
                    for k in range(KT):
                        dve.wait_ge(*at("y_hi", (l, b, k)))
                        dve.tensor_tensor(h_lo[:, k, :T], yraw[:, k, :T], h_hi[:, k, :T].bitcast(F32), ALU.subtract)\
                           .then_inc(*inc("y_lo", (l, b, k)))
                    for m in range(KT):
                        split_lo(dve, n0 + m + 2)
                        dve.wait_ge(C.sem("w_used"), n0 + m + 1)
                        dve.scalar_tensor_tensor(X[:, m, c0:c0 + T], psum[:, m % 4, :T], mod[:, l, 16 + m, s:s + 1],
                                                 X[:, m, c0:c0 + T], ALU.mult, ALU.add).then_inc(*inc("out_acc", (l, b, m)))
                        if l == 0:
                            ada_split(ADA_N + layer_blocks(l).index(b) * KT + m)
                    C.alias("out_end", (l, b), "out_acc")
                if l == 0:
                    ada_end(1)
                for b in layer_blocks(l):
                    c0, T = BLOCKS[b]
                    s = 1 if b == 0 else 0
                    n0 = start["ffn", l, b]
                    if b == layer_blocks(l)[0]:
                        norm(l, 1, b)
                    C.now("gu32", ("ffn", l, b)); C.now("gu_lo", ("ffn", l, b))
                    g32b, glob = C.total["gu32"], C.total["gu_lo"]
                    sgb, ghib = at("sg", ("ffn", l, b))[1], at("gu_hi", ("ffn", l, b))[1]
                    with dve.Fori(0, FT // 2, 1) as i:
                        for j in range(2):
                            split_lo_loop(dve, n0 + 2, i, 4, 2 * j)
                            split_lo_loop(dve, n0 + 2, i, 4, 2 * j + 1)
                            dve.wait_ge(C.sem("w_used"), i * 4 + (n0 + 2 * j + 2))
                            dve.wait_ge(C.sem("sg"), i * 2 + (sgb + j + 1))
                            dve.wait_ge(C.sem("gu_lo"), i * 2 + (glob + j - 1))
                            dve.tensor_tensor(gu32[:, j, :T], sg[:, j, :T], psum[:, 2 * j + 1, :T], ALU.mult).then_inc(C.sem("gu32"), 1)
                            dve.wait_ge(C.sem("gu_hi"), i * 2 + (ghib + j + 1))
                            f1 = bass.ds(i * 2 + j, 1)
                            dve.tensor_tensor(gu_lo[:, f1, :T].rearrange("p o n -> p (o n)"), gu32[:, j, :T],
                                              gu_hi[:, f1, :T].rearrange("p o n -> p (o n)").bitcast(F32), ALU.subtract)\
                               .then_inc(C.sem("gu_lo"), 1)
                    C.skip("gu32", FT); C.skip("gu_lo", FT); C.skip("w_lo", 2 * FT)
                    n1 = n0 + 2 * FT
                    C.now("dn_acc", ("ffn", l, b))
                    nxt = norm_next(l, b)
                    pieces = {1: "sum0", 3: "sum1", 5: "var", 7: "diag"} | {9 + k: str(k) for k in range(KT + 1)}
                    for j in range(3 * KT):
                        split_lo(dve, n1 + j + 2)
                        m = j // 3
                        if j % 3 == 2:
                            dve.wait_ge(C.sem("w_used"), n1 + 3 * m + 3)
                            dve.scalar_tensor_tensor(X[:, m, c0:c0 + T], psum[:, m % 4, :T], mod[:, l, 40 + m, s:s + 1],
                                                     X[:, m, c0:c0 + T], ALU.mult, ALU.add).then_inc(*inc("dn_acc", (l, b, m)))
                        if nxt and j in pieces:
                            norm_piece(*nxt, pieces[j])
                    C.alias("dn_acc_end", (l, b), "dn_acc")

        @block.gpsimd
        def _(pool):
            def norm(l, which, b):
                nt, key = BLOCKS[b][1] // P, (l, which, b)
                pool.wait_ge(*at("norm_var", key))
                pool.tensor_tensor(nst[:, 4:4 + nt], nst[:, 0:nt], half[:, 0:1].to_broadcast([P, nt]), ALU.pow).then_inc(*inc("norm_r", key))

            def small_pow(dst, src, n, name, key):
                pool.tensor_tensor(stat[:, dst:dst + n], stat[:, src:src + n], half[:, 0:1].to_broadcast([P, n]), ALU.pow).then_inc(*inc(name, key))

            def tok(l, b, s):
                T = BLOCKS[b][1]
                nt = dict(sub_tiles(T))[s]
                if s == 0:
                    pool.wait_ge(*at("tok_var", (l, b)))
                    if full(l, b):
                        small_pow(16, 0, T // P, "tok_r", (l, b))
                    small_pow(20, 4, T // P, "tok_r", (l, b))
                pool.wait_ge(*at("krt", (l, b, s)))
                prev_sub_wait(pool, l, b, s, 1)
                for t in range(nt):
                    pool.tensor_copy(qk[:, 1, t, :, NOPE:], krt[:, t, :].unsqueeze(1).to_broadcast([P, HEADS, ROPE]))\
                        .then_inc(*inc("kr_b", (l, b, s)))

            def mix(l, b):
                for s, nt in sub_tiles(BLOCKS[b][1]):
                    pool.wait_ge(*at("vt_var", (l, b, s)))
                    small_pow(72 + s, 68 + s, nt, "vt_r", (l, b, s))

            def head(l, b, s):
                nt = dict(sub_tiles(BLOCKS[b][1]))[s]
                ws = (0, 1) if full(l, b) else (1,)
                n, tile = HEADS * nt, (BLOCKS[b][0] - CTX) // P + s
                for w in ws:
                    pool.wait_ge(*at("hd_var", (l, b, s, w)))
                    small_pow(112 + 48 * w, 96 + 48 * w, n, "hd_r", (l, b, s, w))
                if b == 0:
                    return
                tmp = qk_sq[:, :, :, :].rearrange("p t h d -> p (t h d)")
                tt = [tmp[:, e * n * ROPE // 2:(e + 1) * n * ROPE // 2].rearrange("p (t h d) -> p t h d", t=nt, h=HEADS) for e in range(4)]
                for w in ws:
                    k2 = (l, b, s, w)
                    pool.wait_ge(*at("hd_n", k2))
                    rope = qk[:, w, :nt, :, NOPE:].rearrange("p t h d -> p (t h) d")
                    g = pcol("grope", w * ROPE, (w + 1) * ROPE).unsqueeze(1).to_broadcast([P, n, ROPE])
                    pool.tensor_tensor(rope, rope, g, ALU.mult).then_inc(*inc("qk_gain", k2))
                    pool.wait_ge(*at("qk_gain", k2))
                    x = [qk[:, w, :nt, :, NOPE + e:QKD:2] for e in range(2)]
                    cs = [trig[:, tile:tile + nt, e, :].unsqueeze(2).to_broadcast([P, nt, HEADS, ROPE // 2]) for e in range(2)]
                    if w == 1 and len(ws) == 2:
                        pool.wait_ge(*at("qk_done", (l, b, s, 0)))
                    pool.tensor_tensor(tt[0], x[0], cs[0], ALU.mult)
                    pool.tensor_tensor(tt[1], x[1], cs[1], ALU.mult)
                    pool.tensor_tensor(tt[2], x[0], cs[1], ALU.mult)
                    pool.tensor_tensor(tt[3], x[1], cs[0], ALU.mult).then_inc(*inc("rot", k2))
                    pool.wait_ge(*at("rot", k2))
                    pool.tensor_tensor(x[0], tt[0], tt[1], ALU.subtract)
                    pool.tensor_tensor(x[1], tt[2], tt[3], ALU.add).then_inc(*inc("qk_done", k2))

            pool.wait_ge(*at("ones"))
            for l in range(DEPTH):
                for what, *arg in p1_schedule(l):
                    if what == "norm":
                        norm(l, 0, arg[0])
                    elif what in ("mix", "tok", "head"):
                        {"mix": mix, "tok": tok, "head": head}[what](l, *arg)
                for g, (c0, L) in enumerate(((0, CTX), (CTX, SEQ))):
                    if g == 0 and not full(l, 0):
                        continue
                    if g == 0 or not full(l, 0):
                        for j in range(N_ST):
                            pool.wait_ge(*at(f"qk_store{j}", (l, 2, 2, 1, HEADS - N_ST + j)))
                        pool.wait_ge(*at("v_store", (l, 2, 2)))
                        pool.wait_ge(*at("ya_store", (l, 2, 2)))
                        pool.wait_ge(*at("b_store", (l, 2, 1)))
                    else:
                        pool.wait_ge(*at("yb_store", (l, 0, 1, 0)))
                    pool.memset(pz[:, :, 0:HALO], 0.0).then_inc(*inc("pool_edge", (l, g)))
                    pool.memset(pz[:, :, HALO + L:2 * HALO + L], 0.0).then_inc(*inc("pool_edge", (l, g)))
                    pool.wait_ge(*at("pz_in", (l, g)))
                    pool.wait_ge(*at("pinv_in", (l, g)))
                    pool.wait_ge(*at("pool_edge", (l, g)))
                    W2 = L + 2 * HALO

                    def step(dst, src, d, lo, hi, parts=slice(None)):
                        up = 0 if d == 0 else d
                        pool.tensor_tensor(dst[parts, lo:hi], src[parts, lo - max(d, 1):hi - max(d, 1)], src[parts, lo + up:hi + up],
                                           ALU.add).then_inc(*inc("win", (l, g)))
                        pool.wait_ge(C.sem("win"), C.total["win"])

                    def means(i, parts, ssrc):
                        pool.tensor_tensor(pd[parts, i, :L], ssrc[parts, HALO:HALO + L], pinv[parts, i, :L], ALU.mult)\
                            .then_inc(*inc("win", (l, g)))
                        pool.wait_ge(C.sem("win"), C.total["win"])
                        pool.tensor_tensor(pd[parts, i, :L], pd[parts, i, :L], pz[parts, i, HALO:HALO + L], ALU.subtract)\
                            .then_inc(*inc("pool_d", (l, g, i)))
                        pool.wait_ge(C.sem("pool_d"), C.total["pool_d"])
                    lower, upper = slice(0, 64), slice(64, 128)
                    step(ps2, pz[:, 0, :], 0, 1, W2)
                    step(ps4, ps2, 1, 2, W2 - 1)
                    means(0, lower, ps2)
                    means(0, upper, ps4)
                    step(ps2, pz[:, 1, :], 0, 1, W2)
                    step(ps4, ps2, 1, 2, W2 - 1)
                    step(ps2, ps4, 2, 4, W2 - 3)
                    means(1, lower, ps2)
                    step(ps4, ps2, 4, 8, W2 - 8)
                    means(1, upper, ps4)
                C.alias("pool_done", l, "pool_d")
                st, groups = att_plan(l)
                pool.wait_ge(*at("yb_store", (l, 1, 1, SEQ - NMAX)))
                pool.wait_ge(*at("ones"))
                pool.tensor_copy(flag[:, 4:5], half[:, 0:1]).then_inc(*inc("att_free", l))
                for g, (hd, i, col, nk) in enumerate(st):
                    pool.wait_ge(*at("rden", (l, g)))
                    pool.tensor_tensor(prob[:, g % 4, 0:nk * P], prob[:, g % 4, 0:nk * P],
                                       den[:, 1, g % 4:g % 4 + 1].to_broadcast([P, nk * P]), ALU.mult).then_inc(*inc("pn", (l, g)))
                for b in layer_blocks(l):
                    norm(l, 1, b)
                if l + 1 < DEPTH:
                    norm(l + 1, 0, 0)

        @block.tensor
        def _(pe):
            def three(out, wh, wl, hh, hl, first, last, inc_last=None):
                pe.matmul(out, wh, hh, start=first, stop=False)
                pe.matmul(out, wh, hl, start=False, stop=False)
                return pe.matmul(out, wl, hh, start=False, stop=last)

            def norm_stat(l, which, b):
                T, key = BLOCKS[b][1], (l, which, b)
                pe.wait_ge(*at("norm_sum", (key, 1)))
                for t in range(T // P):
                    for h in range(2):
                        x = pe.matmul(psum[:, 7, t:t + 1], t32[:, h, t * P:(t + 1) * P], ones[:, 0:1], start=(h == 0), stop=(h == 1))
                x.then_inc(*inc("norm_mm", key))

            def norm_bc(l, which, b):
                T, key = BLOCKS[b][1], (l, which, b)
                pe.wait_ge(*at("norm_diag", key))
                pe.matmul(psum[:, 7, :T], ones[:, :], diag[:, :T], start=True, stop=True).then_inc(*inc("norm_bc", key))

            def ada_unit(j):
                m, kh = divmod(j, KT // ADA_K)
                pe.wait_ge(*at("ada_lo", j))
                if kh == 0 and m >= 2:
                    pe.wait_ge(*at("ada_row", m - 2))
                for k in range(ADA_K):
                    first, last = kh == 0 and k == 0, kh == 1 and k == ADA_K - 1
                    pe.matmul(psum[0:4, 4 + m % 2, :], silu_s[:, kh * ADA_K + k, :], ada_hi[:, j % 2, k, :], start=first, stop=False)
                    x = pe.matmul(psum[0:4, 4 + m % 2, :], silu_s[:, kh * ADA_K + k, :], ada_lo[:, j % 2, k, :], start=False, stop=last)
                x.then_inc(*inc("ada_mm", j))

            def ada_transpose(m):
                pe.wait_ge(*at("ada_row", m))
                for i in range(ADA_W // P):
                    col = 4 * ((m % ADA_M) * (ADA_W // P) + i)
                    x = pe.transpose(psum[:, 6, col:col + 4], ada_row[:, m % 2, i * P:(i + 1) * P], ident[0:4, 0:4])
                x.then_inc(*inc("ada_tr", m))

            def in_chunk(l, b, i):
                T = BLOCKS[b][1]
                cs = P1_CHUNKS[full(l, b)]
                kb, nt_all, n = (l, b), T // P, start["p1", l, b] + i
                pe.wait_ge(*at("w_lo", n))
                if i >= 2:
                    pe.wait_ge(*at("in_free", (kb, i - 2)))
                elif (l, b) > (0, 0):
                    prev_banks(pe, l, b)
                for k in range(KT):
                    if i == 0:
                        pe.wait_ge(*at("h_lo", ((l, 0, b), k)))
                    x = three(psum[:, i % 2, :T], w_hi[:, n % 2, k * P:(k + 1) * P], w_lo[:, n % 2, k * P:(k + 1) * P],
                              h_hi[:, k, :T], h_lo[:, k, :T], k == 0, k == KT - 1)
                x.then_inc(*inc("w_used", n))
                if i == len(cs) - 1:
                    pe.wait_ge(*at("pq_sq", (kb, 2)))
                    if kb != (0, 0):
                        hs = [h for h in head_seq() if (h[0], h[1]) < kb and h[4] % 2 == 1]
                        done = [h for h in hs if p1_before(h, l, b)]
                        pe.wait_ge(*at("qk_lo", done[-1]))
                    for t in range(nt_all):
                        if full(l, b):
                            for k in range(2):
                                pe.matmul(psum[:, 3, t:t + 1], pq_sq[:, k, t * P:(t + 1) * P], ones[:, 0:1], start=(k == 0), stop=(k == 1))
                        x = pe.matmul(psum[:, 3, 4 + t:5 + t], pq_sq[:, 2, t * P:(t + 1) * P], ones[:, 0:1], start=True, stop=True)
                    x.then_inc(*inc("tok_mm", kb))

            def mix(l, b):
                T = BLOCKS[b][1]
                pe.wait_ge(*at("in_free", ((l, b), 3)))
                pe.wait_ge(*at("tok_var", (l, b)))
                if (l, b) > (0, 0):
                    done = [h for h in head_seq() if p1_before(h, l, b)]
                    pe.wait_ge(*at("qk_lo", done[-1]))
                    tb = [x for x in tok_seq if tok_before(x, l, b)]
                    for x in tb[-3:]:
                        pe.wait_ge(*(at("v_lo_t", x) if x[3] == "kv" else at("tok_act", x)))
                if b == 2:
                    pe.wait_ge(*at("krt", (l, b, 0)))
                for s, nt in sub_tiles(T):
                    for t in range(nt):
                        for i in range(2):
                            x = pe.transpose(psum[:, 2 + s // 2, t * 256 + i * P:t * 256 + (i + 1) * P],
                                             v_sb[:, i, (s + t) * P:(s + t + 1) * P], ident[:, :])
                    x.then_inc(*inc("mix_tr", (l, b, s)))
                for s, nt in sub_tiles(T):
                    pe.wait_ge(*at("vt_n", (l, b, s)))
                    if s:
                        pe.wait_ge(*at("mix_g", (l, b, s - 2, 1)))
                    for t in range(nt):
                        for hd in range(4):
                            rows = slice(64 * (hd % 2), 64 * (hd % 2) + 64)
                            x = pe.matmul(psum[rows, 4 + hd // 2, t * P:(t + 1) * P], vtok[:, s + t, hd * 64:(hd + 1) * 64],
                                          pcol("wsp", hd * P, (hd + 1) * P), start=True, stop=True)
                    x.then_inc(*inc("mix_mm", (l, b, s)))

            def tok(l, b, s):
                T = BLOCKS[b][1]
                nt = dict(sub_tiles(T))[s]
                pe.wait_ge(*at("wqkv_lo", l))
                pe.wait_ge(*at("pq_lo", ((l, b), 2)))
                mixed = [x[1] for x in p1_schedule(l) if x[0] == "mix" and p1_pos(l, x) < p1_pos(l, ("tok", b, s))]
                if mixed:
                    pe.wait_ge(*at("mix_done", (l, mixed[-1])))
                for t in range(nt):
                    ts = slice((s + t) * P, (s + t + 1) * P)
                    for kind, c in tok_products(l, b, s, t):
                        key = (l, b, s + t, kind, c)
                        bank, i = tok_bank(*key), tok_seq.index(key)
                        if i >= 3:
                            x = tok_seq[i - 3]
                            pe.wait_ge(*(at("v_lo_t", x) if x[3] == "kv" else at("tok_act", x)))
                        if kind == "q":
                            for k in range(2):
                                kc = slice(k * NQ + c * NQ // 2, k * NQ + (c + 1) * NQ // 2)
                                x = three(psum[:, bank, 0:NQ // 2], pq_hi[:, k, ts], pq_lo[:, k, ts],
                                          wqkv_hi[:, kc], wqkv_lo[:, kc], k == 0, k == 1)
                        else:
                            kc = slice(2 * NQ + c * NKV // 2, 2 * NQ + (c + 1) * NKV // 2)
                            x = three(psum[:, bank, :], pq_hi[:, 2, ts], pq_lo[:, 2, ts], wqkv_hi[:, kc], wqkv_lo[:, kc], True, True)
                        x.then_inc(*inc("tok_mm2", key))
                pe.wait_ge(*at("tok_var", (l, b)))
                done = [h for h in head_seq() if subs().index(h[:3]) < subs().index((l, b, s))]
                if done:
                    pe.wait_ge(*at("qk_lo", done[-1]))
                if mixed:
                    pe.wait_ge(*at("vt_n", (l, mixed[-1], sub_tiles(BLOCKS[mixed[-1]][1])[-1][0])))
                for t in range(nt):
                    x = pe.transpose(psum[:, 3, t * P:(t + 1) * P], kr_sb[:, (s + t) * P:(s + t + 1) * P], ident[:, :])
                x.then_inc(*inc("kr_tr", (l, b, s)))

            def head(l, b, s):
                nt = dict(sub_tiles(BLOCKS[b][1]))[s]
                ws = (0, 1) if full(l, b) else (1,)
                for w in ws:
                    pe.wait_ge(*(at("qk_done", (l, b, s, w)) if b else at("hd_n", (l, b, s, w))))
                    for hd in range(HEADS):
                        if hd >= 2:
                            pe.wait_ge(*at("qk_lo", (l, b, s, w, hd - 2)))
                        elif w == 1 and len(ws) == 2:
                            pe.wait_ge(*at("qk_lo", (l, b, s, 0, HEADS - 2 + hd)))
                        if hd == 1:
                            pe.wait_ge(*at("krt", (l, b, s)))
                        if hd == 0:
                            mixed = [x[1] for x in p1_schedule(l) if x[0] == "mix" and p1_pos(l, x) < p1_pos(l, ("head", b, s))]
                            if mixed:
                                pe.wait_ge(*at("vt_n", (l, mixed[-1], sub_tiles(BLOCKS[mixed[-1]][1])[-1][0])))
                        for t in range(nt):
                            x = pe.transpose(psum[:QKD, 2 + hd % 2, t * P:(t + 1) * P], qk[:, w, t, hd, :], ident[:, :])
                        x.then_inc(*inc("qk_tr", (l, b, s, w, hd)))

            pe.wait_ge(*at("silu_s"))
            pe.wait_ge(*at("consts"))
            for j in range(ADA_N):
                ada_unit(j)
                if j % 2 and j > 2:
                    ada_transpose(j // 2 - 1)
            ada_transpose(ADA_M - 1)
            pe.wait_ge(*at("ones"))
            for l in range(DEPTH):
                if l == 0:
                    pe.wait_ge(*at("mod", 0))
                for what, *arg in p1_schedule(l):
                    if what == "norm":
                        norm_stat(l, 0, arg[0])
                        norm_bc(l, 0, arg[0])
                    elif what == "in":
                        for i in range(arg[1], min(arg[2], len(P1_CHUNKS[full(l, arg[0])]))):
                            in_chunk(l, arg[0], i)
                    elif what != "wqkv":
                        {"mix": mix, "tok": tok, "head": head}[what](l, *arg)
                for g, (c0, L) in enumerate(((0, CTX), (CTX, SEQ))):
                    if g == 0 and not full(l, 0):
                        continue
                    for i in range(2):
                        pe.wait_ge(*at("pool_d", (l, g, i)))
                        for q in range(0, L, NMAX):
                            w = min(NMAX, L - q)
                            if i or q or (g and full(l, 0)):
                                prev = pool_seq(l)[pool_seq(l).index((l, g, i, q)) - 1]
                                pe.wait_ge(*at("pool_out", prev))
                            pe.matmul(psum[:, (i * 2 + q // NMAX) % 2, :w], pcol("wpool", i * P, i * P + P), pd[:, i, q:q + w],
                                      start=True, stop=True).then_inc(*inc("pool_mm", (l, g, i, q)))
                st, groups = att_plan(l)
                G, per = len(st), len(steps(l))
                npair = per // 2
                pe.wait_ge(*at("pool_out", pool_seq(l)[-1]))
                for g in range(G + 4):
                    def t_group(q, tg, k0, n):
                        if k0 == 0:
                            pe.wait_ge(*at("pn", (l, q)))
                        if tg >= 2:
                            pe.wait_ge(*at("t_lo", (l, tg - 2)))
                        for k in range(n):
                            x = pe.transpose(psum[:, 5 + tg % 2, k * P:(k + 1) * P], prob[:, q % 4, (k0 + k) * P:(k0 + k + 1) * P],
                                             ident[:, :])
                        x.then_inc(*inc("t_mm", (l, tg)))

                    def s_part(hd, i, col, nk, part):
                        j = hd % 2
                        k0, w = score_parts(g, nk)[part]
                        if part == 0:
                            if i == 0:
                                pe.wait_ge(*at(f"kqv{j}", ("att", l), plus=48 * (hd // 2 + 1)))
                            if g >= 2:
                                pe.wait_ge(*at("exp", (l, g - 2)))
                        if part == len(score_parts(g, nk)) - 1 and g >= 1:
                            pe.wait_ge(*at("exp", (l, g - 1)))
                        kc, qc = slice(k0, k0 + w), slice(col, col + P)
                        return three(scores(g, nk)[:, kc], qh[:, j, 0, qc], qh[:, j, 1, qc], kh[:, j, 0, kc], kh[:, j, 1, kc], True, True)
                    ts = groups[g - 2] if 0 <= g - 2 < G else []
                    n_parts = len(score_parts(g, st[g][3])) if g < G else 0
                    for part in range(3):
                        if part < len(ts):
                            t_group(g - 2, *ts[part])
                        if part < n_parts:
                            x = s_part(*st[g], part)
                            if part == n_parts - 1:
                                x.then_inc(*inc("s_mm", (l, g)))
                    if g >= 4 and g % 2 == 0 and (g - 4) // 2 < G // 2:
                        pr = (g - 4) // 2
                        hq, pi = divmod(pr, npair)
                        nk = steps(l)[2 * pi][1]
                        pe.wait_ge(*at("t_lo", (l, groups[2 * pr + 1][-1][0])))
                        if pr >= 1:
                            h2, p2 = divmod(pr - 1, npair)
                            pe.wait_ge(*at("yc", (l, h2, p2)))
                        out = psum[:, 7, 0:256]
                        for k in range(nk):
                            pe.matmul(out, vh[:, hq % 2, k, :], pt_hi[:, pr % 2, k, :], start=(k == 0), stop=False)
                            x = pe.matmul(out, vh[:, hq % 2, k, :], pt_lo[:, pr % 2, k, :], start=False, stop=(k == nk - 1))
                        x.then_inc(*inc("pv_mm", (l, hq, pi)))
                for b in layer_blocks(l):
                    c0, T = BLOCKS[b]
                    n0 = start["out", l, b]
                    for m in range(KT):
                        n = n0 + m
                        pe.wait_ge(*at("w_lo", n))
                        if m >= 4:
                            pe.wait_ge(*at("out_acc", (l, b, m - 4)))
                        elif b != layer_blocks(l)[0]:
                            pe.wait_ge(*at("out_acc", (l, b - 1, m + 4)))
                        else:
                            pe.wait_ge(*at("yc", (l, HEADS - 1, npair - 1)))
                        for k in range(KT):
                            if m == 0:
                                pe.wait_ge(*at("y_lo", (l, b, k)))
                            x = three(psum[:, m % 4, :T], w_hi[:, n % 2, k * P:(k + 1) * P], w_lo[:, n % 2, k * P:(k + 1) * P],
                                      h_hi[:, k, :T], h_lo[:, k, :T], k == 0, k == KT - 1)
                        x.then_inc(*inc("w_used", n))
                        if l == 0:
                            j = layer_blocks(l).index(b) * KT + m
                            ada_unit(ADA_N + j)
                            if j % 2 and j > 2:
                                ada_transpose(ADA_M + j // 2 - 1)
                if l == 0:
                    ada_transpose(2 * ADA_M - 1)
                for b in layer_blocks(l):
                    c0, T = BLOCKS[b]
                    n0 = start["ffn", l, b]
                    if b == layer_blocks(l)[0]:
                        norm_stat(l, 1, b)
                        norm_bc(l, 1, b)
                    for k in range(KT):
                        pe.wait_ge(*at("h_lo", ((l, 1, b), k)))
                    prev = layer_blocks(l).index(b)
                    pe.wait_ge(*(at("out_acc", (l, layer_blocks(l)[-1], KT - 1)) if prev == 0 else
                                 at("dn_acc_end", (l, layer_blocks(l)[prev - 1]))))
                    g32b = at("gu32", ("ffn", l, b))[1]
                    sgb = at("sg", ("ffn", l, b))[1]
                    with pe.Fori(0, FT // 2, 1) as i:
                        for j in range(4):
                            n = n0 + j
                            pe.wait_ge(C.sem("w_lo"), i * 4 + (n + 1))
                            if j % 2 == 0:
                                pe.wait_ge(C.sem("sg"), i * 2 + (sgb + j // 2 - 1))
                            else:
                                pe.wait_ge(C.sem("gu32"), i * 2 + (g32b + j // 2 - 1))
                            for k in range(KT):
                                x = three(psum[:, j, :T], w_hi[:, n % 2, k * P:(k + 1) * P], w_lo[:, n % 2, k * P:(k + 1) * P],
                                          h_hi[:, k, :T], h_lo[:, k, :T], k == 0, k == KT - 1)
                            x.then_inc(C.sem("w_used"), 1)
                    C.skip("w_used", 2 * FT)
                    n1 = n0 + 2 * FT
                    pe.wait_ge(*at("gu_lo", ("ffn", l, b), plus=FT))
                    nxt = norm_next(l, b)
                    for m in range(KT):
                        k0 = 0
                        for j, nk in enumerate(DN_K):
                            n = n1 + 3 * m + j
                            pe.wait_ge(C.sem("w_lo"), n + 1)
                            if j == 0 and m >= 4:
                                pe.wait_ge(*at("dn_acc", (l, b, m - 4)))
                            for k in range(nk):
                                f = k0 + k
                                x = three(psum[:, m % 4, :T], w_hi[:, n % 2, k * P:(k + 1) * P], w_lo[:, n % 2, k * P:(k + 1) * P],
                                          gu_hi[:, f, :T], gu_lo[:, f, :T], f == 0, f == FT - 1)
                            x.then_inc(C.sem("w_used"), 1)
                            k0 += nk
                            if nxt and 3 * m + j == 4:
                                norm_stat(*nxt)
                            if nxt and 3 * m + j == 8:
                                norm_bc(*nxt)
                    C.skip("w_used", 3 * KT)
    return C


def kernel(**inputs):
    import numpy as np
    import concourse.bacc as bacc
    from concourse import mybir as mb
    from concourse.bass_utils import run_bass_kernel_spmd as run

    a = {k: np.asarray(v) for k, v in inputs.items()}

    def tiles(w):
        return w.reshape(-1, P, w.shape[-1]).transpose(1, 0, 2)

    def cols(v):
        return v.reshape(-1, P).T

    def chunk(w):
        w = tiles(w).reshape(P, -1)
        return np.pad(w, ((0, 0), (0, CH - w.shape[1])))

    chunks, prm, ada_p, w_ada, wqkv = [], [], [], [], []
    for l in range(DEPTH):
        w_in = a["w_in"][l]
        cs = [chunk(w_in[:, P * m:P * m + P]) for m in range(9)] + [chunk(w_in[:, -P:])]
        cs += [chunk(a["w_out"][l][:, P * m:P * m + P]) for m in range(KT)]
        gu = a["w_gate_up"][l]
        for f in range(FT):
            cs += [chunk(gu[:, P * f:P * f + P]), chunk(gu[:, DFF + P * f:DFF + P * f + P])]
        for m in range(KT):
            k0 = 0
            for nk in DN_K:
                cs.append(chunk(a["w_down"][l][k0 * P:(k0 + nk) * P, P * m:P * m + P]))
                k0 += nk
        chunks.append(np.stack(cs))
        wqkv.append(np.concatenate([tiles(a["w_q_b"][l]).reshape(P, -1), a["w_kv_b"][l]], 1))
        pool = np.zeros((P, 2, P), np.float32)
        for g in range(4):
            pool[64 * (g % 2):64 * (g % 2) + 64, g // 2, 64 * (g % 2):64 * (g % 2) + 64] = a["w_pool"][l][g]
        bsp = np.repeat(a["b_spatial"][l].reshape(2, 2, P), 64, axis=1).transpose(1, 0, 2)
        gqk = np.stack([a["q_norm_g"][l], a["k_norm_g"][l]])
        gfull, gnope = np.ones((P, 2), np.float32), np.ones((P, 2), np.float32)
        gfull[:QKD], gnope[:NOPE] = gqk.T, gqk[:, :NOPE].T
        prm.append(np.concatenate([
            cols(a["sgu_norm_g"][l]), cols(a["pool_scale"][l]), cols(a["q_a_norm_g"][l]), cols(a["kv_a_norm_g"][l]),
            gfull, gnope, np.broadcast_to(gqk[:, NOPE:].reshape(1, -1), (P, 2 * ROPE)),
            bsp.reshape(P, -1), pool.reshape(P, -1), a["w_spatial"][l].transpose(2, 0, 1).reshape(P, -1)], 1))
        ada_p.append(np.concatenate([cols(a["norm1_g"][l]), cols(a["norm2_g"][l]), cols(a["b_ada"][l])], 1))
        w_ada.append(tiles(a["w_ada"][l]).reshape(P, KT // ADA_K, ADA_K, ADA_M, ADA_W).transpose(3, 1, 0, 2, 4)
                     .reshape(ADA_N, P, ADA_K, ADA_W))

    def inv(n):
        t = np.arange(n)
        g = [1.0 / (np.clip(t + w // 2, 0, n) - np.clip(t - w // 2, 0, n)) for w in WINDOWS]
        return np.repeat(np.stack(g).reshape(2, 2, n), 64, axis=1).transpose(1, 0, 2).astype(np.float32)

    row, col = np.divmod(np.arange(SEQ), 64)
    f = np.float32(10000.0) ** (-np.arange(ROPE // 4, dtype=np.float32) / np.float32(ROPE // 4))
    ang = np.concatenate([row[:, None].astype(np.float32) * f, col[:, None].astype(np.float32) * f], -1).astype(np.float32)
    trig = np.stack([np.cos(ang), np.sin(ang)], 1).reshape(SEQ // P, P, 2, ROPE // 2).transpose(1, 0, 2, 3)

    arrays = {
        "x": np.concatenate([a["ctx"][0], a["x"][0]]).T,
        "c": np.stack([cols(a["c"][0]), cols(a["c_ctx"])], -1),
        "w": np.stack(chunks), "prm": np.stack(prm), "ada_p": np.stack(ada_p, 1), "w_ada": np.stack(w_ada),
        "wqkv": np.stack(wqkv), "inv_lat": inv(SEQ), "inv_ctx": inv(CTX), "trig": trig.astype(np.float32),
        "ident": np.eye(P, dtype=np.float32),
    }
    arrays = {k: np.ascontiguousarray(v) for k, v in arrays.items()}

    def program(known):
        nc = bacc.Bacc("TRN2", target_bir_lowering=False, num_devices=1)
        t_in = {k: nc.dram_tensor(f"in_{k}", v.shape, mb.dt.from_np(v.dtype), kind="ExternalInput").ap() for k, v in arrays.items()}
        t_in["out"] = nc.dram_tensor("out_0", (DM, SEQ), F32, kind="ExternalOutput").ap()
        return nc, build(nc, t_in, known)

    _, counts = program({})
    nc, _ = program(counts.value)
    r = run(nc, [{f"in_{k}": v for k, v in arrays.items()}], core_ids=[0])
    return np.ascontiguousarray(r.results[0]["out_0"].T)[None]
```

```python
from contextlib import ExitStack

import concourse.bass as bass
from concourse import mybir

F32 = mybir.dt.float32
F32R = mybir.dt.float32r
ALU = mybir.AluOpType
ACT = mybir.ActivationFunctionType
AX = mybir.AxisListType

P = 128
DM = 1024
KT = DM // P
CTX = 256
SEQ = 1024
NTOK = CTX + SEQ
DEPTH = 2
HEADS = 8
VD = 64
NOPE = 64
ROPE = 32
QKD = NOPE + ROPE
DFF = 2816
FT = DFF // P
WINDOWS = (2, 4, 8, 16)
HALO = max(WINDOWS) // 2
EPS = 1e-6
SCALE = QKD ** -0.5

BLOCKS = ((0, CTX), (CTX, 512), (CTX + 512, 512))
NMAX = 512
CH = KT * P

C_IN, N_IN = 0, 10
C_OUT = C_IN + N_IN
C_GU = C_OUT + KT
DN_K = (8, 7, 7)
C_DN = C_GU + 2 * FT
NCH = C_DN + KT * len(DN_K)
P1_CHUNKS = {True: (2, 3, 6, 7, 8, 9, 0, 1, 4, 5), False: (8, 9)}
NQ = HEADS * QKD
NKV = HEADS * (NOPE + VD)

PRM = {}
_at = 0
for _n, _w in (("sgu", 2), ("pscale", 2), ("qa", 2), ("kva", 1),
               ("gfull", 2), ("gnope", 2), ("grope", 2 * ROPE), ("bsp", 256), ("wpool", 256), ("wsp", 512)):
    PRM[_n] = (_at, _at + _w)
    _at += _w
NPRM = _at
LATE = NTOK - 2 * P
N_ST = 4

ADA_W = 512
ADA_K = 4
ADA_M = 6 * DM // ADA_W
N_ADA = 4
ADA_N = ADA_M * KT // ADA_K


def full(l, b):
    return not (l == DEPTH - 1 and b == 0)


def layer_blocks(l):
    return [b for b in range(len(BLOCKS)) if full(l, b)]


class Count:

    def __init__(self, nc, ctx, known):
        self.nc, self.ctx, self.known = nc, ctx, known
        self.sems, self.total, self.value = {}, {}, {}

    def sem(self, name):
        if name not in self.sems:
            self.sems[name] = self.ctx.enter_context(self.nc.semaphore(name))
            self.total[name] = 0
        return self.sems[name]

    def inc(self, name, key=None, by=1):
        s = self.sem(name)
        self.total[name] += by
        self.value[name, key] = name, self.total[name]
        return s, by

    def alias(self, name, key, of):
        self.value[name, key] = of, self.total[of]

    def skip(self, name, n):
        self.sem(name)
        self.total[name] += n

    def now(self, name, tag):
        self.sem(name)
        self.value[name, tag] = name, self.total[name]

    def at(self, name, key=None, plus=0):
        of, value = self.known.get((name, key), (name, 1))
        return self.sem(of), value + plus


def build(nc, t_in, known):
    ctx = ExitStack()
    with ctx:
        C = Count(nc, ctx, known)
        inc, at = C.inc, C.at

        def sb(name, shape, dt=F32):
            return ctx.enter_context(nc.sbuf_tensor(name, shape, dt))

        X = sb("X", [P, KT, NTOK])
        raw = sb("raw", [P, 2, CH])
        w_hi = sb("w_hi", [P, 2, CH], F32R)
        w_lo = sb("w_lo", [P, 2, CH], F32R)
        prm = sb("prm", [P, NPRM])
        ada_p = sb("ada_p", [P, DEPTH, 64])
        mod = sb("mod", [P, DEPTH, 48, 2])
        gain = sb("gain", [P, DEPTH, 2, KT, 2])
        ident = sb("ident", [P, P])
        ones = sb("ones", [P, P])
        half = sb("half", [P, 1])
        t32 = sb("t32", [P, 2, NMAX])
        silu_c = sb("silu_c", [P, 2, KT, 2])
        diag = sb("diag", [P, NMAX])
        flag = sb("flag", [P, 8])
        nst = sb("nst", [P, 8])
        trig = sb("trig", [P, SEQ // P, 2, ROPE // 2])

        psum = ctx.enter_context(nc.psum_tensor("psum", [P, 8, 512], F32))

        qk_scr = nc.dram_tensor("qk_scr", [DEPTH, 2, HEADS, QKD, 2, NTOK], F32).ap()
        v_scr = nc.dram_tensor("v_scr", [DEPTH, HEADS, NTOK, 2 * VD], F32).ap()
        y_scr = nc.dram_tensor("y_scr", [DEPTH, DM, NTOK], F32).ap()
        b_scr = nc.dram_tensor("b_scr", [DEPTH, 2, P, NTOK], F32).ap()

        def overlay(specs):
            with ExitStack() as st:
                return [st.enter_context(nc.sbuf_tensor(n, s, d)) for n, s, d in specs]

        pt_hi, pt_lo, kh, qh, vh, prob, yc, yc_lo, amax, den, pz, ps2, ps4 = overlay([
            ("pt_hi", [P, 2, NTOK // P, 256], F32R), ("pt_lo", [P, 2, NTOK // P, 256], F32R),
            ("kh", [QKD, 2, 2, NTOK], F32R), ("qh", [QKD, 2, 2, NTOK], F32R),
            ("vh", [P, 2, NTOK // P, 2 * VD], F32R), ("prob", [P, 4, NTOK], F32),
            ("yc", [VD, 2, 256], F32), ("yc_lo", [VD, 2, 256], F32),
            ("amax", [P, 2, 4], F32), ("den", [P, 2, 4], F32),
            ("pz", [P, SEQ + 2 * HALO], F32), ("ps2", [P, SEQ + 2 * HALO], F32), ("ps4", [P, SEQ + 2 * HALO], F32)])
        pinv = t32[:, :, :].rearrange("p a n -> p (a n)")
        ada_raw, = overlay([("ada_raw", [P, N_ADA, ADA_K, ADA_W], F32)])
        h_hi = sb("h_hi", [P, KT, NMAX], F32R)
        h_lo = sb("h_lo", [P, KT, NMAX], F32R)
        (nrm_t, wqkv_hi, wqkv_lo, pq_hi, pq_lo, u_sb, v_sb, vtok, kr_sb, qk, qk_sq, v_st, st_qk, mixo, yst,
         stat, krt) = overlay([
             ("nrm_t", [P, 4, NMAX], F32), ("wqkv_hi", [P, 2 * NQ + NKV], F32R), ("wqkv_lo", [P, 2 * NQ + NKV], F32R),
             ("pq_hi", [P, 3, NMAX], F32R), ("pq_lo", [P, 3, NMAX], F32R),
             ("u_sb", [P, 2, NMAX], F32), ("v_sb", [P, 2, NMAX], F32),
             ("vtok", [P, 4, 256], F32), ("kr_sb", [P, NMAX], F32),
             ("qk", [P, 2, 2, HEADS, QKD], F32), ("qk_sq", [P, 2, HEADS, QKD], F32),
             ("v_st", [P, 2, HEADS, 2, VD], F32R), ("st_qk", [QKD, N_ST, 2, 256], F32R),
             ("mixo", [P, 2, NMAX], F32), ("yst", [P, 2, NMAX], F32),
             ("stat", [P, 256], F32), ("krt", [P, 2, ROPE], F32)])
        pq32 = nrm_t
        ada_row = nrm_t[0:2, 0:2, :]
        pq_sq = qk_sq[:, :, :, :].rearrange("p t h d -> p (t h d)")[:, 0:3 * NMAX].rearrange("p (j n) -> p j n", n=NMAX)
        yraw, = overlay([("yraw", [P, KT, NMAX], F32)])
        fnrm_t, gu_hi, gu_lo = overlay([
            ("fnrm_t", [P, 4, NMAX], F32), ("gu_hi", [P, FT, NMAX], F32R), ("gu_lo", [P, FT, NMAX], F32R)])
        sg, gu32 = fnrm_t[:, 0:2, :], fnrm_t[:, 2:4, :]

        def pcol(name, a=0, b=None):
            s, e = PRM[name]
            return prm[:, s + a:(s + b if b is not None else e)]

        block = ctx.enter_context(nc.Block())

        start, stream = {}, []
        for l in range(DEPTH):
            for b in range(len(BLOCKS)):
                start["p1", l, b] = len(stream)
                stream += [(l, c) for c in P1_CHUNKS[full(l, b)]]
            for b in layer_blocks(l):
                start["out", l, b] = len(stream)
                stream += [(l, c) for c in range(C_OUT, C_GU)]
            for b in layer_blocks(l):
                start["ffn", l, b] = len(stream)
                stream += [(l, c) for c in range(C_GU, NCH)]
        n_chunks = len(stream)

        def steps(l):
            lat = [(CTX + P * t, NTOK // P) for t in range(SEQ // P)]
            return lat + ([(P * t, CTX // P) for t in range(CTX // P)] if l < DEPTH - 1 else [])

        def t_groups(nk):
            sizes = [4] * (nk // 4)
            if nk % 4:
                sizes.insert(1, nk % 4)
            return [(sum(sizes[:i]), n) for i, n in enumerate(sizes)]

        sub_tiles = lambda T: [(s, min(2, T // P - s)) for s in range(0, T // P, 2)]

        def at_prev(l, b):
            seq = [(i, j) for i in range(DEPTH) for j in range(len(BLOCKS)) if full(i, j)]
            before = [x for x in seq if x < (l, b)]
            return before[-1]

        def p1_schedule(l):
            first = [("na", 0), ("nb", 0), ("nc", 0), ("nh", 0), ("in", 0, 0, 1), ("wqkv",), ("in", 0, 1, 3),
                     ("mt", 0), ("in", 0, 3, 5), ("na", 1), ("in", 0, 5, 6), ("tok", 0, 0), ("ha", 0, 0), ("in", 0, 6, 7), ("nb", 1),
                     ("in", 0, 7, 8), ("mm", 0), ("nc", 1), ("in", 0, 8, 9), ("ms", 0), ("nh", 1), ("in", 0, 9, 10), ("bs", 0), ("hb", 0, 0),
                     ("in", 1, 0, 1), ("na", 2), ("in", 1, 1, 2), ("ht", 0, 0)]
            last = [("in", 0, 0, 1), ("wqkv",), ("nb", 1), ("in", 0, 1, 2), ("nc", 1), ("nh", 1), ("tok", 0, 0), ("ha", 0, 0),
                    ("in", 1, 0, 1), ("hb", 0, 0), ("na", 2), ("in", 1, 1, 2), ("ht", 0, 0)]
            rest = [("in", 1, 2, 3), ("nb", 2), ("mt", 1), ("in", 1, 3, 5), ("nc", 2),
                    ("in", 1, 5, 6), ("tok", 1, 0), ("ha", 1, 0), ("in", 1, 6, 7), ("hb", 1, 0), ("in", 1, 7, 8), ("mm", 1),
                    ("in", 1, 8, 9), ("ms", 1), ("ht", 1, 0), ("nh", 2), ("in", 1, 9, 10), ("bs", 1), ("tok", 1, 2), ("ha", 1, 2),
                    ("in", 2, 0, 1), ("hb", 1, 2), ("in", 2, 1, 2), ("ht", 1, 2),
                    ("in", 2, 2, 3), ("mt", 2), ("in", 2, 3, 6), ("tok", 2, 0), ("ha", 2, 0), ("in", 2, 6, 7), ("hb", 2, 0),
                    ("in", 2, 7, 8), ("ht", 2, 0), ("tok", 2, 2), ("ha", 2, 2), ("in", 2, 8, 9), ("hb", 2, 2), ("mm", 2),
                    ("in", 2, 9, 10), ("ada", 0, 4), ("ms", 2), ("bs", 2), ("kq",), ("ht", 2, 2), ("ada", 4, ADA_N)]
            return [x for x in (last if l else first) + rest if x[0] != ("kq" if l < DEPTH - 1 else "ada")]

        def before(l, ev, kind):
            evs = [(i,) + x for i in range(DEPTH) for x in p1_schedule(i)]
            end = [y[:1 + len(ev)] for y in evs].index((l,) + ev)
            return [(y[0],) + y[2:] for y in evs[:end] if y[1] == kind]

        def in_ends(l, ev):
            return [y[:2] for y in before(l, ev, "in") if y[3] > P1_CHUNKS[full(y[0], y[1])].index(9)]

        def last_sub(x):
            return x + (sub_tiles(BLOCKS[x[1]][1])[-1][0],)

        def tok_products(l, b, s, t):
            return ([("q", 0), ("q", 1)] if full(l, b) else []) + [("kv", 0), ("kv", 1)]

        tok_seq = []
        for _l in range(DEPTH):
            for _x in p1_schedule(_l):
                if _x[0] == "tok":
                    for _t in range(dict(sub_tiles(BLOCKS[_x[1]][1]))[_x[2]]):
                        tok_seq += [(_l, _x[1], _x[2] + _t) + p for p in tok_products(_l, _x[1], _x[2], _t)]

        def tok_bank(l, b, t, kind, c):
            return 4 + tok_seq.index((l, b, t, kind, c)) % 3

        def norm_next(l, b):
            i = layer_blocks(l).index(b)
            if i + 1 < len(layer_blocks(l)):
                return l, 1, layer_blocks(l)[i + 1]
            return (l + 1, 0, 0) if l + 1 < DEPTH else None

        def pool_jobs(l):
            return [(g, i) for g in ((0, 1) if full(l, 0) else (1,)) for i in range(2)]

        JOB_AT = lambda k: 4 + 15 * k
        POOL_OPS = (6, 8)

        def pool_ops(l, g):
            return [(j, g - JOB_AT(k)) for k, j in enumerate(pool_jobs(l)) if 0 <= g - JOB_AT(k) < POOL_OPS[j[1]]]

        def pool_product(l, it):
            for k, (g, i) in enumerate(pool_jobs(l)):
                q = it - JOB_AT(k) - POOL_OPS[i] - 3
                if 0 <= q * NMAX < (CTX, SEQ)[g] and q >= 0:
                    return g, i, q * NMAX
            return None

        def pool_prev(l, g, i):
            k = pool_jobs(l).index((g, i))
            return pool_jobs(l)[k - 1] if k else None

        def last_q(g):
            return ((CTX, SEQ)[g] - 1) // NMAX * NMAX

        def banks_3_read(pe, l, ev):
            h = before(l, ev, "ht")
            if h:
                pe.wait_ge(*at("qk_lo", h[-1] + (1, HEADS - 1)))
            m = before(l, ev, "mt")
            if m:
                pe.wait_ge(*at("vt_n", last_sub(m[-1])))
            t = before(l, ev, "tok")
            if t:
                pe.wait_ge(*at("krt", t[-1]))
            i = in_ends(l, ev)
            if i:
                pe.wait_ge(*at("tok_var", i[-1]))

        def prev_banks(pe, l, b):
            pl, pb = (l, b - 1) if b else (l - 1, len(BLOCKS) - 1)
            if b:
                pe.wait_ge(*at("in_free", ((pl, pb), len(P1_CHUNKS[full(pl, pb)]) - 1)))
            else:
                pe.wait_ge(*at("dn_acc_end", (pl, pb)))

        def subs():
            return [(l, x[1], x[2]) for l in range(DEPTH) for x in p1_schedule(l) if x[0] == "tok"]

        def prev_sub_wait(eng, l, b, s, w):
            i = subs().index((l, b, s))
            if i == 0:
                return
            pl, pb, pss = subs()[i - 1]
            if w == 1 or full(pl, pb):
                eng.wait_ge(*at("qk_tr", (pl, pb, pss, w, HEADS - 1)))
            if w == 1:
                eng.wait_ge(*at("v_store", (pl, pb, pss)))

        def head_seq():
            return [(l, b, s, w, h) for l, b, s in subs() for w in ((0, 1) if full(l, b) else (1,)) for h in range(HEADS)]

        def prev_head_wait(eng, l, b, s, w, hd):
            i = head_seq().index((l, b, s, w, hd))
            if i >= N_ST:
                eng.wait_ge(*at(f"qk_store{hd % N_ST}", head_seq()[i - N_ST]))

        def att_plan(l):
            st, tg = [], []
            for hd in range(HEADS):
                for i, (col, nk) in enumerate(steps(l)):
                    st.append((hd, i, col, nk))
            out = []
            for g, (hd, i, col, nk) in enumerate(st):
                grp = []
                for k0, n in t_groups(nk):
                    grp.append((len(tg), k0, n))
                    tg.append((g, k0, n))
                out.append(grp)
            return st, out

        psum_flat = psum[:, :, :].rearrange("p a n -> p (a n)")

        def scores(g, nk):
            at0 = (g % 2) * NTOK
            return psum_flat[:, at0:at0 + nk * P]

        def score_parts(g, nk):
            cuts = (0, 512, 1024, NTOK) if g % 2 == 0 else (0, 256, 768, NTOK)
            parts = [(a, min(b, nk * P) - a) for a, b in zip(cuts, cuts[1:]) if a < nk * P]
            return parts if g % 2 == 0 else parts[1:] + parts[:1]

        def t_of(l, g):
            return g - 3 if 0 <= g - 3 < len(att_plan(l)[0]) else None

        def pv_of(l, g):
            pr, half = divmod(g - 5, 2)
            return (pr, half) if 0 <= pr < len(att_plan(l)[0]) // 2 else (None, None)

        def ada_bank(m):
            return (0 if m >= ADA_M else 4) + m % 2

        def pool_bank(l, g):
            return 5 + sum(len(t_groups(nk)) for _, _, _, nk in att_plan(l)[0][:g - 2]) % 2

        def att_iterations(l):
            return len(att_plan(l)[0]) + 6

        def att_act(act, l):
            st, groups = att_plan(l)
            G = len(st)
            npair = len(steps(l)) // 2
            for g in range(att_iterations(l)):
                q = t_of(l, g)

                def t_hi(tg, k0, n):
                    act.wait_ge(*at("t_mm", (l, tg)))
                    if k0 == 0 and q // 2 >= 2:
                        act.wait_ge(*at("pv_mm", (l,) + divmod(q // 2 - 2, npair)))
                    if k0 == 0 and q // 2 < 2:
                        act.wait_ge(*at("att_free", l))
                    act.activation(pt_hi[:, (q // 2) % 2, k0:k0 + n, (q % 2) * P:(q % 2) * P + P],
                                   psum[:, 5 + tg % 2, 0:n * P].rearrange("p (k n) -> p k n", n=P), ACT.Copy)\
                       .then_inc(*inc("t_hi", (l, tg)))
                ts = groups[q] if q is not None else []
                if ts:
                    t_hi(*ts[0])
                e = g - 1
                if 0 <= e < G:
                    hd, i, col, nk = st[e]
                    act.wait_ge(*at("amax", (l, e)))
                    if e >= 4:
                        act.wait_ge(*at("t_mm", (l, groups[e - 4][-1][0])))
                    act.activation(prob[:, e % 4, 0:nk * P], scores(e, nk), ACT.Exp, bias=amax[:, 1, e % 4:e % 4 + 1], scale=SCALE,
                                   accum_out=den[:, 0, e % 4:e % 4 + 1]).then_inc(*inc("exp", (l, e)))
                for x in ts[1:]:
                    t_hi(*x)
                job = pool_product(l, g)
                if job:
                    w = min(NMAX, (CTX, SEQ)[job[0]])
                    act.wait_ge(*at("pool_mm", (l,) + job))
                    act.activation(ps4[:, HALO + job[2]:HALO + job[2] + w], psum[:, pool_bank(l, g), :w], ACT.Copy,
                                   scale=pcol("pscale", job[1], job[1] + 1)).then_inc(*inc("pool_out", (l,) + job))
                pr, pv_part = pv_of(l, g)
                if pv_part == 1:
                    act.wait_ge(*at("pv_mm", (l,) + divmod(pr, npair)))
                    if pr >= 2:
                        act.wait_ge(*at("yc", (l,) + divmod(pr - 2, npair)))
                    act.activation(yc_lo[:, pr % 2, :], psum[VD:2 * VD, 7, 0:256], ACT.Copy)\
                       .then_inc(*inc("yc_lo", (l,) + divmod(pr, npair)))

        @block.sync
        def _(sp):
            sp.dma_start(silu_c[:, 0], t_in["c"]).then_inc(*inc("c_in", by=16))

            def load_ada(j):
                if j % ADA_N >= N_ADA:
                    sp.wait_ge(*at("ada_mm", j - N_ADA))
                sp.dma_start(ada_raw[:, j % N_ADA], t_in["w_ada"][j // ADA_N, j % ADA_N]).then_inc(*inc(f"ada_in{j % N_ADA}", j, 16))

            for j in range(ADA_N):
                load_ada(j)
                if j == 1:
                    sp.dma_start(ident[:, :], t_in["ident"]).then_inc(*inc("consts", by=16))
                    sp.dma_start(trig[:, :, :, :], t_in["trig"]).then_inc(*inc("consts", by=16))
                    sp.dma_start(ada_p[:, :, :], t_in["ada_p"]).then_inc(*inc("consts", by=16))
                    sp.dma_start(prm[:, :], t_in["prm"][0]).then_inc(*inc("prm", 0, 16))
                if j % 4 == 3 and 7 <= j < 23:
                    ks = slice(2 * (j // 4 - 1), 2 * (j // 4))
                    sp.dma_start(X[:, ks, :], t_in["x"].rearrange("(k p) n -> p k n", p=P)[:, ks]).then_inc(*inc("x_in", by=16))

            def load_chunks(n0, count):
                for n in range(n0, min(n0 + count, n_chunks)):
                    if n >= 2:
                        sp.wait_ge(C.sem("w_lo"), n - 1)
                    l, c = stream[n]
                    sp.dma_start(raw[:, n % 2, :], t_in["w"][l, c]).then_inc(*inc(f"w_in{n % 2}", n, 16))

            def load_chunks_loop(n0, turns):
                l, c0 = stream[n0]
                with sp.Fori(0, turns, 1) as i:
                    for j in range(4):
                        src = t_in["w"][l, bass.ds(i * 4 + (c0 + j), 1)].rearrange("o p n -> (o p) n")
                        sp.wait_ge(C.sem("w_lo"), i * 4 + (n0 + j - 1))
                        sp.dma_start(raw[:, (n0 + j) % 2, :], src).then_inc(C.sem(f"w_in{(n0 + j) % 2}"), 16)
                for j in range(2):
                    C.skip(f"w_in{j}", 32 * turns)

            load_chunks(0, 2)
            for l in range(DEPTH):
                if l:
                    sp.wait_ge(*at("pool_out", (l - 1, 1, 1, last_q(1))))
                    sp.dma_start(prm[:, :], t_in["prm"][l]).then_inc(*inc("prm", l, 16))
                    sp.wait_ge(C.sem("w_used"), start["p1", l, 0])
                sp.dma_start(qk[:, :, :, :, :].rearrange("p a b c d -> p (a b c d)")[:, 0:2 * NQ + NKV], t_in["wqkv"][l])\
                  .then_inc(*inc("wqkv_in", l, 16))
                q0 = 0 if l < DEPTH - 1 else CTX

                def kq_load(hd, j, a, e):
                    one, qa = bass.ds(hd, 1), max(a, q0)
                    sp.dma_start(kh[:, j, :, a:e].bitcast(F32), qk_scr[l, 1, one, :, :, a:e].rearrange("o d s n -> (o d) s n"))\
                      .then_inc(C.sem(f"kq{j}"), 16)
                    sp.dma_start(qh[:, j, :, qa:e].bitcast(F32), qk_scr[l, 0, one, :, :, qa:e].rearrange("o d s n -> (o d) s n"))\
                      .then_inc(C.sem(f"kq{j}"), 16)
                    C.skip(f"kq{j}", 32)

                def v_load(hd, j):
                    sp.dma_start(vh[:, j].bitcast(F32), v_scr[l, bass.ds(hd, 1)].rearrange("o (t p) d -> p (o t) d", p=P))\
                      .then_inc(C.sem(f"v{j}"), 16)
                    C.skip(f"v{j}", 16)

                for j in range(2):
                    C.now(f"kq{j}", ("att", l)); C.now(f"v{j}", ("att", l))
                for what, *arg in p1_schedule(l):
                    if what not in ("in", "bs", "ms", "tok", "ht", "ada", "kq"):
                        continue
                    if what == "ada":
                        a, e = arg
                        if a == 0:
                            sp.wait_ge(C.sem("w_used"), start["out", l, layer_blocks(l)[0]])
                        for j in range(a + (N_ADA if a else 0), min(e + N_ADA, ADA_N)):
                            load_ada((l + 1) * ADA_N + j)
                        continue
                    if what == "kq":
                        sp.wait_ge(*at("tok_mm2", [x for x in tok_seq if x[0] == l][-1]))
                        sp.wait_ge(*at("mix_done", (l, 2)))
                        for j in range(N_ST):
                            sp.wait_ge(*at(f"qk_store{j}", (l, 2, 0, 1, HEADS - N_ST + j)))
                        kq_load(0, 0, 0, LATE)
                        continue
                    b = arg[0]
                    c0, T = BLOCKS[b]
                    cs = P1_CHUNKS[full(l, b)]
                    if what == "in":
                        lo, hi = arg[1], min(arg[2], len(cs))
                        load_chunks(start["p1", l, b] + 2 + lo, hi - lo)
                    elif what == "bs":
                        for i in range(2):
                            sp.wait_ge(*at("b_out", (l, b, i)))
                            sp.dma_start(b_scr[l, i, :, c0:c0 + T], yst[:, i, :T]).then_inc(*inc("b_store", (l, b, i), 16))
                    elif what == "ms":
                        sp.wait_ge(*at("mix_done", (l, b)))
                        sp.dma_start(y_scr[l, 0:256, c0:c0 + T].rearrange("(i p) n -> p i n", p=P),
                                     mixo[:, :, :T]).then_inc(*inc("ya_store", (l, b), 16))
                    elif what == "tok":
                        s, nt = arg[1], dict(sub_tiles(T))[arg[1]]
                        cs0 = c0 + s * P
                        sp.wait_ge(*at("v_lo", (l, b, s)))
                        for t in range(nt):
                            sp.dma_start(v_scr[l, :, cs0 + t * P:cs0 + t * P + P, :].rearrange("h p d -> p h d"),
                                         v_st[:, t].rearrange("p h two d -> p h (two d)").bitcast(F32))\
                              .then_inc(*inc("v_store", (l, b, s), 16))
                    elif what == "ht":
                        s, nt = arg[1], dict(sub_tiles(T))[arg[1]]
                        cs0 = c0 + s * P
                        for w in ((0, 1) if full(l, b) else (1,)):
                            for hd in range(HEADS):
                                sp.wait_ge(*at("qk_lo", (l, b, s, w, hd)))
                                sp.dma_start(qk_scr[l, w, hd, :, :, cs0:cs0 + nt * P], st_qk[:, hd % N_ST, :, :nt * P].bitcast(F32))\
                                  .then_inc(*inc(f"qk_store{hd % N_ST}", (l, b, s, w, hd), 16))
                for j in range(N_ST):
                    sp.wait_ge(*at(f"qk_store{j}", (l, 2, 2, 1, HEADS - N_ST + j)))
                sp.wait_ge(*at("v_store", (l, 2, 2)))
                sp.wait_ge(*at("b_store", (l, 2, 1)))
                sp.wait_ge(*at("ya_store", (l, 2)))
                npair = len(steps(l)) // 2

                def yc_store(hd, j, pr):
                    col = steps(l)[2 * pr][0]
                    sp.dma_start(y_scr[l, 2 * 256 + hd * VD:2 * 256 + hd * VD + VD, col:col + 256] if isinstance(hd, int) else
                                 y_scr[l].rearrange("(h d) n -> h d n", d=VD)[bass.ds(hd + HEADS, 1), :, col:col + 256]
                                 .rearrange("o d n -> (o d) n"), yc[:, (j * npair + pr) % 2])\
                      .then_inc(C.sem(f"yc_store{(j * npair + pr) % 2}"), 16)
                    C.skip(f"yc_store{(j * npair + pr) % 2}", 16)

                def pool_moves(it):
                    for k, (g, i) in enumerate(pool_jobs(l)):
                        c0, L = ((0, CTX), (CTX, SEQ))[g]
                        if it == (JOB_AT(k) - 4 if k else 0):
                            if k:
                                sp.wait_ge(*at("pool_d", (l,) + pool_jobs(l)[k - 1]))
                            sp.wait_ge(*at("b_store", (l, min(g * 2, 2), 1)))
                            sp.dma_start(pz[:, HALO:HALO + L], b_scr[l, i, :, c0:c0 + L]).then_inc(*inc("pz_in", (l, g, i), 16))
                            sp.dma_start(pinv[:, :L], t_in["inv_lat" if g else "inv_ctx"][:, i]).then_inc(*inc("pinv_in", (l, g, i), 16))
                    job = pool_product(l, it)
                    if job:
                        g, i, q = job
                        c0, w = (0, CTX)[g] + q, min(NMAX, (CTX, SEQ)[g])
                        sp.wait_ge(*at("pool_out", (l,) + job))
                        sp.dma_start(y_scr[l, 256 + i * P:256 + i * P + P, c0:c0 + w], ps4[:, HALO + q:HALO + q + w])\
                          .then_inc(*inc("yb_store", (l,) + job, 16))

                C.now("yc_store0", ("att", l)); C.now("yc_store1", ("att", l))
                for j in range(2):
                    kq_load(j, j, 0 if j or l < DEPTH - 1 else LATE, NTOK)
                    v_load(j, j)
                for hd in range(HEADS):
                    for pr in range(npair):
                        p = hd * npair + pr
                        for it in range(0 if p == 0 else 2 * p + 5, 2 * p + 7):
                            pool_moves(it)
                        sp.wait_ge(*at("yc", (l, hd, pr)))
                        yc_store(hd, hd % 2, pr)
                    if hd + 2 < HEADS:
                        sp.wait_ge(*at("pv_mm", (l, hd, npair - 1)))
                        kq_load(hd + 2, hd % 2, 0, NTOK)
                        v_load(hd + 2, hd % 2)
                for b in layer_blocks(l):
                    c0, T = BLOCKS[b]
                    n0 = start["out", l, b]
                    if b == layer_blocks(l)[0]:
                        sp.wait_ge(*at("yb_store", (l, 1, 1, last_q(1))))
                        sp.wait_ge(*at("yc", (l, HEADS - 1, npair - 1)))
                    else:
                        sp.wait_ge(*at("y_lo", (l, b - 1, KT - 1)))
                    for part in range(4):
                        if part == 2 and b == layer_blocks(l)[0]:
                            for j in range(2):
                                sp.wait_ge(C.sem(f"yc_store{j}"), C.total[f"yc_store{j}"])
                        ks = slice(2 * part, 2 * part + 2)
                        sp.dma_start(yraw[:, ks, :T], y_scr[l, 2 * part * P:(2 * part + 2) * P, c0:c0 + T].rearrange("(k p) n -> p k n", p=P))\
                          .then_inc(*inc(f"y_in{part}", (l, b), 16))
                    for m in range(KT):
                        load_chunks(n0 + 2 + m, 1)
                for b in layer_blocks(l):
                    n0 = start["ffn", l, b]
                    n_ffn = 2 * FT + 3 * KT
                    load_chunks_loop(n0 + 2, n_ffn // 4 - 1)
                    load_chunks(n0 + 2 + n_ffn - 4, 4)
                    if l == DEPTH - 1:
                        c0, T = BLOCKS[b]
                        sp.wait_ge(*at("dn_acc_end", (l, b)))
                        sp.dma_start(t_in["out"][:, c0 - CTX:c0 - CTX + T].rearrange("(k p) n -> p k n", p=P),
                                     X[:, :, c0:c0 + T]).then_inc(*inc("out", by=16))
            sp.wait_ge(*at("out"))

        def h_free(act, l, which, b, k, under):
            if under is not None:
                act.wait_ge(C.sem("w_used"), start[("ffn",) + under] + 2 * FT)
            elif which == 1:
                out_blocks = layer_blocks(l)
                act.wait_ge(*at("h_used", (("out", l, out_blocks[-1]), k)))
            elif b:
                act.wait_ge(*at("h_used", (("in", l, b - 1), k)))

        def norm_tile(which, k, T):
            return (fnrm_t if which else nrm_t)[:, k % 6, :T] if k % 6 < 4 else t32[:, k % 6 - 4, :T]

        def rotate(eng, l, b, s, w):
            nt, k2 = dict(sub_tiles(BLOCKS[b][1]))[s], (l, b, s, w)
            n, tile = HEADS * nt, (BLOCKS[b][0] - CTX) // P + s
            part = qk_sq.shape[1] * HEADS * QKD // 2
            tmp = qk_sq[:, :, :, :].rearrange("p t h d -> p (t h d)")[:, w * part:(w + 1) * part]
            tt = [tmp[:, e * n * ROPE // 2:(e + 1) * n * ROPE // 2].rearrange("p (t h d) -> p t h d", t=nt, h=HEADS) for e in range(3)]
            rope = qk[:, w, :nt, :, NOPE:].rearrange("p t h d -> p (t h) d")
            g = pcol("grope", w * ROPE, (w + 1) * ROPE).unsqueeze(1).to_broadcast([P, n, ROPE])
            x = [qk[:, w, :nt, :, NOPE + e:QKD:2] for e in range(2)]
            cs = [trig[:, tile:tile + nt, e, :].unsqueeze(2).to_broadcast([P, nt, HEADS, ROPE // 2]) for e in range(2)]
            eng.wait_ge(*at("hd_n", k2))
            eng.tensor_tensor(rope, rope, g, ALU.mult).then_inc(*inc(f"rope_gain{w}", k2))
            eng.wait_ge(*at(f"rope_gain{w}", k2))
            eng.tensor_tensor(tt[0], x[0], cs[0], ALU.mult)
            eng.tensor_tensor(tt[1], x[1], cs[1], ALU.mult)
            eng.tensor_tensor(tt[2], x[0], cs[1], ALU.mult).then_inc(*inc(f"rope_parts{w}", k2))
            eng.wait_ge(*at(f"rope_parts{w}", k2))
            eng.tensor_tensor(x[1], x[1], cs[0], ALU.mult).then_inc(*inc(f"rope_own{w}", k2))
            eng.tensor_tensor(x[0], tt[0], tt[1], ALU.subtract)
            eng.wait_ge(*at(f"rope_own{w}", k2))
            eng.tensor_tensor(x[1], tt[2], x[1], ALU.add).then_inc(*inc(f"roped{w}", k2))

        def split_hi(act, n):
            if isinstance(n, int) and n >= n_chunks:
                return
            slot = n % 2
            act.wait_ge(C.sem(f"w_in{slot}"), 16 * (n // 2 + 1))
            if n >= 2:
                act.wait_ge(C.sem("w_used"), n - 1)
            for a, e, sem in w_parts(n):
                act.activation(w_hi[:, slot, a:e], raw[:, slot, a:e], ACT.Copy).then_inc(*inc(sem, n))

        def w_parts(n):
            short = [x for x in start if start[x] <= n][-1][2] == 0
            return ((0, CH // 2, "w_hi_half"), (CH // 2, CH, "w_hi")) if short else ((0, CH, "w_hi"),)

        def split_lo(dve, n):
            if n >= n_chunks:
                return
            slot = n % 2
            for a, e, sem in w_parts(n):
                dve.wait_ge(*at(sem, n))
                x = dve.tensor_tensor(w_lo[:, slot, a:e], raw[:, slot, a:e], w_hi[:, slot, a:e].bitcast(F32), ALU.subtract)
            x.then_inc(*inc("w_lo", n))

        def split_hi_loop(act, n0, i, per, j, short):
            n = n0 + j
            act.wait_ge(C.sem(f"w_in{n % 2}"), i * (8 * per) + 16 * (n // 2 + 1))
            act.wait_ge(C.sem("w_used"), i * per + (n - 1))
            if short:
                act.activation(w_hi[:, n % 2, 0:CH // 2], raw[:, n % 2, 0:CH // 2], ACT.Copy).then_inc(C.sem("w_hi_half"), 1)
            a = CH // 2 if short else 0
            act.activation(w_hi[:, n % 2, a:CH], raw[:, n % 2, a:CH], ACT.Copy).then_inc(C.sem("w_hi"), 1)

        def split_lo_loop(dve, n0, i, per, j, short):
            n = n0 + j
            a = CH // 2 if short else 0
            if short:
                dve.wait_ge(C.sem("w_hi_half"), i * per + (short + j))
                dve.tensor_tensor(w_lo[:, n % 2, 0:a], raw[:, n % 2, 0:a], w_hi[:, n % 2, 0:a].bitcast(F32), ALU.subtract)
            dve.wait_ge(C.sem("w_hi"), i * per + (n + 1))
            dve.tensor_tensor(w_lo[:, n % 2, a:CH], raw[:, n % 2, a:CH], w_hi[:, n % 2, a:CH].bitcast(F32), ALU.subtract)\
               .then_inc(C.sem("w_lo"), 1)

        qk_flat = qk[:, :, :, :, :].rearrange("p a b c d -> p (a b c d)")[:, 0:2 * NQ + NKV]

        @block.scalar
        def _(act):
            def norm_piece(l, which, b, piece, under=None):
                c0, T = BLOCKS[b]
                key = (l, which, b)
                s = 1 if b == 0 else 0
                tmp = fnrm_t if which else nrm_t
                if piece in ("sq0", "sq1"):
                    h = int(piece[2])
                    if h:
                        act.wait_ge(*at("norm_sum", (key, 0)))
                    else:
                        if which == 1:
                            act.wait_ge(*at("out_end", (l, b)))
                        elif l:
                            act.wait_ge(*at("dn_acc_end", (l - 1, b)))
                        else:
                            act.wait_ge(*at("x_in"))
                        if key == (0, 0, 0):
                            act.wait_ge(*at("mod", 0))
                        if under is not None:
                            act.wait_ge(*at("gu_lo", ("ffn",) + under, plus=FT))
                        elif which == 0 and l and b == 1:
                            act.wait_ge(*at("h_lo", ((l, 0, 0), KT - 1)))
                        elif which == 0 and b == 1:
                            act.wait_ge(*at("pq_lo", ((l, 0), 2)))
                        elif which == 0 and b > 1:
                            act.wait_ge(*at("pq_lo", ((l, b - 2), 2)))
                        elif which == 1:
                            act.wait_ge(*at("y_lo", (l, layer_blocks(l)[-1], KT - 1)))
                    act.activation(tmp[:, :, :T], X[:, 4 * h:4 * h + 4, c0:c0 + T], ACT.Square).then_inc(*inc("norm_sq", (key, h)))
                else:
                    k = int(piece)
                    act.wait_ge(*at("norm_t", (key, k)))
                    if under is None or k == 0:
                        h_free(act, l, which, b, k, under)
                    act.activation(h_hi[:, k, :T], norm_tile(which, k, T), ACT.Identity,
                                   bias=mod[:, l, 24 * which + k, s:s + 1]).then_inc(*inc("h_hi", (key, k)))

            def ada_evac(m):
                act.wait_ge(*at("ada_mm", 2 * m + 1))
                if m % ADA_M >= 2:
                    act.wait_ge(*at("ada_tr", m - 2))
                act.activation(ada_row[:, m % 2, :], psum[0:2, ada_bank(m), :], ACT.Copy).then_inc(*inc("ada_row", m))

            def in_chunk(l, b, i):
                c0, T = BLOCKS[b]
                c = P1_CHUNKS[full(l, b)][i]
                kb, n = (l, b), start["p1", l, b] + i
                split_hi(act, n + 2)
                src = psum[:, i % 2, :T]
                act.wait_ge(C.sem("w_used"), n + 1)
                if c in (0, 1):
                    if (l, b) > (0, 0):
                        act.wait_ge(*at("mix_done", at_prev(l, b)))
                    act.activation(u_sb[:, c, :T], src, ACT.Gelu).then_inc(*inc("in_free", (kb, i)))
                elif c in (2, 3):
                    act.activation(v_sb[:, c - 2, :T], src, ACT.Gelu).then_inc(*inc("in_free", (kb, i)))
                elif c in (4, 5):
                    if (l, b) > (0, 0):
                        act.wait_ge(*at("b_store", at_prev(l, b) + (1,)))
                    act.activation(yst[:, c - 4, :T], src, ACT.Copy).then_inc(*inc("in_free", (kb, i)))
                    C.alias("b_out", (l, b, c - 4), "in_free")
                elif c in (6, 7, 8):
                    j = c - 6
                    g = pcol("qa", j, j + 1) if j < 2 else pcol("kva")
                    if c == 6 or not full(l, b):
                        act.wait_ge(*at("h_lo", ((l, 0, b), KT - 1)))
                        if b + 1 < len(BLOCKS) and (l, b) > (0, 0):
                            act.wait_ge(*at("norm_sum", ((l, 0, b + 1), 1)))
                    act.activation(pq32[:, j, :T], src, ACT.Copy, scale=g).then_inc(*inc("pq32", (kb, j)))
                    act.activation(pq_hi[:, j, :T], src, ACT.Copy, scale=g).then_inc(*inc("pq_hi", (kb, j)))
                    act.activation(pq_sq[:, j, :T], src, ACT.Square).then_inc(*inc("in_free", (kb, i)))
                    C.alias("pq_sq", (kb, j), "in_free")
                elif c == 9:
                    act.activation(kr_sb[:, :T], src, ACT.Copy).then_inc(*inc("in_free", (kb, i)))
                    C.alias("kr_sb", kb, "in_free")

            def mt(l, b):
                T = BLOCKS[b][1]
                for s, nt in sub_tiles(T):
                    for t in range(nt):
                        act.wait_ge(*at("mix_tr", (l, b, s)))
                        act.activation(vtok[:, s + t, :], psum[:, 2 + s // 2, t * 256:(t + 1) * 256], ACT.Square,
                                       accum_out=stat[:, 64 + s + t:65 + s + t]).then_inc(*inc("vt_sq", (l, b, s)))

            def tok(l, b, s):
                T = BLOCKS[b][1]
                nt = dict(sub_tiles(T))[s]
                act.wait_ge(*at("tok_r", (l, b)))
                for t in range(nt):
                    for kind, c in tok_products(l, b, s, t):
                        key = (l, b, s + t, kind, c)
                        bank = tok_bank(*key)
                        act.wait_ge(*at("tok_mm2", key))
                        if c == 0 and t == 0:
                            prev_sub_wait(act, l, b, s, 0 if kind == "q" else 1)
                        if kind == "q":
                            act.activation(qk[:, 0, t, 4 * c:4 * c + 4].rearrange("p h d -> p (h d)"), psum[:, bank, 0:384],
                                           ACT.Copy, scale=stat[:, 16 + s + t:17 + s + t]).then_inc(*inc("tok_act", key))
                        else:
                            src = psum[:, bank, :].rearrange("p (h d) -> p h d", d=P)
                            rs = stat[:, 20 + s + t:21 + s + t]
                            act.activation(qk[:, 1, t, 4 * c:4 * c + 4, 0:NOPE], src[:, :, 0:NOPE], ACT.Copy, scale=rs)\
                               .then_inc(*inc("tok_act", key))
                            act.activation(v_st[:, t, 4 * c:4 * c + 4, 0, :], src[:, :, NOPE:P], ACT.Copy, scale=rs)\
                               .then_inc(*inc("tok_act", key))
                act.wait_ge(*at("kr_tr", (l, b, s)))
                act.activation(krt[:, :nt, :], psum[:, 3, 0:nt * P].rearrange("p (t d) -> p t d", d=P)[:, :, P - ROPE:P],
                               ACT.Copy).then_inc(*inc("krt", (l, b, s)))

            def ha(l, b, s):
                nt = dict(sub_tiles(BLOCKS[b][1]))[s]
                ws = (0, 1) if full(l, b) else (1,)
                act.wait_ge(*at("tok_mm", in_ends(l, ("ha", b, s))[-1]))
                for w in ws:
                    if w == 1:
                        act.wait_ge(*at("kr_b", (l, b, s)))
                    else:
                        act.wait_ge(*at("tok_act", (l, b, s + nt - 1, "q", 1)))
                    if w == 1 and len(ws) == 2:
                        act.wait_ge(*at("hd_sum", (l, b, s, 0)))
                    act.activation(qk_sq[:, :nt].rearrange("p t h d -> p (t h d)"),
                                   qk[:, w, :nt].rearrange("p t h d -> p (t h d)"), ACT.Square).then_inc(*inc("hd_sq", (l, b, s, w)))

            def ht(l, b, s):
                nt = dict(sub_tiles(BLOCKS[b][1]))[s]
                for w in (0, 1) if full(l, b) else (1,):
                    g = pcol("gnope" if b else "gfull", w, w + 1)[:QKD]
                    for hd in range(HEADS):
                        key = (l, b, s, w, hd)
                        act.wait_ge(*at("qk_tr", key))
                        prev_head_wait(act, l, b, s, w, hd)
                        act.activation(st_qk[:, hd % N_ST, 0, :nt * P], psum[:QKD, 2 + hd % 2, 0:nt * P], ACT.Copy, scale=g)\
                           .then_inc(*inc("qk_hi", key))

            C.skip("sg", 2)
            act.wait_ge(*at("c_in"))
            act.activation(silu_c[:, 1], silu_c[:, 0], ACT.Silu).then_inc(*inc("silu_c"))
            for m in range(ADA_M):
                ada_evac(m)
            for l in range(DEPTH):
                if l == 0:
                    act.wait_ge(*at("prm", 0))
                    split_hi(act, 0)
                    split_hi(act, 1)
                for what, *arg in p1_schedule(l):
                    if what in ("na", "nh"):
                        for piece in ("sq0", "sq1") if what == "na" else range(KT):
                            norm_piece(l, 0, arg[0], str(piece))
                    elif what == "ada":
                        for m in range(arg[0] // 2, arg[1] // 2):
                            ada_evac((l + 1) * ADA_M + m)
                    elif what == "wqkv":
                        act.wait_ge(*at("wqkv_in", l))
                        act.activation(wqkv_hi[:, :], qk_flat, ACT.Copy).then_inc(*inc("wqkv_hi", l))
                    elif what == "in":
                        for i in range(arg[1], min(arg[2], len(P1_CHUNKS[full(l, arg[0])]))):
                            in_chunk(l, arg[0], i)
                    elif what in ("mt", "tok", "ha", "ht"):
                        {"mt": mt, "tok": tok, "ha": ha, "ht": ht}[what](l, *arg)
                att_act(act, l)
                for b in layer_blocks(l):
                    c0, T = BLOCKS[b]
                    n0 = start["out", l, b]
                    for k in range(KT):
                        act.wait_ge(*at(f"y_in{k // 2}", (l, b)))
                        if b == layer_blocks(l)[0]:
                            act.wait_ge(C.sem("w_used"), n0)
                        else:
                            act.wait_ge(*at("h_used", (("out", l, b - 1), k)))
                        act.activation(h_hi[:, k, :T], yraw[:, k, :T], ACT.Copy).then_inc(*inc("y_hi", (l, b, k)))
                    for m in range(KT):
                        split_hi(act, n0 + m + 2)
                        if b == layer_blocks(l)[-1]:
                            for piece in {0: ("sq0",), 1: ("sq1",), KT - 2: range(KT)}.get(m, ()):
                                norm_piece(l, 1, layer_blocks(l)[0], str(piece))
                act.activation(flag[:, 5 + l:6 + l], half[:, 0:1], ACT.Silu)
                for b in layer_blocks(l):
                    c0, T = BLOCKS[b]
                    n0 = start["ffn", l, b]
                    if b == 0:
                        C.now("w_hi_half", ("ffn", l, b))
                    C.now("sg", ("ffn", l, b)); C.now("gu_hi", ("ffn", l, b))
                    g32b = at("gu32", ("ffn", l, b))[1]
                    with act.Fori(0, FT // 2, 1) as i:
                        for j in range(2):
                            split_hi_loop(act, n0 + 2, i, 4, 2 * j, b == 0)
                            act.wait_ge(C.sem("w_used"), i * 4 + (n0 + 2 * j + 1))
                            act.wait_ge(C.sem("gu32"), i * 2 + (g32b + j - 1))
                            act.activation(sg[:, j, :T], psum[:, 2 * j, :T], ACT.Silu).then_inc(C.sem("sg"), 1)
                            split_hi_loop(act, n0 + 2, i, 4, 2 * j + 1, b == 0)
                            act.wait_ge(C.sem("gu32"), i * 2 + (g32b + j + 1))
                            act.activation(gu_hi[:, bass.ds(i * 2 + j, 1), :T].rearrange("p o n -> p (o n)"),
                                           gu32[:, j, :T], ACT.Copy).then_inc(C.sem("gu_hi"), 1)
                    C.skip("sg", FT); C.skip("gu_hi", FT); C.skip("w_hi", 2 * FT)
                    if b == 0:
                        C.skip("w_hi_half", 2 * FT)
                    n1 = n0 + 2 * FT
                    nxt = norm_next(l, b)
                    for j in range(3 * KT):
                        split_hi(act, n1 + j + 2)
                        if nxt and j in (0, 2):
                            norm_piece(*nxt, "sq0" if j == 0 else "sq1", (l, b))
                        if nxt and 10 <= j < 10 + KT:
                            norm_piece(*nxt, str(j - 10), (l, b))
                        if nxt and nxt[1] == 0 and j >= 22:
                            norm_piece(l + 1, 0, 1, f"sq{j - 22}")

        @block.vector
        def _(dve):
            dve.memset(ones[:, :], 1.0).then_inc(*inc("ones"))
            dve.memset(half[:, :], -0.5).then_inc(*inc("ones"))
            dve.memset(flag[:, 0:1], 0.0).then_inc(C.sem("gu_lo"), 2)
            C.skip("gu_lo", 2)
            dve.memset(flag[:, 1:2], 0.0).then_inc(C.sem("gu32"), 2)
            C.skip("gu32", 2)
            dve.memset(flag[:, 2:3], 0.0).then_inc(C.sem("sg"), 2)
            def ada_end(l):
                dve.wait_ge(*at("ada_tr", (l + 1) * ADA_M - 1))
                dve.wait_ge(*at("consts"))
                v = psum[:, 6 + l, 0:96].rearrange("p (m s) -> p m s", s=2)
                dve.tensor_tensor(mod[:, l], v, ada_p[:, l, 16:64].unsqueeze(2).to_broadcast([P, 48, 2]), ALU.add)\
                   .then_inc(*inc("mod", (l, 0)))
                dve.wait_ge(*at("mod", (l, 0)))
                for which in range(2):
                    ng = ada_p[:, l, 8 * which:8 * which + 8]
                    dve.scalar_tensor_tensor(gain[:, l, which], mod[:, l, 24 * which + 8:24 * which + 16, :], 1.0,
                                             ng.unsqueeze(2).to_broadcast([P, KT, 2]), ALU.add, ALU.mult).then_inc(*inc("mod", l))

            def h_lo_piece(key, T, k):
                l, which, b = key
                s = 1 if b == 0 else 0
                dve.wait_ge(*at("h_hi", (key, k)))
                dve.scalar_tensor_tensor(h_lo[:, k, :T], norm_tile(which, k, T), mod[:, l, 24 * which + k, s:s + 1],
                                         h_hi[:, k, :T].bitcast(F32), ALU.add, ALU.subtract).then_inc(*inc("h_lo", (key, k)))

            def norm_piece(l, which, b, piece):
                c0, T = BLOCKS[b]
                key = (l, which, b)
                s, nt = (1 if b == 0 else 0), T // P
                tmp = fnrm_t if which else nrm_t
                if piece in ("sum0", "sum1"):
                    h = int(piece[3])
                    dve.wait_ge(*at("norm_sq", (key, h)))
                    dve.tensor_reduce(t32[:, h, :T], tmp[:, :, :T].rearrange("p k n -> p n k"), AX.X, ALU.add)\
                       .then_inc(*inc("norm_sum", (key, h)))
                elif piece == "var":
                    dve.wait_ge(*at("norm_mm", key))
                    dve.tensor_scalar(nst[:, 0:nt], psum[:, 7, 0:nt], 1.0 / DM, EPS, ALU.mult, ALU.add).then_inc(*inc("norm_var", key))
                elif piece == "diag":
                    dve.wait_ge(*at("norm_r", key))
                    dve.tensor_tensor(diag[:, :T].rearrange("p (t j) -> p t j", j=P), ident[:, :].unsqueeze(1).to_broadcast([P, nt, P]),
                                      nst[:, 4:4 + nt].unsqueeze(2).to_broadcast([P, nt, P]), ALU.mult).then_inc(*inc("norm_diag", key))
                else:
                    k = int(piece)
                    if k == 0:
                        dve.wait_ge(*at("norm_bc", key))
                    if k >= 6:
                        h_lo_piece(key, T, k - 6)
                        if k < KT:
                            dve.wait_ge(*at("h_lo", (key, k - 6)))
                    if k == 0 and which == 0 and b:
                        dve.wait_ge(*at("pq_lo", ((l, b - 1), 2)))
                    if k < KT:
                        dve.scalar_tensor_tensor(norm_tile(which, k, T), X[:, k, c0:c0 + T], gain[:, l, which, k, s:s + 1],
                                                 psum[:, 7, :T], ALU.mult, ALU.mult).then_inc(*inc("norm_t", (key, k)))

            def in_chunk(l, b, i):
                c0, T = BLOCKS[b]
                cs = P1_CHUNKS[full(l, b)]
                c, kb, nt_all = cs[i], (l, b), T // P
                split_lo(dve, start["p1", l, b] + i + 2)
                if c in (6, 7, 8):
                    j = c - 6
                    dve.wait_ge(*at("pq_hi", (kb, j)))
                    dve.tensor_tensor(pq_lo[:, j, :T], pq32[:, j, :T], pq_hi[:, j, :T].bitcast(F32), ALU.subtract)\
                       .then_inc(*inc("pq_lo", (kb, j)))
                if c == 9:
                    dve.wait_ge(*at("tok_mm", kb))
                    if full(l, b):
                        dve.tensor_scalar(stat[:, 0:nt_all], psum[:, 3, 0:nt_all], 1.0 / 256, EPS, ALU.mult, ALU.add)\
                           .then_inc(*inc("tok_var", kb))
                    dve.tensor_scalar(stat[:, 4:4 + nt_all], psum[:, 3, 4:4 + nt_all], 1.0 / 128, EPS, ALU.mult, ALU.add)\
                       .then_inc(*inc("tok_var", kb))

            def mt(l, b):
                T = BLOCKS[b][1]
                for s, nt in sub_tiles(T):
                    key = (l, b, s)
                    dve.wait_ge(*at("vt_sq", key))
                    dve.tensor_scalar(stat[:, 68 + s:68 + s + nt], stat[:, 64 + s:64 + s + nt], 1.0 / 256, EPS, ALU.mult, ALU.add)\
                       .then_inc(*inc("vt_var", key))
                    dve.wait_ge(*at("vt_r", key))
                    dve.tensor_tensor(vtok[:, s:s + nt, :], psum[:, 2 + s // 2, 0:nt * 256].rearrange("p (t n) -> p t n", n=256),
                                      stat[:, 72 + s:72 + s + nt].unsqueeze(2).to_broadcast([P, nt, 256]), ALU.mult)\
                       .then_inc(*inc("vt_n", key))

            def mm(l, b):
                dve.wait_ge(*at("in_free", ((l, b), P1_CHUNKS[True].index(1))))
                T = BLOCKS[b][1]
                if (l, b) > (0, 0):
                    dve.wait_ge(*at("ya_store", at_prev(l, b)))
                dve.wait_ge(*at("mix_mm", (l, b)))
                for s, nt in sub_tiles(T):
                    cols = slice(s * P, (s + nt) * P)
                    for pr in range(2):
                        bsp = pcol("bsp", pr * P, pr * P + P).unsqueeze(1).to_broadcast([P, nt, P])
                        dve.scalar_tensor_tensor(mixo[:, pr, cols].rearrange("p (t n) -> p t n", n=P),
                                                 psum[:, 4 + pr, s * P:(s + nt) * P].rearrange("p (t n) -> p t n", n=P),
                                                 pcol("sgu", pr, pr + 1), bsp, ALU.mult, ALU.add).then_inc(*inc("mix_g", (l, b, s, pr)))
                    for pr in range(2):
                        dve.wait_ge(*at("mix_g", (l, b, s, pr)))
                        dve.tensor_tensor(mixo[:, pr, cols], mixo[:, pr, cols], u_sb[:, pr, cols],
                                          ALU.mult).then_inc(*inc("mix_out", (l, b, s, pr)))
                C.alias("mix_done", (l, b), "mix_out")

            def tok(l, b, s):
                nt = dict(sub_tiles(BLOCKS[b][1]))[s]
                for t in range(nt):
                    for c in range(2):
                        key = (l, b, s + t, "kv", c)
                        dve.wait_ge(*at("tok_act", key))
                        src = psum[:, tok_bank(*key), :].rearrange("p (h d) -> p h d", d=P)
                        dve.scalar_tensor_tensor(v_st[:, t, 4 * c:4 * c + 4, 1, :], src[:, :, NOPE:P], stat[:, 20 + s + t:21 + s + t],
                                                 v_st[:, t, 4 * c:4 * c + 4, 0, :].bitcast(F32), ALU.mult, ALU.subtract)\
                           .then_inc(*inc("v_lo", (l, b, s)))
                        C.alias("v_lo_t", key, "v_lo")

            def ha(l, b, s):
                nt = dict(sub_tiles(BLOCKS[b][1]))[s]
                n = HEADS * nt
                for w in (0, 1) if full(l, b) else (1,):
                    k2 = (l, b, s, w)
                    dve.wait_ge(*at("hd_sq", k2))
                    dve.tensor_reduce(stat[:, 80 + 48 * w:80 + 48 * w + n], qk_sq[:, :nt].rearrange("p t h d -> p (t h) d"), AX.X, ALU.add)\
                       .then_inc(*inc("hd_sum", k2))
                    dve.wait_ge(*at("hd_sum", k2))
                    dve.tensor_scalar(stat[:, 96 + 48 * w:96 + 48 * w + n], stat[:, 80 + 48 * w:80 + 48 * w + n], 1.0 / QKD, EPS,
                                      ALU.mult, ALU.add).then_inc(*inc("hd_var", k2))

            def hb(l, b, s):
                nt = dict(sub_tiles(BLOCKS[b][1]))[s]
                n = HEADS * nt
                for w in (1, 0) if full(l, b) else (1,):
                    k2 = (l, b, s, w)
                    a = qk[:, w, :nt].rearrange("p t h d -> p (t h) d")
                    dve.wait_ge(*at("hd_r", k2))
                    dve.tensor_tensor(a, a, stat[:, 112 + 48 * w:112 + 48 * w + n].unsqueeze(2).to_broadcast([P, n, QKD]), ALU.mult)\
                       .then_inc(*inc("hd_n", k2))
                if b and full(l, b):
                    rotate(dve, l, b, s, 0)

            def ht(l, b, s):
                nt = dict(sub_tiles(BLOCKS[b][1]))[s]
                for w in (0, 1) if full(l, b) else (1,):
                    g = pcol("gnope" if b else "gfull", w, w + 1)[:QKD]
                    for hd in range(HEADS):
                        key = (l, b, s, w, hd)
                        dve.wait_ge(*at("qk_hi", key))
                        dve.scalar_tensor_tensor(st_qk[:, hd % N_ST, 1, :nt * P], psum[:QKD, 2 + hd % 2, 0:nt * P], g,
                                                 st_qk[:, hd % N_ST, 0, :nt * P].bitcast(F32), ALU.mult, ALU.subtract)\
                           .then_inc(*inc("qk_lo", key))

            ada_end(0)
            for l in range(DEPTH):
                if l == 0:
                    split_lo(dve, 0)
                    split_lo(dve, 1)
                for what, *arg in p1_schedule(l):
                    if what in ("na", "nb", "nc", "nh"):
                        for piece in {"na": ("sum0", "sum1"), "nb": ("var", "diag"), "nc": range(6), "nh": range(6, KT + 6)}[what]:
                            norm_piece(l, 0, arg[0], str(piece))
                    elif what == "ada" and arg[1] == ADA_N:
                        ada_end(l + 1)
                    elif what == "wqkv":
                        dve.wait_ge(*at("wqkv_hi", l))
                        dve.tensor_tensor(wqkv_lo[:, :], qk_flat, wqkv_hi[:, :].bitcast(F32), ALU.subtract).then_inc(*inc("wqkv_lo", l))
                    elif what == "in":
                        for i in range(arg[1], min(arg[2], len(P1_CHUNKS[full(l, arg[0])]))):
                            in_chunk(l, arg[0], i)
                    elif what in ("mt", "mm", "tok", "ha", "hb", "ht"):
                        {"mt": mt, "mm": mm, "tok": tok, "ha": ha, "hb": hb, "ht": ht}[what](l, *arg)
                st, groups = att_plan(l)
                G, npair = len(st), len(steps(l)) // 2
                for g in range(att_iterations(l)):
                    e, q = g - 1, t_of(l, g)
                    if 0 <= e < G:
                        hd, i, col, nk = st[e]
                        dve.wait_ge(*at("s_mm", (l, e)))
                        if e >= 4:
                            dve.wait_ge(*at("exp", (l, e - 4)))
                        else:
                            dve.wait_ge(*at("att_free", l))
                        dve.reduce_max(amax[:, 0, e % 4:e % 4 + 1], scores(e, nk), AX.X).then_inc(*inc("smax", (l, e)))
                        dve.wait_ge(*at("smax", (l, e)))
                        dve.tensor_scalar(amax[:, 1, e % 4:e % 4 + 1], amax[:, 0, e % 4:e % 4 + 1], -SCALE, None, ALU.mult)\
                           .then_inc(*inc("amax", (l, e)))
                    def t_lo(tg, k0, n):
                        dve.wait_ge(*at("t_hi", (l, tg)))
                        sl = (slice(None), (q // 2) % 2, slice(k0, k0 + n), slice((q % 2) * P, (q % 2) * P + P))
                        dve.tensor_tensor(pt_lo[sl], psum[:, 5 + tg % 2, 0:n * P].rearrange("p (k n) -> p k n", n=P),
                                          pt_hi[sl].bitcast(F32), ALU.subtract).then_inc(*inc("t_lo", (l, tg)))
                    ts = groups[q] if q is not None else []
                    if ts:
                        t_lo(*ts[0])
                    pr, pv_part = pv_of(l, g - 1)
                    if pv_part == 1:
                        dve.wait_ge(*at("yc_lo", (l,) + divmod(pr, npair)))
                        if pr >= 2:
                            dve.wait_ge(*at(f"yc_store{pr % 2}", ("att", l), plus=16 * (pr // 2)))
                        dve.tensor_tensor(yc[:, pr % 2, :], psum[0:VD, 7, 0:256], yc_lo[:, pr % 2, :], ALU.add)\
                           .then_inc(*inc("yc", (l,) + divmod(pr, npair)))
                    if 0 <= e < G:
                        dve.wait_ge(*at("exp", (l, e)))
                        if e >= 4:
                            dve.wait_ge(*at("pn", (l, e - 4)))
                        dve.reciprocal(den[:, 1, e % 4:e % 4 + 1], den[:, 0, e % 4:e % 4 + 1]).then_inc(*inc("rden", (l, e)))
                    for x in ts[1:]:
                        t_lo(*x)
                for b in layer_blocks(l):
                    c0, T = BLOCKS[b]
                    s = 1 if b == 0 else 0
                    n0 = start["out", l, b]
                    for k in range(KT):
                        dve.wait_ge(*at("y_hi", (l, b, k)))
                        dve.tensor_tensor(h_lo[:, k, :T], yraw[:, k, :T], h_hi[:, k, :T].bitcast(F32), ALU.subtract)\
                           .then_inc(*inc("y_lo", (l, b, k)))
                    for m in range(KT):
                        if b == layer_blocks(l)[-1] and m == KT - 1:
                            for k in range(8, 12):
                                norm_piece(l, 1, layer_blocks(l)[0], str(k))
                        split_lo(dve, n0 + m + 2)
                        dve.wait_ge(C.sem("w_used"), n0 + m + 1)
                        dve.scalar_tensor_tensor(X[:, m, c0:c0 + T], psum[:, m % 4, :T], mod[:, l, 16 + m, s:s + 1],
                                                 X[:, m, c0:c0 + T], ALU.mult, ALU.add).then_inc(*inc("out_acc", (l, b, m)))
                        if b == layer_blocks(l)[-1]:
                            for piece in {1: ("sum0",), 2: ("sum1",), 3: ("var",), 4: ("diag",), KT - 3: range(6), KT - 2: range(6, 8), KT - 1: range(12, KT + 6)}.get(m, ()):
                                norm_piece(l, 1, layer_blocks(l)[0], str(piece))
                    C.alias("out_end", (l, b), "out_acc")
                for b in layer_blocks(l):
                    c0, T = BLOCKS[b]
                    s = 1 if b == 0 else 0
                    n0 = start["ffn", l, b]
                    C.now("gu32", ("ffn", l, b)); C.now("gu_lo", ("ffn", l, b))
                    g32b, glob = C.total["gu32"], C.total["gu_lo"]
                    short = at("w_hi_half", ("ffn", l, b))[1] + 1 if b == 0 else 0
                    sgb, ghib = at("sg", ("ffn", l, b))[1], at("gu_hi", ("ffn", l, b))[1]
                    with dve.Fori(0, FT // 2, 1) as i:
                        for j in range(2):
                            split_lo_loop(dve, n0 + 2, i, 4, 2 * j, short)
                            split_lo_loop(dve, n0 + 2, i, 4, 2 * j + 1, short)
                            dve.wait_ge(C.sem("w_used"), i * 4 + (n0 + 2 * j + 2))
                            dve.wait_ge(C.sem("sg"), i * 2 + (sgb + j + 1))
                            dve.wait_ge(C.sem("gu_lo"), i * 2 + (glob + j - 1))
                            dve.tensor_tensor(gu32[:, j, :T], sg[:, j, :T], psum[:, 2 * j + 1, :T], ALU.mult).then_inc(C.sem("gu32"), 1)
                            dve.wait_ge(C.sem("gu_hi"), i * 2 + (ghib + j + 1))
                            f1 = bass.ds(i * 2 + j, 1)
                            dve.tensor_tensor(gu_lo[:, f1, :T].rearrange("p o n -> p (o n)"), gu32[:, j, :T],
                                              gu_hi[:, f1, :T].rearrange("p o n -> p (o n)").bitcast(F32), ALU.subtract)\
                               .then_inc(C.sem("gu_lo"), 1)
                    C.skip("gu32", FT); C.skip("gu_lo", FT); C.skip("w_lo", 2 * FT)
                    n1 = n0 + 2 * FT
                    C.now("dn_acc", ("ffn", l, b))
                    nxt = norm_next(l, b)
                    pieces = {1: ("sum0",), 3: ("sum1",), 5: ("var",), 7: ("diag",)} | {9: "012", 10: "345"} | {11 + k: (str(6 + k),) for k in range(KT)}
                    for j in range(3 * KT):
                        split_lo(dve, n1 + j + 2)
                        m = j // 3
                        if j % 3 == 2:
                            dve.wait_ge(C.sem("w_used"), n1 + 3 * m + 3)
                            dve.scalar_tensor_tensor(X[:, m, c0:c0 + T], psum[:, m % 4, :T], mod[:, l, 40 + m, s:s + 1],
                                                     X[:, m, c0:c0 + T], ALU.mult, ALU.add).then_inc(*inc("dn_acc", (l, b, m)))
                        for piece in pieces.get(j, ()) if nxt else ():
                            norm_piece(*nxt, piece)
                        if nxt and nxt[1] == 0 and j >= 22:
                            norm_piece(l + 1, 0, 1, f"sum{j - 22}")
                    C.alias("dn_acc_end", (l, b), "dn_acc")

        @block.gpsimd
        def _(pool):
            def norm(l, which, b):
                nt, key = BLOCKS[b][1] // P, (l, which, b)
                pool.wait_ge(*at("norm_var", key))
                pool.tensor_tensor(nst[:, 4:4 + nt], nst[:, 0:nt], half[:, 0:1].to_broadcast([P, nt]), ALU.pow).then_inc(*inc("norm_r", key))

            def small_pow(dst, src, n, name, key):
                pool.tensor_tensor(stat[:, dst:dst + n], stat[:, src:src + n], half[:, 0:1].to_broadcast([P, n]), ALU.pow).then_inc(*inc(name, key))

            def tok(l, b, s):
                T = BLOCKS[b][1]
                nt = dict(sub_tiles(T))[s]
                if s == 0:
                    pool.wait_ge(*at("tok_var", (l, b)))
                    if full(l, b):
                        small_pow(16, 0, T // P, "tok_r", (l, b))
                    small_pow(20, 4, T // P, "tok_r", (l, b))
                pool.wait_ge(*at("krt", (l, b, s)))
                prev_sub_wait(pool, l, b, s, 1)
                for t in range(nt):
                    pool.tensor_copy(qk[:, 1, t, :, NOPE:], krt[:, t, :].unsqueeze(1).to_broadcast([P, HEADS, ROPE]))\
                        .then_inc(*inc("kr_b", (l, b, s)))

            def mt(l, b):
                for s, nt in sub_tiles(BLOCKS[b][1]):
                    pool.wait_ge(*at("vt_var", (l, b, s)))
                    small_pow(72 + s, 68 + s, nt, "vt_r", (l, b, s))

            def ha(l, b, s):
                n = HEADS * dict(sub_tiles(BLOCKS[b][1]))[s]
                for w in (0, 1) if full(l, b) else (1,):
                    pool.wait_ge(*at("hd_var", (l, b, s, w)))
                    small_pow(112 + 48 * w, 96 + 48 * w, n, "hd_r", (l, b, s, w))

            def hb(l, b, s):
                if b:
                    rotate(pool, l, b, s, 1)

            pool.wait_ge(*at("ones"))
            for l in range(DEPTH):
                for what, *arg in p1_schedule(l):
                    if what == "nb":
                        norm(l, 0, arg[0])
                    elif what in ("mt", "tok", "ha", "hb"):
                        {"mt": mt, "tok": tok, "ha": ha, "hb": hb}[what](l, *arg)
                for j in range(N_ST):
                    pool.wait_ge(*at(f"qk_store{j}", (l, 2, 2, 1, HEADS - N_ST + j)))
                pool.wait_ge(*at("v_store", (l, 2, 2)))
                pool.wait_ge(*at("ya_store", (l, 2)))
                pool.wait_ge(*at("b_store", (l, 2, 1)))
                if l < DEPTH - 1:
                    pool.wait_ge(*at("ada_mm", (l + 2) * ADA_N - 1))
                pool.tensor_copy(flag[:, 4:5], half[:, 0:1]).then_inc(*inc("att_free", l))

                def pool_op(job, n):
                    g, i = job
                    L, prev = (CTX, SEQ)[g], pool_prev(l, g, i)
                    W2 = L + 2 * HALO

                    def window(dst, src, lo, hi, a, b):
                        return pool.tensor_tensor(dst[:, lo:hi], src[:, lo + a:hi + a], src[:, lo + b:hi + b], ALU.add)
                    if n == 0:
                        if i == 0:
                            if prev:
                                pool.wait_ge(*at("pool_d", (l,) + prev))
                            pool.memset(pz[:, 0:HALO], 0.0).then_inc(*inc("pool_edge", (l, g)))
                            pool.memset(pz[:, HALO + L:W2], 0.0).then_inc(*inc("pool_edge", (l, g)))
                        pool.wait_ge(*at("pz_in", (l, g, i)))
                        pool.wait_ge(*at("pinv_in", (l, g, i)))
                        pool.wait_ge(*at("pool_edge", (l, g)))
                        if prev:
                            pool.wait_ge(*at("yb_store", (l,) + prev + (last_q(prev[0]),)))
                    else:
                        pool.wait_ge(*at("win", (l, g, i, n - 1)))
                    windows = [(ps2, pz, 1, W2, -1, 0), (ps4, ps2, 2, W2 - 1, -1, 1),
                               (ps2, ps4, 4, W2 - 3, -2, 2), (ps4, ps2, 8, W2 - 8, -4, 4)][:2 + 2 * i]
                    halves = ((slice(0, 64), ps2), (slice(64, 128), ps4))
                    if n < len(windows):
                        x = window(*windows[n])
                    elif n < len(windows) + 2:
                        rows, src = halves[n - len(windows)]
                        x = pool.tensor_tensor(src[rows, HALO:HALO + L], src[rows, HALO:HALO + L], pinv[rows, :L], ALU.mult)
                    else:
                        rows, src = halves[n - len(windows) - 2]
                        x = pool.tensor_tensor(ps2[rows, HALO:HALO + L], src[rows, HALO:HALO + L], pz[rows, HALO:HALO + L], ALU.subtract)
                    x.then_inc(*inc("win", (l, g, i, n)))
                    if n == POOL_OPS[i] - 1:
                        C.alias("pool_d", (l, g, i), "win")

                st, groups = att_plan(l)
                for g in range(att_iterations(l)):
                    if g < len(st):
                        hd, i, col, nk = st[g]
                        pool.wait_ge(*at("rden", (l, g)))
                        for job, n in pool_ops(l, g - 1):
                            pool.wait_ge(*at("win", (l,) + job + (n,)))
                        pool.tensor_tensor(prob[:, g % 4, 0:nk * P], prob[:, g % 4, 0:nk * P],
                                           den[:, 1, g % 4:g % 4 + 1].to_broadcast([P, nk * P]), ALU.mult).then_inc(*inc("pn", (l, g)))
                    for job, n in pool_ops(l, g):
                        pool.wait_ge(*at("pn", (l, g)))
                        pool_op(job, n)
                for b in layer_blocks(l):
                    norm(l, 1, b)
                if l + 1 < DEPTH:
                    norm(l + 1, 0, 0)

        @block.tensor
        def _(pe):
            def three(out, wh, wl, hh, hl, first, last, inc_last=None):
                pe.matmul(out, wh, hh, start=first, stop=False)
                pe.matmul(out, wh, hl, start=False, stop=False)
                return pe.matmul(out, wl, hh, start=False, stop=last)

            def norm_stat(l, which, b):
                T, key = BLOCKS[b][1], (l, which, b)
                pe.wait_ge(*at("norm_sum", (key, 1)))
                for t in range(T // P):
                    for h in range(2):
                        x = pe.matmul(psum[:, 7, t:t + 1], t32[:, h, t * P:(t + 1) * P], ones[:, 0:1], start=(h == 0), stop=(h == 1))
                x.then_inc(*inc("norm_mm", key))

            def norm_bc(l, which, b):
                T, key = BLOCKS[b][1], (l, which, b)
                pe.wait_ge(*at("norm_diag", key))
                pe.matmul(psum[:, 7, :T], ones[:, :], diag[:, :T], start=True, stop=True).then_inc(*inc("norm_bc", key))

            def ada_unit(j):
                m, kh = divmod(j, KT // ADA_K)
                pe.wait_ge(*at(f"ada_in{j % N_ADA}", j))
                if kh == 0 and m % ADA_M >= 2:
                    pe.wait_ge(*at("ada_row", m - 2))
                elif j == ADA_N:
                    pe.wait_ge(*at("in_free", ((0, len(BLOCKS) - 1), N_IN - 1)))
                for k in range(ADA_K):
                    first, last = kh == 0 and k == 0, kh == 1 and k == ADA_K - 1
                    x = pe.matmul(psum[0:2, ada_bank(m), :], silu_c[:, 1, kh * ADA_K + k, :], ada_raw[:, j % N_ADA, k, :], start=first, stop=last)
                x.then_inc(*inc("ada_mm", j))

            def ada_transpose(m):
                pe.wait_ge(*at("ada_row", m))
                pe.wait_ge(*at("consts"))
                for i in range(ADA_W // P):
                    col = 2 * ((m % ADA_M) * (ADA_W // P) + i)
                    x = pe.transpose(psum[:, 6 + m // ADA_M, col:col + 2], ada_row[:, m % 2, i * P:(i + 1) * P], ident[0:2, 0:2])
                x.then_inc(*inc("ada_tr", m))

            def in_chunk(l, b, i):
                T = BLOCKS[b][1]
                cs = P1_CHUNKS[full(l, b)]
                kb, nt_all, n = (l, b), T // P, start["p1", l, b] + i
                pe.wait_ge(*at("w_lo", n))
                if i >= 2:
                    pe.wait_ge(*at("in_free", (kb, i - 2)))
                elif (l, b) > (0, 0):
                    prev_banks(pe, l, b)
                for k in range(KT):
                    if i == 0:
                        pe.wait_ge(*at("h_lo", ((l, 0, b), k)))
                    x = three(psum[:, i % 2, :T], w_hi[:, n % 2, k * P:(k + 1) * P], w_lo[:, n % 2, k * P:(k + 1) * P],
                              h_hi[:, k, :T], h_lo[:, k, :T], k == 0, k == KT - 1)
                    if i == len(cs) - 1 and k < KT - 1:
                        x.then_inc(*inc("h_used", (("in", l, b), k)))
                x.then_inc(*inc("w_used", n))
                C.alias("h_used", (("in", l, b), KT - 1), "w_used")
                if cs[i] == 9:
                    pe.wait_ge(*at("pq_sq", (kb, 2)))
                    banks_3_read(pe, l, ("in", b, [y[2] for y in p1_schedule(l) if y[:2] == ("in", b) and y[2] <= i][-1]))
                    for t in range(nt_all):
                        if full(l, b):
                            for k in range(2):
                                pe.matmul(psum[:, 3, t:t + 1], pq_sq[:, k, t * P:(t + 1) * P], ones[:, 0:1], start=(k == 0), stop=(k == 1))
                        x = pe.matmul(psum[:, 3, 4 + t:5 + t], pq_sq[:, 2, t * P:(t + 1) * P], ones[:, 0:1], start=True, stop=True)
                    x.then_inc(*inc("tok_mm", kb))

            def mt(l, b):
                T = BLOCKS[b][1]
                pe.wait_ge(*at("in_free", ((l, b), P1_CHUNKS[True].index(3))))
                banks_3_read(pe, l, ("mt", b))
                for s, nt in sub_tiles(T):
                    for t in range(nt):
                        for i in range(2):
                            x = pe.transpose(psum[:, 2 + s // 2, t * 256 + i * P:t * 256 + (i + 1) * P],
                                             v_sb[:, i, (s + t) * P:(s + t + 1) * P], ident[:, :])
                    x.then_inc(*inc("mix_tr", (l, b, s)))

            def mm(l, b):
                T = BLOCKS[b][1]
                toks = [x for x in tok_seq if x[:2] + (x[2] // 2 * 2,) in before(l, ("mm", b), "tok")]
                for x in toks[-3:]:
                    pe.wait_ge(*(at("v_lo_t", x) if x[3] == "kv" else at("tok_act", x)))
                for s, nt in sub_tiles(T):
                    pe.wait_ge(*at("vt_n", (l, b, s)))
                    for t in range(nt):
                        for hd in range(4):
                            rows = slice(64 * (hd % 2), 64 * (hd % 2) + 64)
                            x = pe.matmul(psum[rows, 4 + hd // 2, (s + t) * P:(s + t + 1) * P], vtok[:, s + t, hd * 64:(hd + 1) * 64],
                                          pcol("wsp", hd * P, (hd + 1) * P), start=True, stop=True)
                x.then_inc(*inc("mix_mm", (l, b)))

            def tok(l, b, s):
                T = BLOCKS[b][1]
                nt = dict(sub_tiles(T))[s]
                pe.wait_ge(*at("wqkv_lo", l))
                pe.wait_ge(*at("pq_lo", ((l, b), 2)))
                mixed = before(l, ("tok", b, s), "mm")
                if mixed:
                    pe.wait_ge(*at("mix_done", mixed[-1]))
                for t in range(nt):
                    ts = slice((s + t) * P, (s + t + 1) * P)
                    for kind, c in tok_products(l, b, s, t):
                        key = (l, b, s + t, kind, c)
                        bank, i = tok_bank(*key), tok_seq.index(key)
                        if i >= 3:
                            x = tok_seq[i - 3]
                            pe.wait_ge(*(at("v_lo_t", x) if x[3] == "kv" else at("tok_act", x)))
                        if kind == "q":
                            for k in range(2):
                                kc = slice(k * NQ + c * NQ // 2, k * NQ + (c + 1) * NQ // 2)
                                x = three(psum[:, bank, 0:NQ // 2], pq_hi[:, k, ts], pq_lo[:, k, ts],
                                          wqkv_hi[:, kc], wqkv_lo[:, kc], k == 0, k == 1)
                        else:
                            kc = slice(2 * NQ + c * NKV // 2, 2 * NQ + (c + 1) * NKV // 2)
                            x = three(psum[:, bank, :], pq_hi[:, 2, ts], pq_lo[:, 2, ts], wqkv_hi[:, kc], wqkv_lo[:, kc], True, True)
                        x.then_inc(*inc("tok_mm2", key))
                banks_3_read(pe, l, ("tok", b, s))
                for t in range(nt):
                    x = pe.transpose(psum[:, 3, t * P:(t + 1) * P], kr_sb[:, (s + t) * P:(s + t + 1) * P], ident[:, :])
                x.then_inc(*inc("kr_tr", (l, b, s)))

            def ht(l, b, s):
                nt = dict(sub_tiles(BLOCKS[b][1]))[s]
                ws = (0, 1) if full(l, b) else (1,)
                banks_3_read(pe, l, ("ht", b, s))
                for w in ws:
                    pe.wait_ge(*(at(f"roped{w}", (l, b, s, w)) if b else at("hd_n", (l, b, s, w))))
                    for hd in range(HEADS):
                        if hd >= 2:
                            pe.wait_ge(*at("qk_lo", (l, b, s, w, hd - 2)))
                        elif w == 1 and len(ws) == 2:
                            pe.wait_ge(*at("qk_lo", (l, b, s, 0, HEADS - 2 + hd)))
                        for t in range(nt):
                            x = pe.transpose(psum[:QKD, 2 + hd % 2, t * P:(t + 1) * P], qk[:, w, t, hd, :], ident[:, :])
                        x.then_inc(*inc("qk_tr", (l, b, s, w, hd)))

            pe.wait_ge(*at("silu_c"))
            for j in range(ADA_N):
                ada_unit(j)
                if j % 2 and j > 2:
                    ada_transpose(j // 2 - 1)
            ada_transpose(ADA_M - 1)
            pe.wait_ge(*at("ones"))
            for l in range(DEPTH):
                if l == 0:
                    pe.wait_ge(*at("mod", 0))
                for what, *arg in p1_schedule(l):
                    if what == "nb":
                        norm_stat(l, 0, arg[0])
                    elif what == "nc":
                        norm_bc(l, 0, arg[0])
                    elif what == "ada":
                        for j in range(*arg):
                            ada_unit((l + 1) * ADA_N + j)
                            if j % 2 and j > 2:
                                ada_transpose((l + 1) * ADA_M + j // 2 - 1)
                        if arg[1] == ADA_N:
                            ada_transpose((l + 2) * ADA_M - 1)
                    elif what == "in":
                        for i in range(arg[1], min(arg[2], len(P1_CHUNKS[full(l, arg[0])]))):
                            in_chunk(l, arg[0], i)
                    elif what in ("mt", "mm", "tok", "ht"):
                        {"mt": mt, "mm": mm, "tok": tok, "ht": ht}[what](l, *arg)
                st, groups = att_plan(l)
                G, per = len(st), len(steps(l))
                npair = per // 2
                for g in range(att_iterations(l)):
                    def t_group(q, tg, k0, n):
                        if k0 == 0:
                            pe.wait_ge(*at("pn", (l, q)))
                        if tg >= 2:
                            pe.wait_ge(*at("t_lo", (l, tg - 2)))
                        if k0 == 0 and pool_product(l, g - 1):
                            pe.wait_ge(*at("pool_out", (l,) + pool_product(l, g - 1)))
                        for k in range(n):
                            x = pe.transpose(psum[:, 5 + tg % 2, k * P:(k + 1) * P], prob[:, q % 4, (k0 + k) * P:(k0 + k + 1) * P],
                                             ident[:, :])
                        x.then_inc(*inc("t_mm", (l, tg)))

                    def s_part(hd, i, col, nk, part):
                        j = hd % 2
                        k0, w = score_parts(g, nk)[part]
                        if part == 0:
                            if i == 0:
                                pe.wait_ge(*at(f"kq{j}", ("att", l), plus=32 * (hd // 2 + (2 if j == 0 and l == DEPTH - 1 else 1))))
                            if g >= 2:
                                pe.wait_ge(*at("exp", (l, g - 2)))
                        if part == len(score_parts(g, nk)) - 1 and g >= 1:
                            pe.wait_ge(*at("exp", (l, g - 1)))
                        kc, qc = slice(k0, k0 + w), slice(col, col + P)
                        return three(scores(g, nk)[:, kc], qh[:, j, 0, qc], qh[:, j, 1, qc], kh[:, j, 0, kc], kh[:, j, 1, kc], True, True)
                    ts = groups[t_of(l, g)] if t_of(l, g) is not None else []
                    n_parts = len(score_parts(g, st[g][3])) if g < G else 0
                    for part in range(max(len(ts), n_parts - 1)):
                        if part < len(ts):
                            t_group(t_of(l, g), *ts[part])
                        if part < n_parts - 1:
                            s_part(*st[g], part)
                    job = pool_product(l, g)
                    if job:
                        w, nxt = min(NMAX, (CTX, SEQ)[job[0]]), ts[-1][0] + 1
                        pe.wait_ge(*at("pool_d", (l,) + job[:2]))
                        pe.wait_ge(*at("t_lo", (l, nxt - 2)))
                        pe.matmul(psum[:, pool_bank(l, g), :w], pcol("wpool", job[1] * P, job[1] * P + P),
                                  ps2[:, HALO + job[2]:HALO + job[2] + w], start=True, stop=True).then_inc(*inc("pool_mm", (l,) + job))
                    pr, pv_part = pv_of(l, g)
                    if pr is not None:
                        hq, pi = divmod(pr, npair)
                        nk = steps(l)[2 * pi][1]
                        if pv_part == 0:
                            pe.wait_ge(*at("t_lo", (l, groups[2 * pr + 1][-1][0])))
                            if pi == 0:
                                pe.wait_ge(*at(f"v{hq % 2}", ("att", l), plus=16 * (hq // 2 + 1)))
                            if pr >= 1:
                                pe.wait_ge(*at("yc", (l,) + divmod(pr - 1, npair)))
                        out = psum[:, 7, 0:256]
                        for k in range(pv_part * nk // 2, (pv_part + 1) * nk // 2):
                            pe.matmul(out, vh[:, hq % 2, k, :], pt_hi[:, pr % 2, k, :], start=(k == 0), stop=False)
                            x = pe.matmul(out, vh[:, hq % 2, k, :], pt_lo[:, pr % 2, k, :], start=False, stop=(k == nk - 1))
                        if pv_part == 1:
                            x.then_inc(*inc("pv_mm", (l, hq, pi)))
                    if n_parts:
                        s_part(*st[g], n_parts - 1).then_inc(*inc("s_mm", (l, g)))
                for b in layer_blocks(l):
                    c0, T = BLOCKS[b]
                    n0 = start["out", l, b]
                    for m in range(KT):
                        n = n0 + m
                        pe.wait_ge(*at("w_lo", n))
                        if m >= 4:
                            pe.wait_ge(*at("out_acc", (l, b, m - 4)))
                        elif b != layer_blocks(l)[0]:
                            pe.wait_ge(*at("out_acc", (l, b - 1, m + 4)))
                        else:
                            pe.wait_ge(*at("yc", (l, HEADS - 1, npair - 1)))
                        for k in range(KT):
                            if m == 0:
                                pe.wait_ge(*at("y_lo", (l, b, k)))
                            x = three(psum[:, m % 4, :T], w_hi[:, n % 2, k * P:(k + 1) * P], w_lo[:, n % 2, k * P:(k + 1) * P],
                                      h_hi[:, k, :T], h_lo[:, k, :T], k == 0, k == KT - 1)
                            if m == KT - 1 and k < KT - 1:
                                x.then_inc(*inc("h_used", (("out", l, b), k)))
                        x.then_inc(*inc("w_used", n))
                        C.alias("h_used", (("out", l, b), KT - 1), "w_used")
                        if b == layer_blocks(l)[-1]:
                            if m == 3:
                                norm_stat(l, 1, layer_blocks(l)[0])
                            if m == 5:
                                norm_bc(l, 1, layer_blocks(l)[0])
                for b in layer_blocks(l):
                    c0, T = BLOCKS[b]
                    n0 = start["ffn", l, b]
                    for k in range(KT):
                        pe.wait_ge(*at("h_lo", ((l, 1, b), k)))
                    prev = layer_blocks(l).index(b)
                    pe.wait_ge(*(at("out_acc", (l, layer_blocks(l)[-1], KT - 1)) if prev == 0 else
                                 at("dn_acc_end", (l, layer_blocks(l)[prev - 1]))))
                    g32b = at("gu32", ("ffn", l, b))[1]
                    sgb = at("sg", ("ffn", l, b))[1]
                    with pe.Fori(0, FT // 2, 1) as i:
                        for j in range(4):
                            n = n0 + j
                            pe.wait_ge(C.sem("w_lo"), i * 4 + (n + 1))
                            if j % 2 == 0:
                                pe.wait_ge(C.sem("sg"), i * 2 + (sgb + j // 2 - 1))
                            else:
                                pe.wait_ge(C.sem("gu32"), i * 2 + (g32b + j // 2 - 1))
                            for k in range(KT):
                                x = three(psum[:, j, :T], w_hi[:, n % 2, k * P:(k + 1) * P], w_lo[:, n % 2, k * P:(k + 1) * P],
                                          h_hi[:, k, :T], h_lo[:, k, :T], k == 0, k == KT - 1)
                            x.then_inc(C.sem("w_used"), 1)
                    C.skip("w_used", 2 * FT)
                    n1 = n0 + 2 * FT
                    pe.wait_ge(C.sem("sg"), sgb + FT - 1)
                    nxt = norm_next(l, b)
                    for m in range(KT):
                        k0 = 0
                        for j, nk in enumerate(DN_K):
                            n = n1 + 3 * m + j
                            pe.wait_ge(C.sem("w_lo"), n + 1)
                            if j == 0 and m >= 4:
                                pe.wait_ge(*at("dn_acc", (l, b, m - 4)))
                            if m == 0:
                                pe.wait_ge(*at("gu_lo", ("ffn", l, b), plus=k0 + nk))
                            for k in range(nk):
                                f = k0 + k
                                x = three(psum[:, m % 4, :T], w_hi[:, n % 2, k * P:(k + 1) * P], w_lo[:, n % 2, k * P:(k + 1) * P],
                                          gu_hi[:, f, :T], gu_lo[:, f, :T], f == 0, f == FT - 1)
                            x.then_inc(C.sem("w_used"), 1)
                            k0 += nk
                            if nxt and 3 * m + j == 4:
                                norm_stat(*nxt)
                            if nxt and 3 * m + j == 8:
                                norm_bc(*nxt)
                    C.skip("w_used", 3 * KT)
    return C


def kernel(**inputs):
    import numpy as np
    import concourse.bacc as bacc
    from concourse import mybir as mb
    from concourse.bass_utils import run_bass_kernel_spmd as run

    a = {k: np.asarray(v) for k, v in inputs.items()}

    def tiles(w):
        return w.reshape(-1, P, w.shape[-1]).transpose(1, 0, 2)

    def cols(v):
        return v.reshape(-1, P).T

    def chunk(w):
        w = tiles(w).reshape(P, -1)
        return np.pad(w, ((0, 0), (0, CH - w.shape[1])))

    chunks, prm, ada_p, w_ada, wqkv = [], [], [], [], []
    for l in range(DEPTH):
        w_in = a["w_in"][l]
        cs = [chunk(w_in[:, P * m:P * m + P]) for m in range(9)] + [chunk(w_in[:, -P:])]
        cs += [chunk(a["w_out"][l][:, P * m:P * m + P]) for m in range(KT)]
        gu = a["w_gate_up"][l]
        for f in range(FT):
            cs += [chunk(gu[:, P * f:P * f + P]), chunk(gu[:, DFF + P * f:DFF + P * f + P])]
        for m in range(KT):
            k0 = 0
            for nk in DN_K:
                cs.append(chunk(a["w_down"][l][k0 * P:(k0 + nk) * P, P * m:P * m + P]))
                k0 += nk
        chunks.append(np.stack(cs))
        wqkv.append(np.concatenate([tiles(a["w_q_b"][l]).reshape(P, -1), a["w_kv_b"][l]], 1))
        pool = np.zeros((P, 2, P), np.float32)
        for g in range(4):
            pool[64 * (g % 2):64 * (g % 2) + 64, g // 2, 64 * (g % 2):64 * (g % 2) + 64] = a["w_pool"][l][g]
        bsp = np.repeat(a["b_spatial"][l].reshape(2, 2, P), 64, axis=1).transpose(1, 0, 2)
        gqk = np.stack([a["q_norm_g"][l], a["k_norm_g"][l]])
        gfull, gnope = np.ones((P, 2), np.float32), np.ones((P, 2), np.float32)
        gfull[:QKD], gnope[:NOPE] = gqk.T, gqk[:, :NOPE].T
        prm.append(np.concatenate([
            cols(a["sgu_norm_g"][l]), cols(a["pool_scale"][l]), cols(a["q_a_norm_g"][l]), cols(a["kv_a_norm_g"][l]),
            gfull, gnope, np.broadcast_to(gqk[:, NOPE:].reshape(1, -1), (P, 2 * ROPE)),
            bsp.reshape(P, -1), pool.reshape(P, -1), a["w_spatial"][l].transpose(2, 0, 1).reshape(P, -1)], 1))
        ada_p.append(np.concatenate([cols(a["norm1_g"][l]), cols(a["norm2_g"][l]), cols(a["b_ada"][l])], 1))
        w_ada.append(tiles(a["w_ada"][l]).reshape(P, KT // ADA_K, ADA_K, ADA_M, ADA_W).transpose(3, 1, 0, 2, 4)
                     .reshape(ADA_N, P, ADA_K, ADA_W))

    def inv(n):
        t = np.arange(n)
        g = [1.0 / (np.clip(t + w // 2, 0, n) - np.clip(t - w // 2, 0, n)) for w in WINDOWS]
        return np.repeat(np.stack(g).reshape(2, 2, n), 64, axis=1).transpose(1, 0, 2).astype(np.float32)

    row, col = np.divmod(np.arange(SEQ), 64)
    f = np.float32(10000.0) ** (-np.arange(ROPE // 4, dtype=np.float32) / np.float32(ROPE // 4))
    ang = np.concatenate([row[:, None].astype(np.float32) * f, col[:, None].astype(np.float32) * f], -1).astype(np.float32)
    trig = np.stack([np.cos(ang), np.sin(ang)], 1).reshape(SEQ // P, P, 2, ROPE // 2).transpose(1, 0, 2, 3)

    arrays = {
        "x": np.concatenate([a["ctx"][0], a["x"][0]]).T,
        "c": np.stack([cols(a["c"][0]), cols(a["c_ctx"])], -1),
        "w": np.stack(chunks), "prm": np.stack(prm), "ada_p": np.stack(ada_p, 1), "w_ada": np.stack(w_ada),
        "wqkv": np.stack(wqkv), "inv_lat": inv(SEQ), "inv_ctx": inv(CTX), "trig": trig.astype(np.float32),
        "ident": np.eye(P, dtype=np.float32),
    }
    arrays = {k: np.ascontiguousarray(v) for k, v in arrays.items()}

    def program(known):
        nc = bacc.Bacc("TRN2", target_bir_lowering=False, num_devices=1)
        t_in = {k: nc.dram_tensor(f"in_{k}", v.shape, mb.dt.from_np(v.dtype), kind="ExternalInput").ap() for k, v in arrays.items()}
        t_in["out"] = nc.dram_tensor("out_0", (DM, SEQ), F32, kind="ExternalOutput").ap()
        return nc, build(nc, t_in, known)

    _, counts = program({})
    nc, _ = program(counts.value)
    r = run(nc, [{f"in_{k}": v for k, v in arrays.items()}], core_ids=[0])
    return np.ascontiguousarray(r.results[0]["out_0"].T)[None]
```
